# Optimizing a Trainium2 kernel written in Bass

```python
import jax, jax.numpy as jnp
from jax import lax
import numpy as np

D_MODEL = 2048
BATCH = 1
SEQ = 512
DEPTH = 1

Q_BLOCK = 128
HEAD_WIDTH = 128
MLA_HEADS = (D_MODEL // 2) // HEAD_WIDTH
MLA_NOPE_DIM = 128
MLA_ROPE_DIM = 64
MLA_V_DIM = 128
MLA_QK_DIM = MLA_NOPE_DIM + MLA_ROPE_DIM
MLA_Q_RANK = 768
MLA_KV_RANK = 512
MLA_WIDTH = MLA_HEADS * MLA_V_DIM
FOX_HEADS = (D_MODEL // 2) // HEAD_WIDTH
FOX_HEAD_DIM = HEAD_WIDTH
FOX_WIDTH = FOX_HEADS * FOX_HEAD_DIM
D_MIX = MLA_WIDTH + FOX_WIDTH
ROPE_THETA = 10000.0
NORM_EPS = 1e-6
IN_SPLITS = (MLA_Q_RANK, MLA_KV_RANK, MLA_ROPE_DIM, MLA_WIDTH,
             FOX_WIDTH, FOX_WIDTH, FOX_WIDTH, FOX_HEADS, FOX_WIDTH)
D_IN = (MLA_Q_RANK + MLA_KV_RANK + MLA_ROPE_DIM + MLA_WIDTH
        + 4 * FOX_WIDTH + FOX_HEADS)


def _rms_norm(x, g):
    xf = x.astype(jnp.float32)
    y = xf * lax.rsqrt(jnp.mean(xf * xf, axis=-1, keepdims=True) + NORM_EPS)
    return (y * g.astype(jnp.float32)).astype(x.dtype)

def _rope_angles(positions, dim):
    inv_freq = ROPE_THETA ** (-jnp.arange(0, dim, 2, dtype=jnp.float32) / dim)
    ang = positions.astype(jnp.float32)[..., None] * inv_freq
    return jnp.cos(ang), jnp.sin(ang)

def _apply_rope(x, cos, sin):
    xf = x.astype(jnp.float32)
    half = xf.shape[-1] // 2
    x1, x2 = xf[..., :half], xf[..., half:]
    out = jnp.concatenate([x1 * cos - x2 * sin, x2 * cos + x1 * sin], axis=-1)
    return out.astype(x.dtype)

def _causal_block_sweep(score_fn, v):
    b, seq = v.shape[0], v.shape[1]
    n_blocks = seq // Q_BLOCK
    key_pos = jnp.arange(seq)

    def one_block(i):
        start = i * Q_BLOCK
        logits = score_fn(start)
        q_pos = start + jnp.arange(Q_BLOCK)
        logits = jnp.where(key_pos[None, :] <= q_pos[:, None], logits, -jnp.inf)
        p = jax.nn.softmax(logits, axis=-1).astype(v.dtype)
        return jnp.einsum('bhqs,bshd->bqhd', p, v)

    out = lax.map(one_block, jnp.arange(n_blocks))
    return out.transpose(1, 0, 2, 3, 4).reshape(b, seq, -1)

def _mla_branch(q_lat, kv_lat, k_rope_raw, g_q, w_uq, g_kv, w_ukv, cos, sin):
    b, s, _ = q_lat.shape
    q = (_rms_norm(q_lat, g_q) @ w_uq).reshape(b, s, MLA_HEADS, MLA_QK_DIM)
    q_nope = q[..., :MLA_NOPE_DIM]
    q_rope = _apply_rope(q[..., MLA_NOPE_DIM:], cos[:, :, None, :], sin[:, :, None, :])
    kv = (_rms_norm(kv_lat, g_kv) @ w_ukv).reshape(b, s, MLA_HEADS, MLA_NOPE_DIM + MLA_V_DIM)
    k_nope, v = kv[..., :MLA_NOPE_DIM], kv[..., MLA_NOPE_DIM:]
    k_rope = _apply_rope(k_rope_raw, cos, sin)
    scale = MLA_QK_DIM ** -0.5

    def score(start):
        qn = lax.dynamic_slice_in_dim(q_nope, start, Q_BLOCK, axis=1)
        qr = lax.dynamic_slice_in_dim(q_rope, start, Q_BLOCK, axis=1)
        s_nope = jnp.einsum('bqhd,bshd->bhqs', qn, k_nope, preferred_element_type=jnp.float32)
        s_rope = jnp.einsum('bqhr,bsr->bhqs', qr, k_rope, preferred_element_type=jnp.float32)
        return (s_nope + s_rope) * scale

    return _causal_block_sweep(score, v)

def _fox_branch(q, k, v, f_logit, b_forget):
    b, s, _ = q.shape
    q = q.reshape(b, s, FOX_HEADS, FOX_HEAD_DIM)
    k = k.reshape(b, s, FOX_HEADS, FOX_HEAD_DIM)
    v = v.reshape(b, s, FOX_HEADS, FOX_HEAD_DIM)
    log_f = jax.nn.log_sigmoid(f_logit.astype(jnp.float32) + b_forget.astype(jnp.float32))
    c = jnp.cumsum(log_f, axis=1).transpose(0, 2, 1)
    scale = FOX_HEAD_DIM ** -0.5

    def score(start):
        qb = lax.dynamic_slice_in_dim(q, start, Q_BLOCK, axis=1)
        cq = lax.dynamic_slice_in_dim(c, start, Q_BLOCK, axis=2)
        logits = jnp.einsum('bqhd,bshd->bhqs', qb, k, preferred_element_type=jnp.float32) * scale
        return logits + cq[:, :, :, None] - c[:, :, None, :]

    return _causal_block_sweep(score, v)

def _hybrid_layer(x, cos, sin, g_pre, w_in, g_q, w_uq, g_kv, w_ukv, b_forget, w_out, g_post):
    h = _rms_norm(x, g_pre)
    proj = h @ w_in
    split_points = np.cumsum(IN_SPLITS)[:-1].tolist()
    (q_lat, kv_lat, k_rope_raw, gate_mla,
     fq, fk, fv, f_logit, gate_fox) = jnp.split(proj, split_points, axis=-1)
    o_mla = _mla_branch(q_lat, kv_lat, k_rope_raw, g_q, w_uq, g_kv, w_ukv, cos, sin) * jax.nn.silu(gate_mla)
    o_fox = _fox_branch(fq, fk, fv, f_logit, b_forget) * jax.nn.silu(gate_fox)
    o = jnp.concatenate([o_mla, o_fox], axis=-1) @ w_out
    return x + _rms_norm(o, g_post)

def first_inputs(seed: int = 0) -> dict:
    key = jax.random.key(seed)
    ks = jax.random.split(key, 12)
    f32 = jnp.float32
    x = jax.random.normal(ks[0], (BATCH, SEQ, D_MODEL), f32)
    offsets = jax.random.randint(ks[1], (BATCH, 1), 0, 1024, dtype=jnp.int32)
    positions = jnp.arange(SEQ, dtype=jnp.int32)[None, :] + offsets
    g_pre = 1.0 + 0.02 * jax.random.normal(ks[2], (DEPTH, D_MODEL), f32)
    w_in = jax.random.normal(ks[3], (DEPTH, D_MODEL, D_IN), f32) * D_MODEL ** -0.5
    g_q_latent = 1.0 + 0.02 * jax.random.normal(ks[4], (DEPTH, MLA_Q_RANK), f32)
    w_uq = jax.random.normal(ks[5], (DEPTH, MLA_Q_RANK, MLA_HEADS * MLA_QK_DIM), f32) * MLA_Q_RANK ** -0.5
    g_kv_latent = 1.0 + 0.02 * jax.random.normal(ks[6], (DEPTH, MLA_KV_RANK), f32)
    w_ukv = jax.random.normal(ks[7], (DEPTH, MLA_KV_RANK, MLA_HEADS * (MLA_NOPE_DIM + MLA_V_DIM)), f32) * MLA_KV_RANK ** -0.5
    b_forget = 3.0 + 0.1 * jax.random.normal(ks[8], (DEPTH, FOX_HEADS), f32)
    w_out = jax.random.normal(ks[9], (DEPTH, D_MIX, D_MODEL), f32) * D_MIX ** -0.5
    g_post = 1.0 + 0.02 * jax.random.normal(ks[10], (DEPTH, D_MODEL), f32)
    return {"x": x, "positions": positions, "g_pre": g_pre, "w_in": w_in,
            "g_q_latent": g_q_latent, "w_uq": w_uq, "g_kv_latent": g_kv_latent,
            "w_ukv": w_ukv, "b_forget": b_forget, "w_out": w_out, "g_post": g_post}

def first_block(x, positions, g_pre, w_in, g_q_latent, w_uq, g_kv_latent, w_ukv, b_forget, w_out, g_post):
    cos, sin = _rope_angles(positions, MLA_ROPE_DIM)
    for l in range(DEPTH):
        x = _hybrid_layer(x, cos, sin, g_pre[l], w_in[l], g_q_latent[l], w_uq[l],
                          g_kv_latent[l], w_ukv[l], b_forget[l], w_out[l], g_post[l])
    return x


D_MIX_2 = D_MODEL
RMS_EPS = 1e-6
NEG_INF = -1e30
TINY = 1e-30

WIDTH_A = D_MIX_2 // 2
HEAD_DIM_A = 128
N_HEADS_A = WIDTH_A // HEAD_DIM_A
N_KV_A = 2
GROUP_A = N_HEADS_A // N_KV_A
KV_A = N_KV_A * HEAD_DIM_A
CMP_BLOCK = 32
CMP_STRIDE = 16
CMP_HIDDEN = 256
SEL_BLOCK = 64
SEL_TOPK = 16
SEL_Q_CHUNK = 32
WIN_A = 512
FORCE_SCORE = 1e4

WIDTH_B = D_MIX_2 - WIDTH_A
HEAD_DIM_B = 64
N_HEADS_B = WIDTH_B // HEAD_DIM_B
N_KV_B = 2
GROUP_B = N_HEADS_B // N_KV_B
KV_B = N_KV_B * HEAD_DIM_B
WIN_B = 128

IN_SIZES = (WIDTH_A, KV_A, KV_A, KV_A, KV_A, KV_A, KV_A, WIDTH_A, 3 * N_HEADS_A,
            WIDTH_B, KV_B, KV_B, WIDTH_B)
D_IN_2 = 2 * WIDTH_A + 6 * KV_A + 3 * N_HEADS_A + 2 * WIDTH_B + 2 * KV_B


def _rmsnorm(x, g):
    xf = x.astype(jnp.float32)
    y = xf * lax.rsqrt(jnp.mean(xf * xf, axis=-1, keepdims=True) + RMS_EPS)
    return (y * g.astype(jnp.float32)).astype(x.dtype)

def _heads(t, n, d):
    return t.reshape(t.shape[0], t.shape[1], n, d)

def _rope(x):
    S, d = x.shape[1], x.shape[-1]
    inv = ROPE_THETA ** (-jnp.arange(0, d, 2, dtype=jnp.float32) / d)
    ang = jnp.arange(S, dtype=jnp.float32)[:, None] * inv[None, :]
    cos = jnp.cos(ang)[None, :, None, :]
    sin = jnp.sin(ang)[None, :, None, :]
    xf = x.astype(jnp.float32)
    x1, x2 = xf[..., : d // 2], xf[..., d // 2:]
    return jnp.concatenate([x1 * cos - x2 * sin, x2 * cos + x1 * sin], axis=-1).astype(x.dtype)

def _masked_softmax(s, mask, sink=None):
    s = jnp.where(mask, s.astype(jnp.float32), NEG_INF)
    m = jnp.max(s, axis=-1, keepdims=True)
    if sink is not None:
        m = jnp.maximum(m, sink)
    e = jnp.where(mask, jnp.exp(s - m), 0.0)
    denom = jnp.sum(e, axis=-1, keepdims=True)
    if sink is not None:
        denom = denom + jnp.exp(sink - m)
    return e / jnp.maximum(denom, TINY)

def _compress(kv, pos_emb, w1, w2):
    B, S, Hkv, D = kv.shape
    n_c = (S - CMP_BLOCK) // CMP_STRIDE + 1
    idx = jnp.arange(n_c)[:, None] * CMP_STRIDE + jnp.arange(CMP_BLOCK)[None, :]
    blocks = kv[:, idx] + pos_emb[None, None, :, None, :].astype(kv.dtype)
    flat = blocks.transpose(0, 1, 3, 2, 4).reshape(B, n_c, Hkv, CMP_BLOCK * D)
    return jax.nn.silu(flat @ w1) @ w2

def _compressed_attention(q, kc, vc):
    S, D = q.shape[1], q.shape[-1]
    n_c = kc.shape[1]
    s = jnp.einsum('bskgd,bckd->bkgsc', q, kc) * (D ** -0.5)
    ends = jnp.arange(n_c) * CMP_STRIDE + CMP_BLOCK - 1
    mask = ends[None, :] <= jnp.arange(S)[:, None]
    p = _masked_softmax(s, mask)
    o = jnp.einsum('bkgsc,bckd->bskgd', p.astype(vc.dtype), vc)
    return o, p

def _select_blocks(p_cmp, S):
    n_c = p_cmp.shape[-1]
    n_sel = S // SEL_BLOCK
    c_start = np.arange(n_c) * CMP_STRIDE
    j_start = np.arange(n_sel) * SEL_BLOCK
    overlap = (c_start[:, None] < j_start[None, :] + SEL_BLOCK) & (c_start[:, None] + CMP_BLOCK > j_start[None, :])
    p_sel = jnp.einsum('bkgsc,cj->bksj', p_cmp, jnp.asarray(overlap, jnp.float32))
    t = jnp.arange(S)[:, None]
    j = jnp.arange(n_sel)[None, :]
    cur = t // SEL_BLOCK
    forced = (j == 0) | (j == cur) | (j == cur - 1)
    valid = j * SEL_BLOCK <= t
    score = jnp.where(forced, FORCE_SCORE, jnp.where(valid, p_sel, -1.0))
    _, idx = lax.top_k(score, min(SEL_TOPK, n_sel))
    return idx

def _selected_attention(q, k, v, idx):
    B, S, Hkv, G, D = q.shape
    K = idx.shape[-1]
    n_sel = S // SEL_BLOCK
    n_ch = S // SEL_Q_CHUNK
    kb = k.reshape(B, n_sel, SEL_BLOCK, Hkv, D).transpose(0, 3, 1, 2, 4)
    vb = v.reshape(B, n_sel, SEL_BLOCK, Hkv, D).transpose(0, 3, 1, 2, 4)
    gather = jax.vmap(jax.vmap(lambda blocks, i: blocks[i]))
    scale = D ** -0.5

    def chunk_fn(args):
        qc, ic, tc = args
        kg = gather(kb, ic)
        vg = gather(vb, ic)
        s = jnp.einsum('bckgd,bkcnld->bkgcnl', qc, kg) * scale
        tok = ic[..., None] * SEL_BLOCK + jnp.arange(SEL_BLOCK)
        mask = (tok <= tc[None, None, :, None, None])[:, :, None]
        C = qc.shape[1]
        p = _masked_softmax(s.reshape(B, Hkv, G, C, K * SEL_BLOCK), mask.reshape(B, Hkv, 1, C, K * SEL_BLOCK))
        p = p.reshape(B, Hkv, G, C, K, SEL_BLOCK)
        return jnp.einsum('bkgcnl,bkcnld->bckgd', p.astype(vg.dtype), vg)

    qs = jnp.moveaxis(q.reshape(B, n_ch, SEL_Q_CHUNK, Hkv, G, D), 1, 0)
    ids = jnp.moveaxis(idx.reshape(B, Hkv, n_ch, SEL_Q_CHUNK, K), 2, 0)
    ts = jnp.arange(S).reshape(n_ch, SEL_Q_CHUNK)
    o = lax.map(chunk_fn, (qs, ids, ts))
    return jnp.moveaxis(o, 0, 1).reshape(B, S, Hkv, G, D)

def _banded_attention(q, k, v, window, sink=None):
    B, S, Hkv, G, D = q.shape
    nq = S // Q_BLOCK
    kv_len = window + Q_BLOCK
    pad = ((0, 0), (window, 0), (0, 0), (0, 0))
    idx = jnp.arange(nq)[:, None] * Q_BLOCK + jnp.arange(kv_len)[None, :]
    kb = jnp.pad(k, pad)[:, idx]
    vb = jnp.pad(v, pad)[:, idx]
    qb = q.reshape(B, nq, Q_BLOCK, Hkv, G, D)
    s = jnp.einsum('bnqkgd,bnjkd->bnkgqj', qb, kb) * (D ** -0.5)
    key_pos = idx - window
    q_pos = jnp.arange(S).reshape(nq, Q_BLOCK)
    diff = q_pos[:, :, None] - key_pos[:, None, :]
    mask = ((diff >= 0) & (diff < window) & (key_pos[:, None, :] >= 0))[None, :, None, None]
    sink_b = None if sink is None else sink.astype(jnp.float32)[None, None, :, :, None, None]
    p = _masked_softmax(s, mask, sink_b)
    o = jnp.einsum('bnkgqj,bnjkd->bnqkgd', p.astype(vb.dtype), vb)
    return o.reshape(B, S, Hkv, G, D)

def second_inputs(seed: int = 0) -> dict:
    key = jax.random.key(seed)
    ks = jax.random.split(key, 12)

    def nrm(k, shape, scale):
        return jax.random.normal(k, shape, jnp.float32) * scale

    flat_in = CMP_BLOCK * HEAD_DIM_A
    return {
        'x': nrm(ks[0], (BATCH, SEQ, D_MODEL), 1.0),
        'w_in': nrm(ks[1], (DEPTH, D_MODEL, D_IN_2), D_MODEL ** -0.5),
        'cmp_k_w1': nrm(ks[2], (DEPTH, flat_in, CMP_HIDDEN), flat_in ** -0.5),
        'cmp_k_w2': nrm(ks[3], (DEPTH, CMP_HIDDEN, HEAD_DIM_A), CMP_HIDDEN ** -0.5),
        'cmp_v_w1': nrm(ks[4], (DEPTH, flat_in, CMP_HIDDEN), flat_in ** -0.5),
        'cmp_v_w2': nrm(ks[5], (DEPTH, CMP_HIDDEN, HEAD_DIM_A), CMP_HIDDEN ** -0.5),
        'cmp_k_pos': nrm(ks[6], (DEPTH, CMP_BLOCK, HEAD_DIM_A), 0.1),
        'cmp_v_pos': nrm(ks[7], (DEPTH, CMP_BLOCK, HEAD_DIM_A), 0.1),
        'sinks': nrm(ks[8], (DEPTH, N_HEADS_B), 1.0),
        'w_out': nrm(ks[9], (DEPTH, D_MIX_2, D_MODEL), D_MIX_2 ** -0.5),
        'norm_g': 1.0 + nrm(ks[10], (DEPTH, D_MODEL), 0.01),
        'final_g': 1.0 + nrm(ks[11], (D_MODEL,), 0.01),
    }

def second_block(x, w_in, cmp_k_w1, cmp_k_w2, cmp_v_w1, cmp_v_w2, cmp_k_pos, cmp_v_pos, sinks, w_out, norm_g, final_g):
    B, S, _ = x.shape
    offsets = np.cumsum(IN_SIZES)[:-1].tolist()
    for l in range(DEPTH):
        h = _rmsnorm(x, norm_g[l])
        proj = h @ w_in[l]
        (qa, kca, vca, ksa, vsa, kwa, vwa, za, ga,
         qb, kb, vb, zb) = jnp.split(proj, offsets, axis=-1)

        qa = _rope(_heads(qa, N_HEADS_A, HEAD_DIM_A)).reshape(B, S, N_KV_A, GROUP_A, HEAD_DIM_A)
        kc = _compress(_rope(_heads(kca, N_KV_A, HEAD_DIM_A)), cmp_k_pos[l], cmp_k_w1[l], cmp_k_w2[l])
        vc = _compress(_heads(vca, N_KV_A, HEAD_DIM_A), cmp_v_pos[l], cmp_v_w1[l], cmp_v_w2[l])
        o_cmp, p_cmp = _compressed_attention(qa, kc, vc)
        sel_idx = _select_blocks(p_cmp, S)
        o_sel = _selected_attention(qa, _rope(_heads(ksa, N_KV_A, HEAD_DIM_A)), _heads(vsa, N_KV_A, HEAD_DIM_A), sel_idx)
        o_win = _banded_attention(qa, _rope(_heads(kwa, N_KV_A, HEAD_DIM_A)), _heads(vwa, N_KV_A, HEAD_DIM_A), WIN_A)
        gates = jax.nn.sigmoid(ga.astype(jnp.float32)).reshape(B, S, N_KV_A, GROUP_A, 3).astype(x.dtype)
        o_a = gates[..., 0:1] * o_cmp + gates[..., 1:2] * o_sel + gates[..., 2:3] * o_win
        y_a = o_a.reshape(B, S, WIDTH_A) * jax.nn.silu(za)

        qb = _rope(_heads(qb, N_HEADS_B, HEAD_DIM_B)).reshape(B, S, N_KV_B, GROUP_B, HEAD_DIM_B)
        o_b = _banded_attention(qb, _rope(_heads(kb, N_KV_B, HEAD_DIM_B)), _heads(vb, N_KV_B, HEAD_DIM_B),
                                WIN_B, sink=sinks[l].reshape(N_KV_B, GROUP_B))
        y_b = o_b.reshape(B, S, WIDTH_B) * jax.nn.silu(zb)

        x = x + jnp.concatenate([y_a, y_b], axis=-1) @ w_out[l]
    return _rmsnorm(x, final_g)


def setup_inputs(seed=0):
    out = dict(first_inputs(seed))
    for name, value in second_inputs(seed + 1).items():
        if name != "x":
            out[name + "_2"] = value
    return out


def reference(
    x, positions, g_pre, w_in, g_q_latent, w_uq, g_kv_latent, w_ukv, b_forget, w_out, g_post,
    w_in_2, cmp_k_w1_2, cmp_k_w2_2, cmp_v_w1_2, cmp_v_w2_2, cmp_k_pos_2, cmp_v_pos_2, sinks_2,
    w_out_2, norm_g_2, final_g_2,
):
    x = first_block(
        x, positions, g_pre, w_in, g_q_latent, w_uq, g_kv_latent, w_ukv, b_forget, w_out,
        g_post,
    )
    return second_block(
        x, w_in_2, cmp_k_w1_2, cmp_k_w2_2, cmp_v_w1_2, cmp_v_w2_2, cmp_k_pos_2, cmp_v_pos_2,
        sinks_2, w_out_2, norm_g_2, final_g_2,
    )


_drawn_inputs = setup_inputs


def setup_inputs(seed=0):
    import zlib

    import numpy as np

    out = dict(_drawn_inputs(seed))
    spreads = {}
    factors = {'g_q_latent': 8.0,
     'g_kv_latent': 7.053,
     'g_post': 4.019,
     'cmp_k_w1_2': 3.95,
     'cmp_k_w2_2': 3.97,
     'cmp_k_pos_2': 8.0,
     'cmp_v_pos_2': 6.965,
     'sinks_2': 27.795,
     'norm_g_2': 8.0,
     'final_g_2': 32.801}
    for name, (base, spread) in spreads.items():
        noise = np.random.default_rng([zlib.crc32(name.encode()), seed]).standard_normal(out[name].shape)
        drawn = base * np.exp(spread * noise) if base else spread * noise
        out[name] = __import__('jax').numpy.asarray(drawn.astype(out[name].dtype))
    for name, factor in factors.items():
        out[name] = (out[name] * factor).astype(out[name].dtype)
    return out
```

```python
import math
from contextlib import ExitStack

import concourse.bass as bass
from concourse import mybir
import numpy as np

F32 = mybir.dt.float32
F32R = mybir.dt.float32r
BF16 = mybir.dt.bfloat16
I32 = mybir.dt.int32
ALU = mybir.AluOpType
ACT = mybir.ActivationFunctionType
AX = mybir.AxisListType

S = 512
P = 128
NQ = S // P
D = 2048
KT = D // P
QR_T, KV_T = 6, 4
NHEAD = 8
NPAIR = 8
NCMP, JB = 31, 32
EPS = 1e-6
NEG = -1e30
SLOTS = 4
LEAD = 2

U_MISC = 0
U_FOX = 2
U_GATE = U_FOX + 8 * NHEAD
U_LAT = U_GATE + 16
U_MLA = U_LAT + 20
U_OUT1 = U_MLA + 32
U_CMPIN = U_OUT1 + 32
U_KV = U_CMPIN + 8
U_GA = U_KV + 16
U_W1 = U_GA + 2
U_Q0 = U_W1 + 16
U_W2 = U_Q0 + 2
U_A = U_W2 + 3
U_KVB = U_A + 4 * (NHEAD - 1)
U_B = U_KVB + 4
U_OUT2 = U_B + 4 * NPAIR
U_END = U_OUT2 + 32

N_MISC = 0
N_FOX = 1
N_GATE = N_FOX + 4 * NHEAD
N_LAT = N_GATE + 8
N_MLA = N_LAT + 10
N_OUT1 = N_MLA + 28
N_CMPIN = N_OUT1 + 16
N_KV = N_CMPIN + 4
N_GA = N_KV + 8
N_A = N_GA + 1
N_KVB = N_A + 16
N_B = N_KVB + 2
N_OUT2 = N_B + 16

A_FOX, A_MLA, A_A = 0, 8, 16
ROW = [0, 128, 384, 768]
COL = [0, 512, 896, 1152]
CAUSAL = 1280
WROW = [0, 128, 384, 640]
WCOL = [0, 256, 512, 768]
BANDED = 896

MLA_TILES = [6, 4, 4, 3, 3, 6, 4, 4]
SC_FOX, SC_MLA, SC_A, SC_B = 128 ** -0.5, 192 ** -0.5, 128 ** -0.5, 64 ** -0.5


class At:

    def __init__(self, base, lap=0, per=0):
        self.base, self.lap, self.per = base, lap, per

    def __call__(self, more=0):
        return self.base + more + self.lap * self.per if self.per else self.base + more

    def on(self, more):
        return At(self.base + more, self.lap, self.per)

    def slot(self):
        assert self.per % SLOTS == 0
        return self.base % SLOTS

    def round(self):
        r = self.base // SLOTS
        return r + self.lap * (self.per // SLOTS) if self.per else r


def build(nc, t):
    ctx = ExitStack()
    with ctx:
        _build(nc, t, ctx)


def _build(nc, d, ctx):
    base = -(-nc.sbuf_base // 32) * 32
    arena = nc.sbuf_usable_end - base
    at = {"next": base}

    def place(name, shape, dtype=F32, offset=None):
        size = int(np.prod(shape[1:])) * (2 if dtype == BF16 else 4)
        if offset is None:
            offset = at["next"]
            at["next"] = offset + -(-size // 32) * 32
        at[name] = offset
        assert offset + size <= base + arena, (name, offset + size - base - arena)
        return nc.alloc_sbuf_tensor_at(name, shape, dtype, offset=offset)

    raw = [place(f"raw{s}", [P, 1024]) for s in range(SLOTS)]
    wh = [place(f"wh{s}", [P, 1024], F32R) for s in range(SLOTS)]
    wl = [place(f"wl{s}", [P, 1024], F32R) for s in range(SLOTS)]
    xh = place("xh", [P, KT, S], F32R)
    xl = place("xl", [P, KT, S], F32R)
    o = place("o", [P, KT, S])
    rb = place("rb", [P, S])
    y = place("y", [P, S])
    yv = place("yv", [P, S])
    e_t = place("e_t", [P, S])
    gate = place("gate", [P, S])
    prob = place("prob", [P, 2 * BANDED])
    pth = place("pth", [P, 2 * BANDED], F32R)
    ptl = place("ptl", [P, 2 * BANDED], F32R)
    ident = place("ident", [P, P])
    ones = place("ones", [P, P])
    identb = place("identb", [P, P], BF16)
    maskd = place("maskd", [P, P], BF16)
    maskw = place("maskw", [P, P], BF16)
    maskc = place("maskc", [P, P], BF16)
    cvec = place("cvec", [P, 256])
    nm = place("nm", [P, 16])
    nms = place("nms", [P, 16])
    lsum = place("lsum", [P, 16])
    rinv = place("rinv", [P, 16])
    nsink = place("nsink", [P, 16])
    stage = at["next"]
    acc = place("acc", [P, S], offset=at["prob"])
    sq = [place("sq0", [P, S], offset=at["prob"] + 2048), place("sq1", [P, S], offset=at["prob"] + 4096)]
    nrm = place("nrm", [P, S], offset=at["ptl"])
    nrt = place("nrt", [P, S], offset=at["ptl"] + 2048)

    def pair(name, shape, offset=None):
        size = 4 * int(np.prod(shape[1:]))
        if offset is None:
            offset = at["next"]
            at["next"] = offset + 2 * size
        return (place(name + "_h", shape, F32R, offset), place(name + "_l", shape, F32R, offset + size))

    cos_t = place("cos_t", [P, S])
    sin_t = place("sin_t", [P, S])
    kr = pair("kr", [P, S])
    after_kr = at["next"]
    q = pair("q", [P, S])
    k = pair("k", [P, S])
    v = pair("v", [P, NQ, P])
    augq = place("augq", [P, S], F32R)
    augk = place("augk", [P, S], F32R)
    selr = place("selr", [P, 256], F32R)
    sel = place("sel", [P, NHEAD, 256], offset=at["o"])
    trif = place("trif", [P, S], offset=at["o"] + 8192)
    tri = place("tri", [P, S], F32R, offset=at["o"] + 10240)
    cum = place("cum", [P, S], F32R, offset=at["o"] + 12288)
    lf = pair("lf", [P, NQ, P], offset=at["pth"])
    zf = place("zf", [P, 3, 32], offset=at["prob"])
    ang = [e_t, y, gate]
    posi = place("posi", [P, S], I32, offset=at["yv"])
    lat = place("lat", [P, QR_T + KV_T, S], offset=after_kr)
    at["next"] = after_kr
    qa = pair("qa", [P, S])
    ka = pair("ka", [P, S])
    va = pair("va", [P, NQ, P])
    qr = pair("qr", [P, S])
    cosq, sinq = place("cosq", [P, S]), place("sinq", [P, S])
    rkv = place("rkv", [P, S], offset=at["xh"] + 10 * 2048)
    rq = place("rq", [P, S], offset=at["xh"] + 11 * 2048)
    qb = pair("qb", [P, S], offset=at["xh"] + 12 * 2048)
    kb = pair("kb", [P, S], offset=at["xh"] + 14 * 2048)
    vb = pair("vb", [P, NQ, P], offset=at["xl"] + 10 * 2048)
    x_again = [place("xa", [P, 14, S], offset=stage), place("xb", [P, 2, S], offset=at["y"])]
    again = [(x_again[0], j) for j in range(14)] + [(x_again[1], j) for j in range(2)]
    at["next"] = stage
    cos2 = place("cos2", [P, S])
    sin2 = place("sin2", [P, S])
    kcp = pair("kcp", [P, 64])
    vcp = pair("vcp", [32, 2, P])
    gat = place("gat", [P, NQ, 24])
    gaw = place("gaw", [P, 12])
    kv0 = at["next"]

    def group_kv(g, where):
        return {n: pair(f"{n}{g}", [P, S] if n[0] == "k" else [P, NQ, P], where + 4096 * i)
                for i, n in enumerate(("ks", "kw", "vs", "vw"))}

    kvg = [group_kv(0, kv0), group_kv(1, at["o"] + 8 * 2048)]
    q2 = pair("q2", [P, S], offset=kv0 + 16384)
    pc = place("pc", [P, NQ, 32], offset=kv0 + 20480)
    ptc = (place("ptc_h", [32, S], F32R, kv0 + 20992), place("ptc_l", [32, S], F32R, at["yv"]))
    cmp_in = [place("cmp_k", [P, 2, S], offset=at["gate"] + 12288), place("cmp_v", [P, 2, S], offset=at["gate"] + 8192)]
    blk = place("blk", [P, JB // 2, 64], offset=kv0 + 16384)
    blkp = [(place("blk_kh", [P, JB, 64], F32R, at["o"]), place("blk_kl", [P, JB, 64], F32R, at["gate"])),
            (place("blk_vh", [P, JB, 64], F32R, at["o"] + 8192), place("blk_vl", [P, JB, 64], F32R, at["gate"] + 12288))]
    hid = place("hid", [64, 2 * P], offset=at["o"])
    hide = place("hide", [64, 2 * P], offset=at["o"] + 1024)
    hidp = (place("hid_h", [P, 2, 2, 64], F32R, at["o"] + 2048),
            place("hid_l", [P, 2, 2, 64], F32R, at["o"] + 3072))
    vct = place("vct", [P, 64], offset=kv0 + 20480)
    kbb = pair("kbb", [P, S], offset=kv0)
    vbz = (place("vbz_h", [P, 2, NQ, P], F32R, kv0 + 4096), place("vbz_l", [P, 2, NQ, P], F32R, kv0 + 8192))
    xr2 = [place("xr20", [P, S], offset=kv0), place("xr21", [P, S], offset=kv0 + 2048)]

    names = [("g_pre", 16), ("g_q", QR_T), ("g_kv", KV_T), ("g_post", 16), ("g_2", 16), ("g_fin", 16),
             ("bf", 32), ("sinks", 16), ("invf", 1), ("sgn64", 1), ("rowok", 4), ("pos_k", 32), ("pos_v", 32)]
    cv, n = {}, 0
    for name, w in names:
        cv[name] = (n, w)
        n += w

    def c(name, j=0, w=1):
        return cvec[:, cv[name][0] + j:cv[name][0] + j + w]

    def bank(name):
        return ctx.enter_context(nc.psum_tensor(name, [P, S], F32))

    sb = [bank(f"scores{i}") for i in range(4)]
    pj = [bank(f"strip{i}") for i in range(2)]
    po, px = bank("outputs"), bank("odds")

    def sem(name):
        return ctx.enter_context(nc.semaphore(name))

    raw_full = [sem(f"raw_full{s}") for s in range(SLOTS)]
    w_hi, w_lo, w_used = sem("w_hi"), sem("w_lo"), sem("w_used")
    consts_in, cvt_done, x_in = sem("consts_in"), sem("cvt_done"), [sem(f"x_in{i}") for i in range(4)]
    pos_in, tri_in, tab2_in = sem("pos_in"), sem("tri_in"), sem("tab2_in")
    x_hi, x_lo, sq_done, sq_used = sem("x_hi"), sem("x_lo"), sem("sq_done"), sem("sq_used")
    acc_ready, sum_done, ms_done, rs_done, rb_done = (sem("acc_ready"), sem("sum_done"), sem("ms_done"),
                                                      sem("rs_done"), sem("rb_done"))
    y_done, ev_act, r_done = sem("y_done"), sem("ev_act"), sem("r_done")
    vt_done = sem("vt_done")
    s_done, nm_done, p_exp, p_norm = sem("s_done"), sem("nm_done"), sem("p_exp"), sem("p_norm")
    pt_done, pt_hi, pt_lo, pv_done, o_done = (sem("pt_done"), sem("pt_hi"), sem("pt_lo"), sem("pv_done"),
                                              sem("o_done"))
    sc_done, pc_exp, pc_norm, ptc_done, ptc_hi, ptc_lo = (sem("sc_done"), sem("pc_exp"), sem("pc_norm"),
                                                          sem("ptc_done"), sem("ptc_hi"), sem("ptc_lo"))
    red, tab, lfs, lft, cumd, aug, augd, selc = (sem("red"), sem("tab"), sem("lfs"), sem("lft"), sem("cumd"),
                                                 sem("aug"), sem("augd"), sem("selc"))
    krd, lat_act, cumh = sem("krd"), sem("lat_act"), sem("cumh")
    xn_in, xn_done, xn_out, x_back = sem("xn_in"), sem("xn_done"), sem("xn_out"), sem("x_back")
    xn_in2 = sem("xn_in2")
    gad, hact, hdve, hpe, fin, stored = sem("gad"), sem("hact"), sem("hdve"), sem("hpe"), sem("fin"), sem("stored")
    blk_made, blk_hi, blk_lo, hid_turned = sem("blk_made"), sem("blk_hi"), sem("blk_lo"), sem("hid_turned")
    scaled = sem("scaled")
    block = ctx.enter_context(nc.Block())

    @block.sync
    def _(sp):
        for dst, name in ((ident, "ident"), (ones, "ones"), (cvec, "cvec")):
            sp.dma_start(dst[:, :n] if dst is cvec else dst[:, :], d[name]).then_inc(consts_in, 16)
        for dst, name in ((identb, "identb"), (maskd, "maskd"), (maskw, "maskw"), (maskc, "maskc")):
            sp.dma_start(dst[:, :], d[name]).then_inc(consts_in, 16)

        def x_part(i):
            sp.dma_start(o[:, 4 * i:4 * i + 4, :], d["xt"][:, 4 * i:4 * i + 4, :]).then_inc(x_in[i], 16)

        x_part(0)
        for u in range(SLOTS):
            sp.dma_start(raw[u][:, :], d["w"][u, :, :]).then_inc(raw_full[u], 16)
            if u in (1, 2):
                x_part(u)
        x_part(3)

        def rounds(first, end):
            with sp.Fori(first, end) as r:
                for s in range(SLOTS):
                    sp.wait_ge(w_lo, r * SLOTS + (s + 1 - SLOTS))
                    sp.dma_start(raw[s][:, :], d["w"][bass.ds(r * SLOTS + s, 1), :, :].rearrange("a p n -> p (a n)"))\
                      .then_inc(raw_full[s], 16)

        between = (U_CMPIN + 8) // SLOTS
        rounds(1, between)
        for j in range(0, KT, 4):
            sp.wait_ge(xn_done, j + 4)
            sp.dma_start(d["xn"][:, j:j + 4, :], o[:, j:j + 4, :]).then_inc(xn_out, 16)
        rounds(between, U_END // SLOTS)
        for u in range(U_END // SLOTS * SLOTS, U_END):
            sp.wait_ge(w_lo, u + 1 - SLOTS)
            sp.dma_start(raw[u % SLOTS][:, :], d["w"][u, :, :]).then_inc(raw_full[u % SLOTS], 16)

    @block.gpsimd
    def _(g):
        g.dma_start(posi[:, :], d["pos"]).then_inc(pos_in, 16)
        g.wait_ge(x_lo, KT)
        g.dma_start(sel[:, :, :], d["sel"]).then_inc(tri_in, 16)
        g.dma_start(trif[:, :], d["tri"]).then_inc(tri_in, 16)
        g.wait_ge(o_done, 16)
        for j, w in ((0, 4), (4, 4), (8, 4), (12, 2)):
            g.dma_start(x_again[0][:, j:j + w, :], d["xt"][:, j:j + w, :]).then_inc(x_back, 16)
        g.dma_start(x_again[1][:, :, :], d["xt"][:, 14:16, :]).then_inc(x_back, 16)
        g.wait_ge(x_back, 16 * 5)
        for j in range(KT):
            g.wait_ge(scaled, j + 1)
            g.tensor_tensor(o[:, j, :], o[:, j, :], again[j][0][:, again[j][1], :], ALU.add).then_inc(xn_done, 1)
        g.wait_ge(xn_out, 16 * 4)
        g.wait_ge(rb_done, 5)
        g.dma_start(cos2[:, :], d["cos_a"]).then_inc(tab2_in, 16)
        g.dma_start(sin2[:, :], d["sin_a"]).then_inc(tab2_in, 16)
        g.wait_ge(r_done, N_KVB)
        g.dma_start(cos2[:, :], d["cos_b"]).then_inc(tab2_in, 16)
        g.dma_start(sin2[:, :], d["sin_b"]).then_inc(tab2_in, 16)
        g.wait_ge(o_done, 32)
        for j in range(2):
            g.dma_start(xr2[j][:, :], d["xn"][:, j, :]).then_inc(xn_in if j == 0 else xn_in2, 16)
        with g.Fori(0, KT // 2 - 1) as i:
            for j in range(2):
                g.wait_ge(y_done, N_OUT2 + 1 + j + i * 2)
                g.dma_start(xr2[j][:, :], d["xn"][:, bass.ds(2 * i + 2 + j, 1), :].rearrange("p a n -> p (a n)"))\
                 .then_inc(xn_in if j == 0 else xn_in2, 16)
        for j in range(KT):
            g.wait_ge(fin, j + 1)
            g.dma_start(d["out"][:, j, :], o[:, j, :]).then_inc(stored, 16)
        g.wait_ge(stored, 16 * KT)


    def three(pe, out, ah, al, bh, bl, first, last, shared=False):
        pe.matmul(out, ah, bh, start=first, stop=False, skip_group_check=shared)
        pe.matmul(out, ah, bl, start=False, stop=False, skip_group_check=shared)
        return pe.matmul(out, al, bh, start=False, stop=last, skip_group_check=shared)

    def unit(pe, u, tiles, out, first, last, operand=(xh, xl), ready=None, free=None):
        s = u.slot()
        pe.wait_ge(w_lo, u(1))
        if free is not None:
            pe.wait_ge(y_done, free)
        for i, (a, b) in enumerate(tiles):
            if ready is not None:
                pe.wait_ge(ready[0], ready[1] + b + 1)
            cols = slice(128 * a, 128 * a + 128)
            ins = three(pe, out, wh[s][:, cols], wl[s][:, cols], operand[0][:, b, :], operand[1][:, b, :],
                        first and i == 0, last and i == len(tiles) - 1)
        ins.then_inc(w_used, 1)

    def half(pe, u, n_at, h, free, ready=None):
        unit(pe, u, [(i, 8 * h + i) for i in range(8)], pj[n_at % 2][:, :], h == 0, h == 1,
             ready=ready, free=free if h == 0 else None)

    def scores(pe, a, terms, last_a=None):
        for t in range(NQ):
            keys = slice(0, P * (t + 1))
            mine = slice(P * t, P * t + P)
            out = sb[t][:, keys]
            for i, (qq, kk, p0, rows) in enumerate(terms):
                r = slice(p0, p0 + rows)
                three(pe, out, qq[0][r, mine], qq[1][r, mine], kk[0][r, keys], kk[1][r, keys], i == 0, False)
            yield t, out, mine, keys

    def causal(pe, t, a):
        pe.matmul(sb[t][:, P * t:P * t + P], identb[:, :], maskd[:, :], start=False, stop=True).then_inc(s_done, 1)

    def pe_scores(pe, a, terms, extra=False):
        for t, out, mine, keys in scores(pe, a, terms):
            if extra:
                pe.matmul(out, augq[:, mine], augk[:, keys], start=False, stop=False)
            causal(pe, t, a)

    def pe_turn(pe, a):
        pe.wait_ge(p_norm, a + 1)
        for t in range(NQ):
            for w in range(t, NQ):
                ins = pe.transpose(sb[t][:, P * (w - t):P * (w - t) + P], prob[:, ROW[w] + P * t:ROW[w] + P * t + P],
                                   ident[:, :])
            ins.then_inc(pt_done, 1)

    def pe_out(pe, a, vv, first=True, last=True, outs_done=None):
        if first and outs_done is not None:
            pe.wait_ge(o_done, outs_done)
        for t in range(NQ):
            pe.wait_ge(pt_lo, 4 * a + t + 1)
            cols = slice(COL[t], COL[t] + S - P * t)
            ins = three(pe, po[:, P * t:S], vv[0][:, t, :], vv[1][:, t, :], pth[:, cols], ptl[:, cols],
                        first and t == 0, last and t == NQ - 1)
        if last:
            ins.then_inc(pv_done, 1)

    def pe_turn_v(pe, strip):
        pe.wait_ge(y_done, strip)
        pe.wait_ge(r_done, strip - 1)
        for t in range(NQ):
            ins = pe.transpose(px[:, P * t:P * t + P], yv[:, P * t:P * t + P], ident[:, :])
        ins.then_inc(vt_done, 1)

    def pe_aug(pe, i, which):
        pe.wait_ge(selc, i + 1)
        pe.matmul(px[:, :], selr[:, P * which:P * which + P], cum[:, :], start=True, stop=True).then_inc(aug, 1)

    def pe_first(pe, u, n_at, count, squares):
        for j in range(KT):
            pe.wait_ge(x_lo, count + j + 1)
            for s in range(2):
                v_ = At(u + 2 * (j // 8) + s)
                if j % 8 == 0:
                    pe.wait_ge(w_lo, v_(1))
                cols = slice(P * (j % 8), P * (j % 8) + P)
                ins = three(pe, pj[(n_at + s) % 2][:, :], wh[v_.slot()][:, cols], wl[v_.slot()][:, cols],
                            xh[:, j, :], xl[:, j, :], j == 0, j == KT - 1)
                if j % 8 == 7:
                    ins.then_inc(w_used, 1)
            pe.wait_ge(sq_done, squares + j + 1)
            pe.matmul(px[:, :], ones[:, :], sq[j % 2][:, :], start=j == 0, stop=j == KT - 1).then_inc(sq_used, 1)

    def pe_sum(pe, i):
        pe.wait_ge(acc_ready, i + 1)
        pe.matmul(px[:, :], ones[:, :], acc[:, :], start=True, stop=True).then_inc(sum_done, 1)

    @block.tensor
    def _(pe):
        pe.wait_ge(consts_in, 16 * 7)
        pe_first(pe, U_MISC, N_MISC, 0, 0)
        for i in range(4):
            for h in range(2):
                if i == 1 and h == 0:
                    pe.wait_ge(lfs, 1)
                    for t in range(NQ):
                        ins = pe.transpose(px[:, P * t:P * t + P], yv[:, P * t:P * t + P], ident[:, :])
                    ins.then_inc(lft, 1)
                if i == 2 and h == 0:
                    pe.wait_ge(lfs, 3)
                    for t in range(NQ):
                        for part in range(2):
                            ins = pe.matmul(px[:, P * t:S], lf[part][:, t, :], tri[:, 0:S - P * t],
                                            start=t == 0 and part == 0, stop=t == NQ - 1 and part == 1)
                    ins.then_inc(cumd, 1)
                if i == 2 and h == 1:
                    pe_aug(pe, 0, 0)
                if i == 3 and h == 0:
                    pe.wait_ge(augd, 1)
                    pe_aug(pe, 0, 1)
                if i == 3 and h == 1:
                    pe.wait_ge(augd, 2)
                    pe_turn_v(pe, N_FOX + 3)
                n_ = N_FOX + i
                if i:
                    half(pe, At(U_FOX + 2 * i + h), n_, h, n_ - 1)

        def fox(h, u, n_, last):
            for s in range(8):
                if s == 0:
                    pe.wait_ge(r_done, n_(-1))
                    pe_scores(pe, h, [(q, k, 0, P)], extra=True)
                if s == 2:
                    pe_turn(pe, h)
                if s == 4:
                    pe_out(pe, h, v)
                if not last:
                    if s == 5:
                        pe_aug(pe, h + 1, 0)
                    if s == 6:
                        pe.wait_ge(augd, 2 * h + 3)
                        pe_aug(pe, h + 1, 1)
                    if s == 7:
                        pe.wait_ge(augd, 2 * h + 4)
                        pe_turn_v(pe, n_(3))
                half(pe, u.on(s), n_.base + s // 2, s % 2, n_(s // 2 - 1))

        with pe.Fori(0, NHEAD - 1) as h:
            fox(h, At(U_FOX + 8, h, 8), At(N_FOX + 4, h, 4), False)
        fox(NHEAD - 1, At(U_GATE), At(N_GATE), True)
        with pe.Fori(0, 2) as i:
            for s in range(4):
                half(pe, At(U_GATE + 8 + s, i, 4), N_GATE + 4 + s // 2, s % 2, N_GATE + 3 + s // 2 + i * 2)
        with pe.Fori(0, 5) as i:
            for s in range(4):
                half(pe, At(U_LAT + s, i, 4), N_LAT + s // 2, s % 2, N_LAT - 1 + s // 2 + i * 2)
        pe_sum(pe, 0)
        pe.wait_ge(ms_done, 2)
        pe_sum(pe, 1)

        def mla_unit(s, u, n_, first):
            which = [0, 1, 2, 3, 3, 4, 5, 6][s]
            if s < 2 or s >= 5 or s == 2:
                tiles = [(i, (0 if MLA_TILES[s] == 6 else QR_T) + i) for i in range(MLA_TILES[s])]
                f, l = True, True
            else:
                tiles = [(i, 3 * (s - 3) + i) for i in range(3)]
                f, l = s == 3, s == 4
            free = n_(which - 1) if which else n_(0)
            unit(pe, u.on(s), tiles, pj[which % 2][:, :], f, l, ready=(x_lo, KT) if first else None,
                 free=free if f else None)

        def pe_mla_scores(a, qq, kk, part):
            pe_scores(pe, a, [(qq, kk, 0, P), (qr, kr, 64 * part, 64)])

        def mla(p, u, n_, steps):
            a = A_MLA + 2 * p
            pe.wait_ge(r_done, n_(-1))
            pe_mla_scores(a, qa, ka, 0)
            if steps:
                mla_unit(0, u, n_, False)
            pe_turn_v(pe, n_(0))
            if steps:
                mla_unit(1, u, n_, False)
            pe_turn(pe, a)
            if steps:
                mla_unit(2, u, n_, False)
                mla_unit(3, u, n_, False)
            pe_out(pe, a, va, outs_done=a)
            pe_mla_scores(a + 1, qb, kb, 1)
            if steps:
                mla_unit(4, u, n_, False)
                pe_turn_v(pe, n_(3))
                mla_unit(5, u, n_, False)
            pe_turn(pe, a + 1)
            if steps:
                mla_unit(6, u, n_, False)
                mla_unit(7, u, n_, False)
            else:
                pe.wait_ge(r_done, n_(0))
            pe_out(pe, a + 1, vb, outs_done=a + 1)

        n0 = At(N_MLA)
        for s in range(8):
            if s == 5:
                pe_turn_v(pe, n0(3))
            mla_unit(s, At(U_MLA), n0, True)
        with pe.Fori(0, 3) as p:
            mla(p, At(U_MLA + 8, p, 8), At(N_MLA + 7, p, 7), True)
        mla(3, At(U_OUT1), At(N_OUT1), False)
        half(pe, At(U_OUT1), N_OUT1, 0, N_OUT1, ready=(x_lo, 2 * KT - 6))
        half(pe, At(U_OUT1 + 1), N_OUT1, 1, None, ready=(x_lo, 2 * KT - 6))
        half(pe, At(U_OUT1 + 2), N_OUT1 + 1, 0, N_OUT1)
        half(pe, At(U_OUT1 + 3), N_OUT1 + 1, 1, None)
        with pe.Fori(0, KT // 2 - 1) as i:
            for s in range(4):
                half(pe, At(U_OUT1 + 4 + s, i, 4), N_OUT1 + s // 2, s % 2, N_OUT1 + 1 + s // 2 + i * 2)
        pe_sum(pe, 2)
        pe_first(pe, U_CMPIN, N_CMPIN, 3 * KT - 6, KT)
        for s in range(4, 8):
            half(pe, At(U_CMPIN + s), N_CMPIN + s // 2, s % 2, N_CMPIN - 1 + s // 2)
        with pe.Fori(0, 2) as i:
            for s in range(4):
                half(pe, At(U_KV + s, i, 4), N_KV + s // 2, s % 2, N_KV - 1 + s // 2 + i * 2)
        with pe.Fori(0, 2) as i:
            for s in range(4):
                half(pe, At(U_KV + 8 + s, i, 4), N_KV + 4 + s // 2, s % 2, N_KV + 3 + s // 2 + i * 2)
                if s % 2 == 1:
                    pe_turn_v(pe, N_KV + 5 + s // 2 + i * 2)
        half(pe, At(U_GA), N_GA, 0, N_GA - 1)
        half(pe, At(U_GA + 1), N_GA, 1, None)
        pe_turn_v(pe, N_GA + 1)
        def turn_hidden(which):
            pe.wait_ge(gad, which + 1)
            for m in range(2):
                ins = pe.transpose(sb[2 + which][:, 64 * m:64 * m + 64], hid[:, P * m:P * m + P], ident[0:64, 0:64])
            ins.then_inc(hid_turned, 1)

        for which in range(2):
            pe.wait_ge(blk_lo, 2 * which + 2)
            for i in range(8):
                u = At(U_W1 + 8 * which + i)
                pe.wait_ge(w_lo, u(1))
                for a in range(4):
                    j = 4 * i + a
                    cols = slice(256 * a, 256 * a + 256)
                    ins = three(pe, sb[which][0:64, 0:256], blkp[which][0][:, j, :], blkp[which][1][:, j, :],
                                wh[u.slot()][:, cols], wl[u.slot()][:, cols], j == 0, j == JB - 1)
                ins.then_inc(w_used, 1)
                if which and i == 1:
                    turn_hidden(0)
        half(pe, At(U_Q0), N_A, 0, N_A - 1)
        turn_hidden(1)
        half(pe, At(U_Q0 + 1), N_A, 1, None)
        pe.wait_ge(hdve, 2)
        u = At(U_W2)
        pe.wait_ge(w_lo, u(1))
        pe.wait_ge(r_done, N_A)
        for which in range(2):
            for m in range(2):
                cols = slice(256 * which + 128 * m, 256 * which + 128 * m + 128)
                ins = three(pe, px[:, 64 * which:64 * which + 64], wh[u.slot()][:, cols], wl[u.slot()][:, cols],
                            hidp[0][:, which, m, :], hidp[1][:, which, m, :], m == 0, m == 1)
        ins.then_inc(w_used, 1)
        half(pe, At(U_W2 + 1), N_A + 1, 0, N_A)
        pe.wait_ge(hdve, 3)
        for g_ in range(2):
            ins = pe.transpose(px[0:32, P * g_:P * g_ + P], vct[:, 32 * g_:32 * g_ + 32], ident[:, :])
        ins.then_inc(hpe, 1)
        half(pe, At(U_W2 + 2), N_A + 1, 1, None)

        def a_head(h, g_, u, n_):
            kv = kvg[g_]
            a = A_A + 2 * h
            pe.wait_ge(r_done, n_(-1))
            pe_scores(pe, a, [(q2, kv["ks"], 0, P)])
            for t in range(NQ):
                mine = slice(P * t, P * t + P)
                three(pe, px[:, 32 * t:32 * t + 32], q2[0][:, mine], q2[1][:, mine],
                      kcp[0][:, 32 * g_:32 * g_ + 32], kcp[1][:, 32 * g_:32 * g_ + 32], True, False)
                ins = pe.matmul(px[:, 32 * t:32 * t + 32], identb[:, :], maskc[:, 32 * t:32 * t + 32],
                                start=False, stop=True)
            ins.then_inc(sc_done, 1)
            half(pe, u, n_.base, 0, n_(-1))
            pe_turn(pe, a)
            pe.wait_ge(pc_norm, h + 1)
            for t in range(NQ):
                ins = pe.transpose(px[0:32, P * t:P * t + P], pc[:, t, :], ident[:, :])
            ins.then_inc(ptc_done, 1)
            half(pe, u.on(1), n_.base, 1, None)
            pe_out(pe, a, kv["vs"], last=False, outs_done=16 + h)
            pe.wait_ge(ptc_lo, h + 1)
            three(pe, po[:, :], vcp[0][:, g_, :], vcp[1][:, g_, :], ptc[0][:, :], ptc[1][:, :], False, False)
            pe_scores(pe, a + 1, [(q2, kv["kw"], 0, P)])
            half(pe, u.on(2), n_.base + 1, 0, n_(0))
            pe_turn(pe, a + 1)
            half(pe, u.on(3), n_.base + 1, 1, None)
            pe_out(pe, a + 1, kv["vw"], first=False)

        pe.wait_ge(hdve, 4)
        with pe.Fori(0, 4) as h:
            a_head(h, 0, At(U_A, h, 4), At(N_A + 2, h, 2))
        with pe.Fori(4, 7) as h:
            a_head(h, 1, At(U_A, h, 4), At(N_A + 2, h, 2))
        a_head(7, 1, At(U_KVB), At(N_KVB))
        for s in range(4):
            if s == 1:
                pe_turn_v(pe, N_KVB + 2)
            half(pe, At(U_B + s), N_B + s // 2, s % 2, N_B - 1 + s // 2)

        def b_scores(p):
            for hh in range(2):
                r = slice(64 * hh, 64 * hh + 64)
                for t in range(NQ):
                    lo_ = max(t - 1, 0)
                    c0 = WROW[t] - (384 if t >= 2 else 0)
                    out = sb[2 * hh + t // 2]
                    w = P * (t + 1 - lo_)
                    mine = slice(P * t, P * t + P)
                    keys = slice(P * lo_, P * t + P)
                    three(pe, out[:, c0:c0 + w], q2[0][r, mine], q2[1][r, mine], kbb[0][r, keys], kbb[1][r, keys],
                          True, False)
                    if t:
                        pe.matmul(out[:, c0:c0 + P], identb[:, :], maskw[:, :], start=False, stop=False)
                    pe.matmul(out[:, c0 + w - P:c0 + w], identb[:, :], maskd[:, :], start=False, stop=True)\
                      .then_inc(s_done, 1)

        def b_pair(p, u, n_, steps):
            a = 2 * NHEAD + 16
            pe.wait_ge(r_done, n_(-1))
            b_scores(p)
            if steps:
                half(pe, u, n_.base, 0, n_(-1))
                half(pe, u.on(1), n_.base, 1, None)
            pe.wait_ge(p_norm, a + p + 1)
            for hh in range(2):
                for t in range(NQ):
                    for w in range(t, min(t + 2, NQ)):
                        c0 = BANDED * hh + WROW[w] + (0 if w > t or t == 0 else P)
                        ins = pe.transpose(sb[2 * hh + t // 2][:, 256 * (t % 2) + P * (w - t):256 * (t % 2) + P * (w - t) + P],
                                           prob[:, c0:c0 + P], ident[:, :])
                ins.then_inc(pt_done, 1)
            if steps:
                half(pe, u.on(2), n_.base + 1, 0, n_(0))
            pe.wait_ge(o_done, 24 + p)
            pe.wait_ge(pt_lo, 4 * a + 2 * p + 2)
            for hh in range(2):
                for t in range(NQ):
                    w = P * (min(t + 2, NQ) - t)
                    cols = slice(BANDED * hh + WCOL[t], BANDED * hh + WCOL[t] + w)
                    ins = three(pe, po[:, P * t:P * t + w], vbz[0][:, hh, t, :], vbz[1][:, hh, t, :],
                                pth[:, cols], ptl[:, cols], hh == 0 and t == 0, hh == 1 and t == NQ - 1, True)
            ins.then_inc(pv_done, 1)
            if steps:
                half(pe, u.on(3), n_.base + 1, 1, None)

        with pe.Fori(0, NPAIR - 1) as p:
            b_pair(p, At(U_B + 4, p, 4), At(N_B + 2, p, 2), True)
        b_pair(NPAIR - 1, At(U_OUT2), At(N_OUT2), False)
        for s in range(4):
            half(pe, At(U_OUT2 + s), N_OUT2 + s // 2, s % 2, N_OUT2 - 1 + s // 2,
                 ready=(x_lo, 4 * KT - 6) if s < 2 else None)
        with pe.Fori(0, KT // 2 - 1) as i:
            for s in range(4):
                half(pe, At(U_OUT2 + 4 + s, i, 4), N_OUT2 + s // 2, s % 2, N_OUT2 + 1 + s // 2 + i * 2)
        pe_sum(pe, 3)

    def act_hi(a, u, cols=1024):
        s = u.slot()
        a.wait_ge(raw_full[s], (u.round() + 1) * 16)
        if u.per or u.base >= SLOTS:
            a.wait_ge(w_used, u(1 - SLOTS))
        a.activation(wh[s][:, :cols], raw[s][:, :cols], ACT.Copy).then_inc(w_hi, 1)

    def act_part(a, n_, dst, src):
        a.wait_ge(y_done, n_ + 1)
        a.activation(dst, src, ACT.Copy).then_inc(ev_act, 1)

    def act_part_v(a, turned, dst):
        a.wait_ge(vt_done, turned)
        a.activation(dst, px[:, :].rearrange("p (t d) -> p t d", t=NQ), ACT.Copy).then_inc(ev_act, 1)

    def act_gate(a, n_, src):
        a.wait_ge(y_done, n_ + 1)
        a.activation(e_t[:, :], src, ACT.Tanh, scale=0.5).then_inc(ev_act, 1)

    def act_exps(a, i, scale):
        a.wait_ge(nm_done, i + 1)
        for t in range(NQ):
            w = P * (t + 1)
            a.activation(prob[:, ROW[t]:ROW[t] + w], sb[t][:, 0:w], ACT.Exp, bias=nms[:, t:t + 1], scale=scale,
                         accum_out=lsum[:, t:t + 1]).then_inc(p_exp, 1)

    def act_turned(a, i):
        for t in range(NQ):
            a.wait_ge(pt_done, 4 * i + t + 1)
            w = S - P * t
            a.activation(pth[:, COL[t]:COL[t] + w], sb[t][:, 0:w], ACT.Copy).then_inc(pt_hi, 1)

    def act_rms(a, i):
        a.wait_ge(ms_done, i + 1)
        a.activation(nrt[:, :], nrm[:, :], ACT.Ln)
        a.drain()
        a.activation(nrt[:, :], nrt[:, :], ACT.Exp, scale=-0.5).then_inc(rs_done, 1)

    @block.scalar
    def _(a):
        a.wait_ge(consts_in, 16 * 7)
        act_hi(a, At(0))
        act_hi(a, At(1))
        for j in range(KT):
            if j % 4 == 0:
                a.wait_ge(x_in[j // 4], 16)
            a.activation(xh[:, j, :], o[:, j, :], ACT.Copy, scale=c("g_pre", j)).then_inc(x_hi, 1)
            if j >= 2:
                a.wait_ge(sq_used, j - 1)
            a.activation(sq[j % 2][:, :], o[:, j, :], ACT.Square).then_inc(sq_done, 1)
            if j in (4, 6):
                act_hi(a, At(j // 2))
        a.wait_ge(tab, 1)
        a.activation(sin_t[:, :], ang[0][:, :], ACT.Sin)
        a.activation(cos_t[:, :], ang[2][:, :], ACT.Sin).then_inc(red, 1)
        act_rms(a, 0)
        a.wait_ge(y_done, 1)
        a.activation(kr[0][0:64, :], y[0:64, :], ACT.Copy)
        a.activation(kr[0][64:128, :], y[0:64, :], ACT.Copy).then_inc(ev_act, 1)
        act_hi(a, At(4))
        act_hi(a, At(5))
        act_part(a, N_FOX, q[0][:, :], y[:, :])
        a.wait_ge(lft, 1)
        a.wait_ge(tri_in, 32)
        a.activation(tri[:, :], trif[:, :], ACT.Copy)
        a.wait_ge(lfs, 2)
        a.activation(zf[:, 1, :], zf[:, 1, :], ACT.Exp, scale=-1.0)
        a.drain()
        a.activation(zf[:, 1, :], zf[:, 1, :], ACT.Ln, bias=1.0).then_inc(lat_act, 1)
        act_hi(a, At(6))
        act_hi(a, At(7))
        act_part(a, N_FOX + 1, k[0][:, :], y[:, :])
        a.wait_ge(cumd, 1)
        a.activation(cum[0:64, :], px[0:64, :], ACT.Copy, scale=1.0 / SC_FOX).then_inc(cumh, 1)
        a.wait_ge(krd, 1)

        def act_sel(i, reg):
            a.activation(selr[:, :], sel[:, reg, :].rearrange("p a n -> p (a n)") if not isinstance(reg, int)
                         else sel[:, reg, :], ACT.Copy).then_inc(selc, 1)

        def act_aug(count, dst):
            a.wait_ge(aug, count)
            a.activation(dst[:, :], px[:, :], ACT.Copy).then_inc(augd, 1)

        act_sel(0, 0)
        act_hi(a, At(8))
        act_hi(a, At(9))
        act_aug(1, augk)
        act_hi(a, At(10))
        act_aug(2, augq)
        act_hi(a, At(11))
        act_part_v(a, 1, v[0][:, :, :])

        def fox(h, u, n_, last):
            for s in range(8):
                act_hi(a, u.on(s + LEAD))
                if s == 0:
                    act_gate(a, n_(-1), y[:, :])
                    act_exps(a, h, SC_FOX)
                if s == 1 and not last:
                    act_sel(h + 1, bass.ds(h + 1, 1))
                if s == 2:
                    if last:
                        act_gate(a, n_(0), y[:, :])
                    else:
                        act_part(a, n_(0), q[0][:, :], y[:, :])
                    act_turned(a, h)
                if s == 4:
                    if last:
                        act_gate(a, n_(1), y[:, :])
                    else:
                        act_part(a, n_(1), k[0][:, :], y[:, :])
                if s == 5 and not last:
                    act_aug(2 * h + 3, augk)
                if s == 6:
                    if last:
                        act_gate(a, n_(2), y[:, :])
                    else:
                        act_aug(2 * h + 4, augq)
                if s == 7:
                    if last:
                        act_gate(a, n_(3), y[:, :])
                    else:
                        act_part_v(a, h + 2, v[0][:, :, :])

        with a.Fori(0, NHEAD - 1) as h:
            fox(h, At(U_FOX + 8, h, 8), At(N_FOX + 4, h, 4), False)
        fox(NHEAD - 1, At(U_GATE), At(N_GATE), True)

        def two_strips(u, evac):
            act_hi(a, u.on(2))
            act_hi(a, u.on(3))
            evac(0)
            act_hi(a, u.on(4))
            act_hi(a, u.on(5))
            evac(1)

        with a.Fori(0, 2) as i:
            two_strips(At(U_GATE + 8, i, 4), lambda j: act_gate(a, N_GATE + 4 + j + i * 2, y[:, :]))

        def lat_square(n_, src):
            a.wait_ge(y_done, n_ + 1)
            a.activation(e_t[:, :], src, ACT.Square).then_inc(ev_act, 1)

        with a.Fori(0, 5) as i:
            two_strips(At(U_LAT, i, 4), lambda j: lat_square(
                N_LAT + j + i * 2, lat[:, bass.ds(2 * i + j, 1), :].rearrange("p a n -> p (a n)")))
        a.wait_ge(w_used, U_MLA)
        for j in range(QR_T + KV_T):
            g_ = c("g_q", j) if j < QR_T else c("g_kv", j - QR_T)
            a.activation(xh[:, j, :], lat[:, j, :], ACT.Copy, scale=g_).then_inc(x_hi, 1)
        act_rms(a, 1)
        act_rms(a, 2)

        def mla_evacs(n_, k_):
            if k_ in (2, 6):
                return
            dst = {0: qa, 1: ka, 3: qr, 4: qb, 5: kb}[k_]
            act_part(a, n_(k_), dst[0][:, :], y[:, :])

        def mla_hi(u, s):
            m = (s + LEAD) % 8
            act_hi(a, u.on(s + LEAD), 1024 if m < 2 else 128 * MLA_TILES[m])

        n0 = At(N_MLA)
        u0 = At(U_MLA)
        for s, strip in enumerate([None, 0, 1, None, None, 3, 4, 5]):
            mla_hi(u0, s)
            if s == 5:
                act_part_v(a, NHEAD + 1, va[0][:, :, :])
            if strip is not None:
                mla_evacs(n0, strip)

        def mla(p, u, n_, steps):
            i = A_MLA + 2 * p
            if steps:
                mla_hi(u, 0)
            act_exps(a, i, SC_MLA)
            if steps:
                mla_hi(u, 1)
            act_part_v(a, NHEAD + 2 + p * 2, vb[0][:, :, :])
            if steps:
                mla_evacs(n_, 0)
                mla_hi(u, 2)
                mla_evacs(n_, 1)
            act_turned(a, i)
            if steps:
                mla_hi(u, 3)
                mla_hi(u, 4)
            act_exps(a, i + 1, SC_MLA)
            if steps:
                mla_hi(u, 5)
                act_part_v(a, NHEAD + 3 + p * 2, va[0][:, :, :])
                mla_evacs(n_, 3)
                mla_hi(u, 6)
                mla_evacs(n_, 4)
            act_turned(a, i + 1)
            if steps:
                mla_hi(u, 7)
                mla_evacs(n_, 5)

        with a.Fori(0, 3) as p:
            mla(p, At(U_MLA + 8, p, 8), At(N_MLA + 7, p, 7), True)
        mla(3, At(U_OUT1), At(N_OUT1), False)
        a.wait_ge(o_done, 16)
        for j in range(KT):
            a.activation(xh[:, j, :], o[:, j, :], ACT.Copy).then_inc(x_hi, 1)

        def out_square(n_, src):
            a.wait_ge(y_done, n_ + 1)
            a.activation(e_t[:, :], src, ACT.Square).then_inc(ev_act, 1)

        two_strips(At(U_OUT1), lambda j: out_square(N_OUT1 + j, o[:, j, :]))
        with a.Fori(0, KT // 2 - 1) as i:
            two_strips(At(U_OUT1 + 4, i, 4), lambda j: out_square(
                N_OUT1 + 2 + j + i * 2, o[:, bass.ds(2 * i + 2 + j, 1), :].rearrange("p a n -> p (a n)")))
        act_hi(a, At(U_CMPIN + 2))
        act_hi(a, At(U_CMPIN + 3))
        act_rms(a, 3)
        for j in range(KT):
            a.wait_ge(xn_done, j + 1)
            a.activation(xh[:, j, :], o[:, j, :], ACT.Copy, scale=c("g_2", j)).then_inc(x_hi, 1)
            if j >= 2:
                a.wait_ge(sq_used, KT + j - 1)
            a.activation(sq[j % 2][:, :], o[:, j, :], ACT.Square).then_inc(sq_done, 1)
        act_hi(a, At(U_CMPIN + 4))
        act_hi(a, At(U_CMPIN + 5))
        act_rms(a, 4)
        two_strips(At(U_CMPIN + 4), lambda j: None)

        def kv_loop(base, nbase, first_turn):
            for g_ in range(2):
                def evac(j):
                    n_ = nbase + 2 * g_ + j
                    if first_turn is None:
                        blocks_hi(2 * g_ + j)
                        act_part(a, n_, kvg[g_][("ks", "kw")[j]][0][:, :], y[:, :])
                    else:
                        act_part_v(a, first_turn + 2 * g_ + j, kvg[g_][("vs", "vw")[j]][0][:, :, :])
                two_strips(At(base + 4 * g_), evac)

        def blocks_hi(i):
            a.wait_ge(blk_made, i + 1)
            a.activation(blkp[i // 2][0][:, 16 * (i % 2):16 * (i % 2) + 16, :], blk[:, :, :], ACT.Copy).then_inc(blk_hi, 1)

        kv_loop(U_KV, N_KV, None)
        kv_loop(U_KV + 8, N_KV + 4, 17)
        act_hi(a, At(U_GA + 2))
        act_hi(a, At(U_GA + 3))
        a.wait_ge(vt_done, 21)
        a.activation(gat[:, :, :], px[:, :].rearrange("p (t d) -> p t d", t=NQ)[:, :, 0:24], ACT.Tanh,
                     scale=0.5).then_inc(ev_act, 1)
        def hidden_hi(which):
            a.wait_ge(hid_turned, which + 1)
            a.activation(hidp[0][:, which, :, :], sb[2 + which][:, 0:P].rearrange("p (m c) -> p m c", m=2), ACT.Copy,
                         scale=0.5).then_inc(hact, 1)

        for which in range(2):
            for i in range(8):
                act_hi(a, At(U_W1 + 8 * which + i + LEAD))
                if which and i == 2:
                    hidden_hi(0)
            a.wait_ge(w_used, U_W1 + 8 * which + 8)
            a.activation(hide[:, :], sb[which][0:64, 0:256], ACT.Tanh, scale=0.5).then_inc(hact, 1)
        act_hi(a, At(U_W2), 512)
        hidden_hi(1)
        act_hi(a, At(U_W2 + 1))
        act_part(a, N_A, q2[0][:, :], y[:, :])
        a.wait_ge(w_used, U_W2 + 1)
        a.activation(kcp[0][:, :], px[:, 0:64], ACT.Copy).then_inc(hact, 1)
        act_hi(a, At(U_W2 + 2))
        a.wait_ge(hpe, 1)
        a.activation(vcp[0][:, :, :], px[0:32, 0:256].rearrange("p (g d) -> p g d", g=2), ACT.Copy).then_inc(hact, 1)
        act_hi(a, At(U_A))
        act_hi(a, At(U_A + 1))

        def a_head(h, g_, u, n_, last):
            i = A_A + 2 * h
            act_hi(a, u.on(2))
            act_gate(a, n_(-1), y[:, :])
            act_exps(a, i, SC_A)
            a.wait_ge(pc_exp, h + 1)
            for t in range(NQ):
                ins = a.activation(pc[:, t, :], px[:, 32 * t:32 * t + 32], ACT.Exp, bias=nms[:, 4 + t:5 + t],
                                   scale=SC_A, accum_out=lsum[:, 4 + t:5 + t])
            ins.then_inc(hact, 1)
            act_hi(a, u.on(3))
            act_turned(a, i)
            a.wait_ge(ptc_done, h + 1)
            a.activation(ptc[0][:, :], px[0:32, :], ACT.Copy).then_inc(ptc_hi, 1)
            act_hi(a, u.on(4))
            act_exps(a, i + 1, SC_A)
            if last:
                act_part(a, n_(0), kbb[0][:, :], y[:, :])
            else:
                act_part(a, n_(0), q2[0][:, :], y[:, :])
            act_hi(a, u.on(5))
            act_turned(a, i + 1)

        with a.Fori(0, 4) as h:
            a_head(h, 0, At(U_A, h, 4), At(N_A + 2, h, 2), False)
        with a.Fori(4, 7) as h:
            a_head(h, 1, At(U_A, h, 4), At(N_A + 2, h, 2), False)
        a_head(7, 1, At(U_KVB), At(N_KVB), True)
        act_hi(a, At(U_B + 2))
        a.wait_ge(vt_done, 22)
        pxv = px[:, :].rearrange("p (t d) -> p t d", t=NQ)
        a.activation(vbz[0][:, 0, :, 0:64], pxv[:, :, 0:64], ACT.Copy)
        a.activation(vbz[0][:, 1, :, 64:128], pxv[:, :, 64:128], ACT.Copy).then_inc(ev_act, 1)
        act_hi(a, At(U_B + 3))
        act_part(a, N_B, q2[0][:, :], y[:, :])
        act_hi(a, At(U_B + 4))
        act_hi(a, At(U_B + 5))

        def b_pair(p, u, n_, steps):
            if steps:
                act_hi(a, u.on(2))
            act_gate(a, n_(-1), y[:, :])
            a.wait_ge(nm_done, 33 + p)
            for hh in range(2):
                snk = cvec[:, bass.ds(p + (cv["sinks"][0] + 8 * hh), 1)]
                for t in range(NQ):
                    w = P if t == 0 else 2 * P
                    c0 = WROW[t] - (384 if t >= 2 else 0)
                    a.activation(prob[:, BANDED * hh + WROW[t]:BANDED * hh + WROW[t] + w],
                                 sb[2 * hh + t // 2][:, c0:c0 + w], ACT.Exp, bias=nms[:, 4 * hh + t:4 * hh + t + 1],
                                 scale=SC_B, accum_out=lsum[:, 4 * hh + t:4 * hh + t + 1])
                ins = a.activation(lsum[:, 8 + 4 * hh:12 + 4 * hh], nms[:, 4 * hh:4 * hh + 4], ACT.Exp, bias=snk)
            ins.then_inc(p_exp, 1)
            if steps:
                act_hi(a, u.on(3))
                act_part(a, n_(0), q2[0][:, :], y[:, :])
                act_hi(a, u.on(4))
            for hh in range(2):
                for b_ in range(2):
                    w = 512 if b_ == 0 else 384
                    if b_ == 0:
                        a.wait_ge(pt_done, 4 * 32 + 2 * p + hh + 1)
                    c0 = BANDED * hh + 512 * b_
                    ins = a.activation(pth[:, c0:c0 + w], sb[2 * hh + b_][:, 0:w], ACT.Copy)
                ins.then_inc(pt_hi, 1)
            if steps:
                act_hi(a, u.on(5))

        with a.Fori(0, NPAIR - 1) as p:
            b_pair(p, At(U_B + 4, p, 4), At(N_B + 2, p, 2), True)
        b_pair(NPAIR - 1, At(U_OUT2), At(N_OUT2), False)
        a.wait_ge(o_done, 32)
        for j in range(KT):
            a.activation(xh[:, j, :], o[:, j, :], ACT.Copy).then_inc(x_hi, 1)
        two_strips(At(U_OUT2), lambda j: out_square(N_OUT2 + j, o[:, j, :]))
        with a.Fori(0, KT // 2 - 2) as i:
            two_strips(At(U_OUT2 + 4, i, 4), lambda j: out_square(
                N_OUT2 + 2 + j + i * 2, o[:, bass.ds(2 * i + 2 + j, 1), :].rearrange("p a n -> p (a n)")))
        act_hi(a, At(U_END - 2))
        act_hi(a, At(U_END - 1))
        for j in range(2):
            out_square(N_OUT2 + 14 + j, o[:, 14 + j, :])
        act_rms(a, 5)

    def lo(v_, u, cols=1024):
        s = u.slot()
        v_.wait_ge(w_hi, u(1))
        v_.tensor_tensor(wl[s][:, :cols], raw[s][:, :cols], wh[s][:, :cols].bitcast(F32), ALU.subtract)\
          .then_inc(w_lo, 1)

    def take(v_, n_, bank_, used, times, dst):
        v_.drain()
        v_.wait_ge(w_used, used)
        v_.tensor_tensor(dst, pj[bank_][:, :], times[:, :], ALU.mult).then_inc(y_done, 1)

    def take_rope(v_, bank_, used, cos_, sin_, half_, dst, rows=P, bump=True):
        v_.drain()
        v_.wait_ge(w_used, used)
        for p0 in range(0, rows, 2 * half_):
            a_, b_ = slice(p0, p0 + half_), slice(p0 + half_, p0 + 2 * half_)
            v_.tensor_tensor(e_t[a_, :], pj[bank_][b_, :], sin_[a_, :], ALU.mult)
            v_.tensor_tensor(e_t[b_, :], pj[bank_][a_, :], sin_[b_, :], ALU.mult)
        v_.tensor_tensor(dst, pj[bank_][0:rows, :], cos_[0:rows, :], ALU.mult)
        v_.drain()
        v_.tensor_tensor(dst, dst, e_t[0:rows, :], ALU.add).then_inc(y_done, 1)

    def rest(v_, n_, dst, src, hi):
        v_.drain()
        v_.wait_ge(ev_act, n_ + 1)
        v_.tensor_tensor(dst, src, hi.bitcast(F32), ALU.subtract).then_inc(r_done, 1)

    def rest_y(v_, n_, pr):
        rest(v_, n_, pr[1][:, :], y[:, :], pr[0][:, :])

    def rest_v(v_, n_, pr):
        rest(v_, n_, pr[1][:, :, :], px[:, :].rearrange("p (t d) -> p t d", t=NQ), pr[0][:, :, :])

    def silu(v_, n_, dst):
        v_.drain()
        v_.wait_ge(ev_act, n_ + 1)
        v_.scalar_tensor_tensor(dst, e_t[:, :], 1.0, y[:, :], ALU.add, ALU.mult).then_inc(r_done, 1)

    def maxima(v_, i, scale):
        v_.drain()
        for t in range(NQ):
            v_.wait_ge(s_done, 4 * i + t + 1)
            v_.tensor_reduce(nm[:, t:t + 1], sb[t][:, 0:P * (t + 1)], AX.X, ALU.max, negate=True)
        v_.drain()
        v_.tensor_scalar(nms[:, 0:4], nm[:, 0:4], scale, None, ALU.mult).then_inc(nm_done, 1)

    def divide(v_, i, times=None):
        v_.drain()
        v_.wait_ge(p_exp, 4 * i + 4)
        v_.reciprocal(rinv[:, 0:4], lsum[:, 0:4])
        v_.drain()
        if times is not None:
            v_.tensor_tensor(rinv[:, 0:4], rinv[:, 0:4], times, ALU.mult)
            v_.drain()
        for t in range(NQ):
            cols = slice(ROW[t], ROW[t] + P * (t + 1))
            ins = v_.tensor_scalar(prob[:, cols], prob[:, cols], rinv[:, t:t + 1], None, ALU.mult)
        ins.then_inc(p_norm, 1)

    def turned(v_, i):
        for t in range(NQ):
            v_.wait_ge(pt_hi, 4 * i + t + 1)
            w = S - P * t
            cols = slice(COL[t], COL[t] + w)
            v_.tensor_tensor(ptl[:, cols], sb[t][:, 0:w], pth[:, cols].bitcast(F32), ALU.subtract)\
              .then_inc(pt_lo, 1)

    def head_out(v_, i, dst, by):
        v_.drain()
        v_.wait_ge(pv_done, i + 1)
        v_.scalar_tensor_tensor(dst, po[:, :], 0.5, by, ALU.mult, ALU.mult).then_inc(o_done, 1)

    def o_at(reg):
        if isinstance(reg, int):
            return o[:, reg, :]
        return o[:, bass.ds(reg, 1), :].rearrange("p a n -> p (a n)")

    def rms_ms(v_, i, width):
        v_.drain()
        if i in (0, 4):
            v_.wait_ge(sq_used, KT if i == 0 else 2 * KT)
        else:
            v_.wait_ge(sum_done, i if i < 4 else 4)
        v_.tensor_scalar(nrm[:, :], px[:, :], 1.0 / width, EPS, ALU.mult, ALU.add).then_inc(ms_done, 1)

    def rms_rb(v_, i, dst):
        v_.drain()
        v_.wait_ge(rs_done, i + 1)
        v_.tensor_tensor(e_t[:, :], nrt[:, :], nrt[:, :], ALU.mult)
        v_.drain()
        v_.tensor_tensor(e_t[:, :], e_t[:, :], nrm[:, :], ALU.mult)
        v_.drain()
        v_.tensor_scalar(e_t[:, :], e_t[:, :], -0.5, 1.5, ALU.mult, ALU.add)
        v_.drain()
        v_.tensor_tensor(dst[:, :], nrt[:, :], e_t[:, :], ALU.mult).then_inc(rb_done, 1)
        v_.drain()

    @block.vector
    def _(v_):
        v_.wait_ge(consts_in, 16 * 7)
        lo(v_, At(0))
        lo(v_, At(1))

        def x_rest(j, src, g_, count):
            v_.wait_ge(x_hi, count + j + 1)
            if g_ is None:
                v_.tensor_tensor(xl[:, j, :], src, xh[:, j, :].bitcast(F32), ALU.subtract).then_inc(x_lo, 1)
            else:
                v_.scalar_tensor_tensor(xl[:, j, :], src, g_, xh[:, j, :].bitcast(F32), ALU.mult, ALU.subtract)\
                  .then_inc(x_lo, 1)

        for j in range(KT):
            x_rest(j, o[:, j, :], c("g_pre", j), 0)
            if j in (4, 6):
                lo(v_, At(j // 2))
        v_.wait_ge(pos_in, 16)
        v_.tensor_copy(ang[0][:, :], posi[:, :])
        v_.drain()
        v_.tensor_scalar(ang[0][:, :], ang[0][:, :], c("invf"), None, ALU.mult)
        v_.drain()
        v_.tensor_scalar(ang[1][:, :], ang[0][:, :], 1.0 / (2 * math.pi), 12582912.0, ALU.mult, ALU.add)
        v_.drain()
        v_.tensor_scalar(ang[1][:, :], ang[1][:, :], -12582912.0, None, ALU.add)
        c1 = 6.28125
        c2 = float(np.float32(np.round((2 * math.pi - c1) * 2 ** 20) / 2 ** 20))
        c3 = 2 * math.pi - c1 - c2
        for part in (c1, c2, c3):
            v_.drain()
            v_.scalar_tensor_tensor(ang[0][:, :], ang[1][:, :], -part, ang[0][:, :], ALU.mult, ALU.add)
        v_.drain()
        pi = 3.1415925
        v_.tensor_scalar(ang[2][:, :], ang[0][:, :], math.pi / 2, None, ALU.add)
        v_.drain()
        v_.tensor_scalar(ang[1][:, :], ang[2][:, :], math.pi, -2 * math.pi, ALU.is_gt, ALU.mult)
        v_.tensor_scalar(ang[0][:, :], ang[0][:, :], pi, -pi, ALU.min, ALU.max)
        v_.drain()
        v_.tensor_tensor(ang[2][:, :], ang[2][:, :], ang[1][:, :], ALU.add)
        v_.drain()
        v_.tensor_scalar(ang[2][:, :], ang[2][:, :], pi, -pi, ALU.min, ALU.max).then_inc(tab, 1)
        v_.wait_ge(red, 1)
        v_.tensor_scalar(sin_t[:, :], sin_t[:, :], c("sgn64"), None, ALU.mult)
        rms_ms(v_, 0, D)
        rms_rb(v_, 0, rb)
        v_.tensor_tensor(gate[:, :], cos_t[:, :], rb[:, :], ALU.mult)
        v_.tensor_tensor(nrt[:, :], sin_t[:, :], rb[:, :], ALU.mult)
        v_.wait_ge(w_used, 3)
        v_.tensor_tensor(yv[:, :], pj[0][:, :], rb[:, :], ALU.mult).then_inc(lfs, 1)
        take_rope(v_, 0, 3, gate, nrt, 32, y[0:64, :], rows=64)
        v_.drain()
        v_.wait_ge(ev_act, 1)
        v_.tensor_tensor(kr[1][0:64, :], y[0:64, :], kr[0][0:64, :].bitcast(F32), ALU.subtract)
        v_.drain()
        v_.tensor_copy(kr[1][64:128, :], kr[1][0:64, :].bitcast(F32)).then_inc(r_done, 1)
        lo(v_, At(4))
        lo(v_, At(5))
        take(v_, N_FOX, 1, U_FOX + 2, rb, y[:, :])
        rest_y(v_, N_FOX, q)
        v_.wait_ge(lft, 1)
        z = [zf[:, i, :].rearrange("p (t h) -> p t h", t=NQ) for i in range(3)]
        v_.memset(lf[0][:, :, :].bitcast(F32), 0.0)
        v_.memset(lf[1][:, :, :].bitcast(F32), 0.0)
        v_.tensor_tensor(z[0], px[:, :].rearrange("p (t d) -> p t d", t=NQ)[:, :, 64:72],
                         c("bf", 0, 32).rearrange("p (t h) -> p t h", t=NQ), ALU.add)
        v_.drain()
        v_.scalar_tensor_tensor(zf[:, 1, :], zf[:, 0, :], -1.0, zf[:, 0, :], ALU.mult, ALU.max).then_inc(lfs, 1)
        v_.wait_ge(lat_act, 1)
        v_.scalar_tensor_tensor(zf[:, 2, :], zf[:, 0, :], 0.0, zf[:, 1, :], ALU.min, ALU.subtract)
        v_.drain()
        for col in (0, 32):
            v_.tensor_copy(lf[0][:, :, col:col + 8], z[2])
        v_.drain()
        for col in (0, 32):
            ins = v_.tensor_tensor(lf[1][:, :, col:col + 8], z[2], lf[0][:, :, col:col + 8].bitcast(F32), ALU.subtract)
        ins.then_inc(lfs, 1)
        lo(v_, At(6))
        lo(v_, At(7))
        take(v_, N_FOX + 1, 0, U_FOX + 4, rb, y[:, :])
        rest_y(v_, N_FOX + 1, k)
        v_.memset(cum[64:96, :].bitcast(F32), 1.0)
        v_.memset(cum[96:128, :].bitcast(F32), 0.0)
        v_.wait_ge(cumh, 1)
        v_.scalar_tensor_tensor(cum[32:64, :], px[32:64, :], 1.0 / SC_FOX, cum[32:64, :].bitcast(F32), ALU.mult,
                                ALU.subtract).then_inc(krd, 1)
        lo(v_, At(8))
        lo(v_, At(9))
        take(v_, N_FOX + 2, 1, U_FOX + 6, rb, yv[:, :])
        lo(v_, At(10))
        lo(v_, At(11))
        rest_v(v_, N_FOX + 2, v)

        def fox(h, u, n_, last):
            b = n_.base % 2
            lo(v_, u.on(2))
            take(v_, None, 1 - b, u(0), rb, y[:, :])
            maxima(v_, h, SC_FOX)
            lo(v_, u.on(3))
            divide(v_, h)
            silu(v_, n_(-1), gate[:, :])
            for s in range(2, 8):
                lo(v_, u.on(s + LEAD))
                if s in (2, 4, 6):
                    j = s // 2 - 1
                    take(v_, None, (b + j) % 2, u(s), rb, yv[:, :] if j == 2 and not last else y[:, :])
                if s == 2:
                    turned(v_, h)
                    if last:
                        silu(v_, n_(0), o[:, 0, :])
                    else:
                        rest_y(v_, n_(0), q)
                if s == 4:
                    if last:
                        silu(v_, n_(1), o[:, 1, :])
                    else:
                        rest_y(v_, n_(1), k)
                    head_out(v_, h, o_at(h + 8), gate[:, :])
                if s == 6 and last:
                    silu(v_, n_(2), o[:, 2, :])
                if s == 7:
                    if last:
                        take(v_, None, (b + 3) % 2, u(8), rb, y[:, :])
                        silu(v_, n_(3), o[:, 3, :])
                    else:
                        rest_v(v_, n_(2), v)

        with v_.Fori(0, NHEAD - 1) as h:
            fox(h, At(U_FOX + 8, h, 8), At(N_FOX + 4, h, 4), False)
        fox(NHEAD - 1, At(U_GATE), At(N_GATE), True)

        def two_strips(u, evac):
            lo(v_, u.on(2))
            lo(v_, u.on(3))
            evac(0, u(2))
            lo(v_, u.on(4))
            lo(v_, u.on(5))
            evac(1, u(4))

        with v_.Fori(0, 2) as i:
            def evac(j, used):
                take(v_, None, (N_GATE + j) % 2, used, rb, y[:, :])
                silu(v_, N_GATE + 4 + j + i * 2, o_at(4 + j + i * 2))
            two_strips(At(U_GATE + 8, i, 4), evac)
        v_.memset(acc[:, :], 0.0)
        v_.memset(sq[0][:, :], 0.0)
        for first, laps, into in ((0, 3, acc), (3, 2, sq[0])):
            with v_.Fori(first, first + laps) as i:
                def evac(j, used):
                    take(v_, None, (N_LAT + j) % 2, used, rb,
                         lat[:, bass.ds(i * 2 + j, 1), :].rearrange("p a n -> p (a n)"))
                    v_.drain()
                    v_.wait_ge(ev_act, N_LAT + j + 1 + i * 2)
                    v_.tensor_tensor(into[:, :], into[:, :], e_t[:, :], ALU.add).then_inc(r_done, 1)
                two_strips(At(U_LAT, i, 4), evac)
        v_.drain().then_inc(acc_ready, 1)
        for j in range(QR_T + KV_T):
            x_rest(j, lat[:, j, :], c("g_q", j) if j < QR_T else c("g_kv", j - QR_T), KT)
            if j == 1:
                rms_ms(v_, 1, QR_T * P)
                v_.tensor_copy(acc[:, :], sq[0][:, :]).then_inc(acc_ready, 1)
        rms_rb(v_, 1, rq)
        rms_ms(v_, 2, KV_T * P)
        rms_rb(v_, 2, rkv)
        v_.tensor_tensor(cosq[:, :], cos_t[:, :], rq[:, :], ALU.mult)
        v_.tensor_tensor(sinq[:, :], sin_t[:, :], rq[:, :], ALU.mult)

        def mla_lo(u, s):
            m = (s + LEAD) % 8
            lo(v_, u.on(s + LEAD), 1024 if m < 2 else 128 * MLA_TILES[m])

        def mla_take(k_, used):
            if k_ == 3:
                take_rope(v_, 1, used, cosq, sinq, 32, y[:, :])
            else:
                take(v_, None, k_ % 2, used, rq if k_ in (0, 4) else rkv, yv[:, :] if k_ in (2, 6) else y[:, :])

        dst = {0: qa, 1: ka, 3: qr, 4: qb, 5: kb}
        n0, u0 = At(N_MLA), At(U_MLA)
        for s, strip in enumerate([None, 0, 1, 2, None, 3, 4, 5]):
            mla_lo(u0, s)
            if strip is not None:
                mla_take(strip, u0(s))
            if s == 5:
                rest_v(v_, n0(2), va)
            if strip is not None and strip != 2:
                rest_y(v_, n0(strip), dst[strip])

        def mla(p, u, n_, steps):
            i = A_MLA + 2 * p
            if steps:
                mla_lo(u, 0)
            mla_take(6, u(0))
            maxima(v_, i, SC_MLA)
            if steps:
                mla_lo(u, 1)
            rest_v(v_, n_(-1), vb)
            divide(v_, i)
            if steps:
                mla_take(0, u(1))
                rest_y(v_, n_(0), qa)
                mla_lo(u, 2)
                mla_take(1, u(2))
                rest_y(v_, n_(1), ka)
            turned(v_, i)
            if steps:
                mla_lo(u, 3)
                mla_take(2, u(3))
                mla_lo(u, 4)
            head_out(v_, i, o_at(p * 2), o_at(p * 2))
            maxima(v_, i + 1, SC_MLA)
            if steps:
                mla_lo(u, 5)
            divide(v_, i + 1)
            if steps:
                mla_take(3, u(5))
                rest_v(v_, n_(2), va)
                rest_y(v_, n_(3), qr)
                mla_lo(u, 6)
                mla_take(4, u(6))
                rest_y(v_, n_(4), qb)
            turned(v_, i + 1)
            if steps:
                mla_lo(u, 7)
                mla_take(5, u(7))
                rest_y(v_, n_(5), kb)
            head_out(v_, i + 1, o_at(p * 2 + 1), o_at(p * 2 + 1))

        with v_.Fori(0, 3) as p:
            mla(p, At(U_MLA + 8, p, 8), At(N_MLA + 7, p, 7), True)
        mla(3, At(U_OUT1), At(N_OUT1), False)
        for j in range(KT):
            x_rest(j, o[:, j, :], None, 2 * KT - 6)
        v_.memset(acc[:, :], 0.0)

        def add_square(n_):
            v_.drain()
            v_.wait_ge(ev_act, n_)
            v_.tensor_tensor(acc[:, :], acc[:, :], e_t[:, :], ALU.add).then_inc(r_done, 1)

        def out1(first, i):
            def evac(j, used):
                v_.drain()
                v_.wait_ge(w_used, used)
                v_.tensor_copy(o_at(first + j + i * 2), pj[(N_OUT1 + j) % 2][:, :]).then_inc(y_done, 1)
                add_square(N_OUT1 + 1 + first + j + i * 2)
            return evac

        two_strips(At(U_OUT1), out1(0, 0))
        with v_.Fori(0, KT // 2 - 1) as i:
            two_strips(At(U_OUT1 + 4, i, 4), out1(2, i))
        v_.drain().then_inc(acc_ready, 1)
        lo(v_, At(U_CMPIN + 2))
        lo(v_, At(U_CMPIN + 3))
        rms_ms(v_, 3, D)
        rms_rb(v_, 3, rb)

        def scale_tile(j):
            v_.scalar_tensor_tensor(o[:, j, :], o[:, j, :], c("g_post", j), rb[:, :], ALU.mult, ALU.mult)\
              .then_inc(scaled, 1)

        for j in range(3):
            scale_tile(j)
        for j in range(KT):
            if j + 3 < KT:
                scale_tile(j + 3)
            x_rest(j, o[:, j, :], c("g_2", j), 3 * KT - 6)
        lo(v_, At(U_CMPIN + 4))
        lo(v_, At(U_CMPIN + 5))
        rms_ms(v_, 4, D)
        rms_rb(v_, 4, rb)
        v_.wait_ge(tab2_in, 32)
        v_.tensor_tensor(cos2[:, :], cos2[:, :], rb[:, :], ALU.mult)
        v_.tensor_tensor(sin2[:, :], sin2[:, :], rb[:, :], ALU.mult)

        def take_cmp(j, used):
            b = (N_CMPIN + j) % 2
            if j < 2:
                take_rope(v_, b, used, cos2, sin2, 64, cmp_in[0][:, j, :])
            else:
                take(v_, None, b, used, rb, cmp_in[1][:, j - 2, :])
            v_.drain().then_inc(r_done, 1)

        take_cmp(0, U_CMPIN + 3)
        take_cmp(1, U_CMPIN + 4)
        lo(v_, At(U_CMPIN + 6))
        lo(v_, At(U_CMPIN + 7))
        take_cmp(2, U_CMPIN + 6)
        lo(v_, At(U_CMPIN + 8))
        lo(v_, At(U_CMPIN + 9))
        take_cmp(3, U_CMPIN + 8)
        v_.wait_ge(xn_out, 16 * 4)
        v_.memset(blk[:, :, :], 0.0)

        def blocks(i):
            pos = c("pos_v" if i // 2 else "pos_k", 0, 32)
            jh = i % 2
            v_.drain()
            for g_ in range(2):
                src = cmp_in[i // 2][:, g_, :].rearrange("p (c j) -> p c j", j=16)
                ins = v_.tensor_tensor(blk[:, :, 32 * g_:32 * g_ + NCMP],
                                       src[:, jh:jh + NCMP, :].rearrange("p c j -> p j c"),
                                       pos[:, 16 * jh:16 * jh + 16].unsqueeze(2).to_broadcast([P, 16, NCMP]), ALU.add)
            ins.then_inc(blk_made, 1)

        def blocks_lo(i):
            v_.drain()
            v_.wait_ge(blk_hi, i + 1)
            half_ = slice(16 * (i % 2), 16 * (i % 2) + 16)
            v_.tensor_tensor(blkp[i // 2][1][:, half_, :], blk[:, :, :], blkp[i // 2][0][:, half_, :].bitcast(F32),
                             ALU.subtract).then_inc(blk_lo, 1)

        for g_ in range(2):
            def evac(j, used):
                blocks(2 * g_ + j)
                take_rope(v_, (N_KV + j) % 2, used, cos2, sin2, 64, y[:, :])
                blocks_lo(2 * g_ + j)
                rest_y(v_, N_KV + 2 * g_ + j - 4, kvg[g_][("ks", "kw")[j]])
            two_strips(At(U_KV + 4 * g_), evac)

        for g_ in range(2):
            def evac(j, used):
                take(v_, None, (N_KV + j) % 2, used, rb, yv[:, :])
                rest_v(v_, N_KV + 4 + 2 * g_ + j - 4, kvg[g_][("vs", "vw")[j]])
            two_strips(At(U_KV + 8 + 4 * g_), evac)
        lo(v_, At(U_GA + 2))
        lo(v_, At(U_GA + 3))
        take(v_, None, N_GA % 2, U_GA + 2, rb, yv[:, :])
        v_.wait_ge(ev_act, N_GA + 1 - 4)
        v_.tensor_scalar(gat[:, :, :], gat[:, :, :], 1.0, 0.5, ALU.add, ALU.mult).then_inc(r_done, 1)
        def hidden_lo(which):
            v_.drain()
            v_.wait_ge(hact, 2 * which + 2)
            v_.scalar_tensor_tensor(hidp[1][:, which, :, :], sb[2 + which][:, 0:P].rearrange("p (m c) -> p m c", m=2),
                                    0.5, hidp[0][:, which, :, :].bitcast(F32), ALU.mult, ALU.subtract).then_inc(hdve, 1)

        for which in range(2):
            for i in range(8):
                lo(v_, At(U_W1 + 8 * which + i + LEAD))
                if which and i == 2:
                    hidden_lo(0)
            v_.drain()
            v_.wait_ge(hact, 2 * which + 1)
            v_.scalar_tensor_tensor(hid[:, :], hide[:, :], 1.0, sb[which][0:64, 0:256], ALU.add, ALU.mult).then_inc(gad, 1)
        lo(v_, At(U_W2), 512)
        hidden_lo(1)
        lo(v_, At(U_W2 + 1))
        take_rope(v_, N_A % 2, U_Q0 + 2, cos2, sin2, 64, y[:, :])
        rest_y(v_, N_A - 4, q2)
        v_.wait_ge(hact, 5)
        v_.tensor_tensor(kcp[1][:, :], px[:, 0:64], kcp[0][:, :].bitcast(F32), ALU.subtract)
        v_.tensor_copy(vct[:, :], px[:, 64:128]).then_inc(hdve, 1)
        lo(v_, At(U_W2 + 2))
        v_.wait_ge(hact, 6)
        v_.tensor_tensor(vcp[1][:, :, :], px[0:32, 0:256].rearrange("p (g d) -> p g d", g=2),
                         vcp[0][:, :, :].bitcast(F32), ALU.subtract).then_inc(hdve, 1)
        lo(v_, At(U_A))
        lo(v_, At(U_A + 1))

        def a_head(h, g_, u, n_, last):
            i = A_A + 2 * h
            b = n_.base % 2

            def gate_of(branch):
                return gat[:, :, bass.ds(h * 3 + branch, 1)].rearrange("p t a -> p (t a)")

            lo(v_, u.on(2))
            take(v_, None, 1 - b, u(0), rb, y[:, :])
            maxima(v_, i, SC_A)
            v_.wait_ge(sc_done, h + 1)
            v_.tensor_reduce(nm[:, 4:8], px[:, 0:128].rearrange("p (t c) -> p t c", t=NQ), AX.X, ALU.max, negate=True)
            v_.drain()
            v_.tensor_scalar(nms[:, 4:8], nm[:, 4:8], SC_A, 1e20, ALU.mult, ALU.min).then_inc(pc_exp, 1)
            divide(v_, i, gate_of(1))
            v_.wait_ge(hact, h + 7)
            v_.tensor_scalar(rinv[:, 4:8], lsum[:, 4:8], 1e-30, None, ALU.max)
            v_.drain()
            v_.reciprocal(rinv[:, 4:8], rinv[:, 4:8])
            v_.drain()
            v_.tensor_tensor(rinv[:, 4:8], rinv[:, 4:8], gate_of(0), ALU.mult)
            v_.drain()
            v_.tensor_tensor(rinv[:, 4:8], rinv[:, 4:8], c("rowok", 0, 4), ALU.mult)
            v_.drain()
            v_.tensor_tensor(pc[:, :, :], pc[:, :, :], rinv[:, 4:8].unsqueeze(2).to_broadcast([P, NQ, 32]), ALU.mult)\
              .then_inc(pc_norm, 1)
            lo(v_, u.on(3))
            turned(v_, i)
            v_.wait_ge(ptc_hi, h + 1)
            v_.tensor_tensor(ptc[1][:, :], px[0:32, :], ptc[0][:, :].bitcast(F32), ALU.subtract).then_inc(ptc_lo, 1)
            silu(v_, n_(-1) - 4, gate[:, :])
            lo(v_, u.on(4))
            maxima(v_, i + 1, SC_A)
            if last:
                v_.wait_ge(tab2_in, 64)
                v_.tensor_tensor(cos2[:, :], cos2[:, :], rb[:, :], ALU.mult)
                v_.tensor_tensor(sin2[:, :], sin2[:, :], rb[:, :], ALU.mult)
            divide(v_, i + 1, gate_of(2))
            take_rope(v_, b, u(2), cos2, sin2, 32 if last else 64, y[:, :])
            rest_y(v_, n_(0) - 4, kbb if last else q2)
            lo(v_, u.on(5))
            turned(v_, i + 1)
            if last:
                v_.memset(vbz[0][:, :, :, :].bitcast(F32), 0.0)
                v_.memset(vbz[1][:, :, :, :].bitcast(F32), 0.0)
                take(v_, None, 1 - b, u(4), rb, yv[:, :])
            head_out(v_, h + 16, o_at(h), gate[:, :])

        with v_.Fori(0, 4) as h:
            a_head(h, 0, At(U_A, h, 4), At(N_A + 2, h, 2), False)
        with v_.Fori(4, 7) as h:
            a_head(h, 1, At(U_A, h, 4), At(N_A + 2, h, 2), False)
        a_head(7, 1, At(U_KVB), At(N_KVB), True)
        lo(v_, At(U_B + 2))
        v_.wait_ge(ev_act, N_KVB + 2 - 4)
        pxv = px[:, :].rearrange("p (t d) -> p t d", t=NQ)
        v_.tensor_tensor(vbz[1][:, 0, :, 0:64], pxv[:, :, 0:64], vbz[0][:, 0, :, 0:64].bitcast(F32), ALU.subtract)
        v_.tensor_tensor(vbz[1][:, 1, :, 64:128], pxv[:, :, 64:128], vbz[0][:, 1, :, 64:128].bitcast(F32),
                         ALU.subtract).then_inc(r_done, 1)
        lo(v_, At(U_B + 3))
        take_rope(v_, N_B % 2, U_B + 2, cos2, sin2, 32, y[:, :])
        rest_y(v_, N_B - 4, q2)
        v_.tensor_scalar(nsink[:, :], c("sinks", 0, 16), -1.0, None, ALU.mult)
        lo(v_, At(U_B + 4))
        lo(v_, At(U_B + 5))

        def b_pair(p, u, n_, steps):
            b = n_.base % 2
            if steps:
                lo(v_, u.on(2))
            take(v_, None, 1 - b, u(0), rb, y[:, :])
            for hh in range(2):
                for t in range(NQ):
                    if t % 2 == 0:
                        v_.wait_ge(s_done, 4 * 32 + 8 * p + 4 * hh + t + 2)
                    w = P if t == 0 else 2 * P
                    c0 = WROW[t] - (384 if t >= 2 else 0)
                    v_.tensor_reduce(nm[:, 4 * hh + t:4 * hh + t + 1], sb[2 * hh + t // 2][:, c0:c0 + w], AX.X, ALU.max,
                                     negate=True)
            v_.drain()
            for hh in range(2):
                ins = v_.tensor_scalar(nms[:, 4 * hh:4 * hh + 4], nm[:, 4 * hh:4 * hh + 4], SC_B,
                                       nsink[:, bass.ds(p + 8 * hh, 1)], ALU.mult, ALU.min)
            ins.then_inc(nm_done, 1)
            v_.wait_ge(p_exp, 4 * 32 + 1 + p)
            v_.tensor_tensor(rinv[:, 0:8], lsum[:, 0:8], lsum[:, 8:16], ALU.add)
            v_.drain()
            v_.reciprocal(rinv[:, 0:8], rinv[:, 0:8])
            v_.drain()
            for hh in range(2):
                for t in range(NQ):
                    w = P if t == 0 else 2 * P
                    cols = slice(BANDED * hh + WROW[t], BANDED * hh + WROW[t] + w)
                    ins = v_.tensor_scalar(prob[:, cols], prob[:, cols], rinv[:, 4 * hh + t:4 * hh + t + 1], None, ALU.mult)
            ins.then_inc(p_norm, 1)
            if steps:
                lo(v_, u.on(3))
            silu(v_, n_(-1) - 4, gate[:, :])
            if steps:
                take_rope(v_, b, u(2), cos2, sin2, 32, y[:, :])
                rest_y(v_, n_(0) - 4, q2)
                lo(v_, u.on(4))
            for hh in range(2):
                v_.wait_ge(pt_hi, 4 * 32 + 2 * p + hh + 1)
                for b_ in range(2):
                    w = 512 if b_ == 0 else 384
                    c0 = BANDED * hh + 512 * b_
                    ins = v_.tensor_tensor(ptl[:, c0:c0 + w], sb[2 * hh + b_][:, 0:w], pth[:, c0:c0 + w].bitcast(F32),
                                           ALU.subtract)
                ins.then_inc(pt_lo, 1)
            if steps:
                lo(v_, u.on(5))
            head_out(v_, p + 24, o_at(p + 8), gate[:, :])

        with v_.Fori(0, NPAIR - 1) as p:
            b_pair(p, At(U_B + 4, p, 4), At(N_B + 2, p, 2), True)
        b_pair(NPAIR - 1, At(U_OUT2), At(N_OUT2), False)
        for j in range(KT):
            x_rest(j, o[:, j, :], None, 4 * KT - 6)
        v_.memset(acc[:, :], 0.0)

        def out2(first, i):
            def evac(j, used):
                v_.drain()
                v_.wait_ge(xn_in if j == 0 else xn_in2, 16 * (first // 2 + 1) + i * 16)
                v_.wait_ge(w_used, used)
                v_.tensor_tensor(o_at(first + j + i * 2), pj[(N_OUT2 + j) % 2][:, :], xr2[j][:, :], ALU.add)\
                  .then_inc(y_done, 1)
                add_square(N_OUT2 + 1 - 4 + first + j + i * 2)
            return evac

        two_strips(At(U_OUT2), out2(0, 0))
        with v_.Fori(0, KT // 2 - 2) as i:
            two_strips(At(U_OUT2 + 4, i, 4), out2(2, i))
        lo(v_, At(U_END - 2))
        lo(v_, At(U_END - 1))
        out2(14, 0)(0, U_END - 2)
        out2(14, 0)(1, U_END)
        v_.drain().then_inc(acc_ready, 1)
        rms_ms(v_, 5, D)
        rms_rb(v_, 5, rb)
        for j in range(KT):
            v_.scalar_tensor_tensor(o[:, j, :], o[:, j, :], c("g_fin", j), rb[:, :], ALU.mult, ALU.mult)\
              .then_inc(fin, 1)


def kernel(**inputs):
    import concourse.bacc as bacc
    from concourse.bass_utils import run_bass_kernel_spmd

    a = {k_: np.asarray(v_) for k_, v_ in inputs.items()}
    f = np.float32

    def cols(g):
        return np.ascontiguousarray(g.reshape(-1, P).T)

    units = []

    def put(tiles):
        u = np.zeros((P, 1024), f)
        for i, tile in enumerate(tiles):
            u[:, P * i:P * i + tile.shape[1]] = tile
        units.append(u)

    def strip(w, order, per=8):
        kt = w.shape[0] // P
        for k0 in range(0, kt, per):
            put([w[P * i:P * i + P][:, order] for i in range(k0, min(k0 + per, kt))])

    r = np.arange
    w1, w2 = a["w_in"][0], a["w_in_2"][0]
    off = np.cumsum([0, 768, 512, 64, 1024, 1024, 1024, 1024, 8, 1024])
    misc = np.concatenate([w1[:, off[2]:off[3]], w1[:, off[7]:off[8]]], 1)
    strip(misc, r(misc.shape[1]))
    for h in range(NHEAD):
        for part in (4, 5, 6, 8):
            strip(w1, off[part] + P * h + r(P))
    units[1], units[2] = units[2], units[1]
    for h in range(NHEAD):
        strip(w1, off[3] + P * h + r(P))
    for i in range(QR_T):
        strip(w1, off[0] + P * i + r(P))
    for i in range(KV_T):
        strip(w1, off[1] + P * i + r(P))
    uq, ukv = a["w_uq"][0], a["w_ukv"][0]
    for p in range(4):
        ha, hb = 2 * p, 2 * p + 1
        strip(uq, 192 * ha + r(P))
        strip(ukv, 256 * ha + r(P))
        strip(ukv, 256 * ha + P + r(P))
        strip(uq, np.concatenate([192 * ha + P + r(64), 192 * hb + P + r(64)]), per=3)
        strip(uq, 192 * hb + r(P))
        strip(ukv, 256 * hb + r(P))
        strip(ukv, 256 * hb + P + r(P))
    for j in range(KT):
        strip(a["w_out"][0], P * j + r(P))
    off = np.cumsum([0, 1024, 256, 256, 256, 256, 256, 256, 1024, 24, 1024, 128, 128, 1024])
    for part in (1, 2):
        for g in range(2):
            strip(w2, off[part] + P * g + r(P))
    units[U_CMPIN + 1], units[U_CMPIN + 2] = units[U_CMPIN + 2], units[U_CMPIN + 1]
    for parts in ((3, 5), (4, 6)):
        for g in range(2):
            for part in parts:
                strip(w2, off[part] + P * g + r(P))
    strip(w2, off[8] + r(24))
    for name in ("cmp_k_w1_2", "cmp_v_w1_2"):
        w = a[name][0]
        for i in range(8):
            put([w[P * (4 * i + t // 2):P * (4 * i + t // 2) + P, P * (t % 2):P * (t % 2) + P] for t in range(8)])
    strip(w2, off[0] + r(P))
    put([a[name][0][P * m:P * m + P] for name in ("cmp_k_w2_2", "cmp_v_w2_2") for m in range(2)])
    strip(w2, off[7] + r(P))
    for h in range(1, NHEAD):
        strip(w2, off[0] + P * h + r(P))
        strip(w2, off[7] + P * h + r(P))
    strip(w2, off[10] + r(P))
    strip(w2, off[11] + r(P))
    both = [np.concatenate([64 * p + r(64), 64 * (p + 8) + r(64)]) for p in range(NPAIR)]
    for p in range(NPAIR):
        strip(w2, off[9] + both[p])
        strip(w2, off[12] + both[p])
    wo2 = np.concatenate([a["w_out_2"][0][:1024]] + [a["w_out_2"][0][1024 + b] for b in both], 0)
    for j in range(KT):
        strip(wo2, P * j + r(P))
    assert len(units) == U_END

    inv64 = (np.float32(10000.0) ** (-r(0, 64, 2).astype(f) / np.float32(64))).astype(f)
    inv128 = (np.float32(10000.0) ** (-r(0, 128, 2).astype(f) / np.float32(128))).astype(f)
    part = r(P)
    sgn64 = np.where(part % 64 < 32, -1, 1).astype(f)
    sgn128 = np.where(part < 64, -1, 1).astype(f)
    tok = r(S).astype(f)
    ang_a = (tok[None, :] * inv128[part % 64][:, None]).astype(f)
    ang_b = (tok[None, :] * inv64[part % 32][:, None]).astype(f)
    rowok = ((P * r(NQ)[None, :] + part[:, None]) >= JB - 1).astype(f)
    bf = np.broadcast_to(np.tile(a["b_forget"][0], NQ), (P, 4 * NHEAD))
    cvec = np.concatenate([
        cols(a["g_pre"][0]), cols(a["g_q_latent"][0]), cols(a["g_kv_latent"][0]), cols(a["g_post"][0]),
        cols(a["norm_g_2"][0]), cols(a["final_g_2"]), bf, np.broadcast_to(a["sinks_2"][0], (P, 16)),
        inv64[part % 32][:, None], sgn64[:, None], rowok, a["cmp_k_pos_2"][0].T, a["cmp_v_pos_2"][0].T], 1).astype(f)
    import ml_dtypes
    bf16 = ml_dtypes.bfloat16
    i_, j_ = part[:, None], part[None, :]
    c_ = r(32)
    cmask = np.zeros((P, NQ, 32), f)
    for t in range(NQ):
        cmask[:, t, :] = np.where((c_[None, :] < NCMP) & (16 * c_[None, :] + JB - 1 <= P * t + part[:, None]), 0, NEG)
    sel = np.zeros((P, NHEAD, 256), f)
    for h in range(NHEAD):
        sel[h, h, 0], sel[32 + h, h, 32], sel[64, h, 64], sel[64, h, 96] = -1, -1, 1, 1
        sel[64, h, P], sel[64, h, P + 32], sel[h, h, P + 64], sel[32 + h, h, P + 96] = 1, 1, 1, 1
    tri = np.concatenate([(i_ <= j_).astype(f), np.ones((P, S - P), f)], 1)
    arrays = {
        "w": np.stack(units), "xt": np.ascontiguousarray(a["x"][0].T.reshape(KT, P, S).transpose(1, 0, 2)),
        "pos": np.ascontiguousarray(np.broadcast_to(a["positions"][0], (P, S))).astype(np.int32),
        "cvec": np.ascontiguousarray(cvec), "ident": np.eye(P, dtype=f), "ones": np.ones((P, P), f),
        "identb": np.eye(P).astype(bf16), "maskd": np.where(j_ <= i_, 0, NEG).astype(bf16),
        "maskw": np.where(j_ > i_, 0, NEG).astype(bf16), "maskc": cmask.reshape(P, P).astype(bf16),
        "sel": sel, "tri": tri,
        "cos_a": np.cos(ang_a).astype(f), "sin_a": (np.sin(ang_a) * sgn128[:, None]).astype(f),
        "cos_b": np.cos(ang_b).astype(f), "sin_b": (np.sin(ang_b) * sgn64[:, None]).astype(f),
    }
    nc = bacc.Bacc("TRN2", target_bir_lowering=False, num_devices=1)
    d = {k_: nc.dram_tensor(f"in_{k_}", v_.shape, mybir.dt.from_np(v_.dtype), kind="ExternalInput").ap()
         for k_, v_ in arrays.items()}
    d["xn"] = nc.dram_tensor("xn", (P, KT, S), F32, kind="Internal").ap()
    d["out"] = nc.dram_tensor("out", (P, KT, S), F32, kind="ExternalOutput").ap()
    build(nc, d)
    res = run_bass_kernel_spmd(nc, [{f"in_{k_}": v_ for k_, v_ in arrays.items()}], core_ids=[0])
    out = res.results[0]["out"]
    return np.ascontiguousarray(out.transpose(1, 0, 2).reshape(D, S).T)[None]
```

```python
import math
from contextlib import ExitStack

import concourse.bass as bass
from concourse import mybir
import numpy as np

F32 = mybir.dt.float32
F32R = mybir.dt.float32r
BF16 = mybir.dt.bfloat16
I32 = mybir.dt.int32
ALU = mybir.AluOpType
ACT = mybir.ActivationFunctionType
AX = mybir.AxisListType

S = 512
P = 128
NQ = S // P
D = 2048
KT = D // P
QR_T, KV_T = 6, 4
NHEAD = 8
NPAIR = 8
NCMP, JB = 31, 32
EPS = 1e-6
NEG = -1e30
SLOTS = 4
LEAD = 2

U_MISC = 0
U_FOX = 2
U_GATE = U_FOX + 8 * NHEAD
U_LAT = U_GATE + 16
U_MLA = U_LAT + 20
U_OUT1 = U_MLA + 32
U_CMPIN = U_OUT1 + 32
U_KV = U_CMPIN + 8
U_GA = U_KV + 16
U_W1 = U_GA + 2
U_Q0 = U_W1 + 16
U_W2 = U_Q0 + 2
U_A = U_W2 + 3
U_KVB = U_A + 4 * (NHEAD - 1)
U_B = U_KVB + 4
U_OUT2 = U_B + 4 * NPAIR
U_END = U_OUT2 + 32

N_MISC = 0
N_FOX = 1
N_GATE = N_FOX + 4 * NHEAD
N_LAT = N_GATE + 8
N_MLA = N_LAT + 10
N_OUT1 = N_MLA + 28
N_CMPIN = N_OUT1 + 16
N_KV = N_CMPIN + 4
N_GA = N_KV + 8
N_A = N_GA + 1
N_KVB = N_A + 16
N_B = N_KVB + 2
N_OUT2 = N_B + 16

A_FOX, A_MLA, A_A = 0, 8, 16
ROW = [0, 128, 384, 768]
COL = [0, 512, 896, 1152]
CAUSAL = 1280
WROW = [0, 128, 384, 640]
WCOL = [0, 256, 512, 768]
BANDED = 896

EARLY = [0, 1, 2, 3, 4, 5, 8, 9, 6, 12, 13, 14, 15, 10, 11, 7]
NATURAL = list(range(KT))
X_PARTS = [0, 2, 4, 8, 12, KT]
POOL_TILES = 6

MLA_TILES = [6, 4, 4, 3, 3, 6, 4, 4]
FIRST_BANK = {2: 0, 3: 1, 4: 2}
SC_FOX, SC_MLA, SC_A, SC_B = 128 ** -0.5, 192 ** -0.5, 128 ** -0.5, 64 ** -0.5


class At:

    def __init__(self, base, lap=0, per=0):
        self.base, self.lap, self.per = base, lap, per

    def __call__(self, more=0):
        return self.base + more + self.lap * self.per if self.per else self.base + more

    def on(self, more):
        return At(self.base + more, self.lap, self.per)

    def slot(self):
        assert self.per % SLOTS == 0
        return self.base % SLOTS

    def round(self):
        r = self.base // SLOTS
        return r + self.lap * (self.per // SLOTS) if self.per else r


def build(nc, t):
    ctx = ExitStack()
    with ctx:
        _build(nc, t, ctx)


def _build(nc, d, ctx):
    base = -(-nc.sbuf_base // 32) * 32
    arena = nc.sbuf_usable_end - base
    at = {"next": base}

    def place(name, shape, dtype=F32, offset=None):
        size = int(np.prod(shape[1:])) * (2 if dtype == BF16 else 4)
        if offset is None:
            offset = at["next"]
            at["next"] = offset + -(-size // 32) * 32
        at[name] = offset
        assert offset + size <= base + arena, (name, offset + size - base - arena)
        return nc.alloc_sbuf_tensor_at(name, shape, dtype, offset=offset)

    raw = [place(f"raw{s}", [P, 1024]) for s in range(SLOTS)]
    wh = [place(f"wh{s}", [P, 1024], F32R) for s in range(SLOTS)]
    wl = [place(f"wl{s}", [P, 1024], F32R) for s in range(SLOTS)]
    xh = place("xh", [P, KT, S], F32R)
    xl = place("xl", [P, KT, S], F32R)
    o = place("o", [P, KT, S])
    rb = place("rb", [P, S])
    y = place("y", [P, S])
    yv = place("yv", [P, S])
    e_t = place("e_t", [P, S])
    gate = place("gate", [P, S])
    prob = place("prob", [P, 2 * BANDED])
    pth = place("pth", [P, 2 * BANDED], F32R)
    ptl = place("ptl", [P, 2 * BANDED], F32R)
    ident = place("ident", [P, P])
    ones = place("ones", [P, P])
    identb = place("identb", [P, P], BF16)
    maskd = place("maskd", [P, P], BF16)
    maskw = place("maskw", [P, P], BF16)
    maskc = place("maskc", [P, P], BF16)
    cvec = place("cvec", [P, 256])
    nm = place("nm", [P, 16])
    nms = place("nms", [P, 16])
    lsum = place("lsum", [P, 16])
    rinv = place("rinv", [P, 16])
    nsink = place("nsink", [P, 16])
    stage = at["next"]
    acc = place("acc", [P, S], offset=at["prob"])
    sq = [place("sq0", [P, S], offset=at["prob"] + 2048), place("sq1", [P, S], offset=at["prob"] + 4096)]
    nrm = place("nrm", [P, S], offset=at["ptl"])
    nrt = place("nrt", [P, S], offset=at["ptl"] + 2048)

    def pair(name, shape, offset=None):
        size = 4 * int(np.prod(shape[1:]))
        if offset is None:
            offset = at["next"]
            at["next"] = offset + 2 * size
        return (place(name + "_h", shape, F32R, offset), place(name + "_l", shape, F32R, offset + size))

    cos_t = place("cos_t", [P, S])
    sin_t = place("sin_t", [P, S])
    kr = pair("kr", [P, S])
    after_kr = at["next"]
    q = pair("q", [P, S])
    k = pair("k", [P, S])
    v = pair("v", [P, NQ, P])
    augq = place("augq", [P, S], F32R)
    augk = place("augk", [P, S], F32R)
    selr = place("selr", [P, 256], F32R)
    sel = place("sel", [P, NHEAD, 256], offset=at["o"])
    trif = place("trif", [P, S], offset=at["o"] + 8192)
    tri = place("tri", [P, S], F32R, offset=at["o"] + 10240)
    cum = place("cum", [P, S], F32R, offset=at["o"] + 12288)
    lf = pair("lf", [P, NQ, P], offset=at["pth"])
    zf = place("zf", [P, 3, 32], offset=at["prob"])
    ang = [e_t, y, gate]
    posi = place("posi", [P, S], I32, offset=at["yv"])
    lat = place("lat", [P, QR_T + KV_T, S], offset=after_kr)
    at["next"] = after_kr
    qa = pair("qa", [P, S])
    ka = pair("ka", [P, S])
    va = pair("va", [P, NQ, P])
    qr = pair("qr", [P, S])
    cosq, sinq = place("cosq", [P, S]), place("sinq", [P, S])
    rkv = place("rkv", [P, S], offset=at["xh"] + 10 * 2048)
    rq = place("rq", [P, S], offset=at["xh"] + 11 * 2048)
    qb = pair("qb", [P, S], offset=at["xh"] + 12 * 2048)
    kb = pair("kb", [P, S], offset=at["xh"] + 14 * 2048)
    vb = pair("vb", [P, NQ, P], offset=at["xl"] + 10 * 2048)
    x_again = [place("xa", [P, 14, S], offset=stage), place("xb", [P, 2, S], offset=at["y"])]
    again = [(x_again[0], j) for j in range(14)] + [(x_again[1], j) for j in range(2)]
    at["next"] = stage
    cos2 = place("cos2", [P, S])
    sin2 = place("sin2", [P, S])
    kcp = pair("kcp", [P, 64])
    vcp = pair("vcp", [32, 2, P])
    gat = place("gat", [P, NQ, 24])
    kv0 = at["next"]

    def group_kv(g, where):
        return {n: pair(f"{n}{g}", [P, S] if n[0] == "k" else [P, NQ, P], where + 4096 * i)
                for i, n in enumerate(("ks", "kw", "vs", "vw"))}

    kvg = [group_kv(0, kv0), group_kv(1, at["o"] + 8 * 2048)]
    q2 = pair("q2", [P, S], offset=kv0 + 16384)
    pc = place("pc", [P, NQ, 32], offset=kv0 + 20480)
    ptc = (place("ptc_h", [32, S], F32R, kv0 + 20992), place("ptc_l", [32, S], F32R, at["yv"]))
    cmp_in = [place("cmp_k", [P, 2, S], offset=at["gate"] + 12288), place("cmp_v", [P, 2, S], offset=at["gate"] + 8192)]
    blk = place("blk", [P, JB // 2, 64], offset=kv0 + 16384)
    blkp = [(place("blk_kh", [P, JB, 64], F32R, at["o"]), place("blk_kl", [P, JB, 64], F32R, at["gate"])),
            (place("blk_vh", [P, JB, 64], F32R, at["o"] + 8192), place("blk_vl", [P, JB, 64], F32R, at["gate"] + 12288))]
    hid = place("hid", [64, 2 * P], offset=at["o"])
    hide = place("hide", [64, 2 * P], offset=at["o"] + 1024)
    hidp = (place("hid_h", [P, 2, 2, 64], F32R, at["o"] + 2048),
            place("hid_l", [P, 2, 2, 64], F32R, at["o"] + 3072))
    vct = place("vct", [P, 64], offset=kv0 + 20480)
    kbb = pair("kbb", [P, S], offset=kv0)
    vbz = (place("vbz_h", [P, 2, NQ, P], F32R, kv0 + 4096), place("vbz_l", [P, 2, NQ, P], F32R, kv0 + 8192))
    xr2 = [place("xr20", [P, S], offset=kv0), place("xr21", [P, S], offset=kv0 + 2048)]

    names = [("g_pre", 16), ("g_q", QR_T), ("g_kv", KV_T), ("g_post", 16), ("g_2", 16), ("g_fin", 16),
             ("bf", 32), ("sinks", 16), ("invf", 1), ("sgn64", 1), ("rowok", 4), ("pos_k", 32), ("pos_v", 32)]
    cv, n = {}, 0
    for name, w in names:
        cv[name] = (n, w)
        n += w

    def c(name, j=0, w=1):
        return cvec[:, cv[name][0] + j:cv[name][0] + j + w]

    def bank(name):
        return ctx.enter_context(nc.psum_tensor(name, [P, S], F32))

    sb = [bank(f"scores{i}") for i in range(4)]
    pj = [bank(f"strip{i}") for i in range(2)]
    po, px = bank("outputs"), bank("odds")

    def sem(name):
        return ctx.enter_context(nc.semaphore(name))

    raw_full = [sem(f"raw_full{s}") for s in range(SLOTS)]
    w_hi, w_lo, w_used = sem("w_hi"), sem("w_lo"), sem("w_used")
    cvec_in, consts_in, x_in = sem("cvec_in"), sem("consts_in"), [sem(f"x_in{i}") for i in range(5)]
    pos_in, tri_in, tab2_in = sem("pos_in"), sem("tri_in"), sem("tab2_in")
    x_hi, x_lo, sq_done, sq_used = sem("x_hi"), sem("x_lo"), sem("sq_done"), sem("sq_used")
    acc_ready, sum_done, ms_done, rs_done, rb_done = (sem("acc_ready"), sem("sum_done"), sem("ms_done"),
                                                      sem("rs_done"), sem("rb_done"))
    y_done, ev_act, r_done = sem("y_done"), sem("ev_act"), sem("r_done")
    vt_done = sem("vt_done")
    s_done, nm_done, p_exp, p_norm = sem("s_done"), sem("nm_done"), sem("p_exp"), sem("p_norm")
    pt_done, pt_hi, pt_lo, pv_done, o_done = (sem("pt_done"), sem("pt_hi"), sem("pt_lo"), sem("pv_done"),
                                              sem("o_done"))
    sc_done, pc_exp, pc_norm, ptc_done, ptc_hi, ptc_lo = (sem("sc_done"), sem("pc_exp"), sem("pc_norm"),
                                                          sem("ptc_done"), sem("ptc_hi"), sem("ptc_lo"))
    red, tab, lfs, lft, cumd, aug, augd, selc = (sem("red"), sem("tab"), sem("lfs"), sem("lft"), sem("cumd"),
                                                 sem("aug"), sem("augd"), sem("selc"))
    krd, lat_act, cumh = sem("krd"), sem("lat_act"), sem("cumh")
    xn_in, xn_done, xn_out, x_back = sem("xn_in"), sem("xn_done"), sem("xn_out"), sem("x_back")
    xn_in2 = sem("xn_in2")
    gad, hact, hdve, hpe, fin, stored = sem("gad"), sem("hact"), sem("hdve"), sem("hpe"), sem("fin"), sem("stored")
    blk_made, blk_hi, blk_lo, hid_turned = sem("blk_made"), sem("blk_hi"), sem("blk_lo"), sem("hid_turned")
    prescaled, fin_pool = sem("prescaled"), sem("fin_pool")
    scaled = sem("scaled")
    block = ctx.enter_context(nc.Block())

    @block.sync
    def _(sp):
        sp.dma_start(cvec[:, :n], d["cvec"]).then_inc(cvec_in, 16)

        def x_part(i):
            tiles = slice(X_PARTS[i], X_PARTS[i + 1])
            sp.dma_start(o[:, tiles, :], d["xt"][:, tiles, :]).then_inc(x_in[i], 16)

        def first_unit(u):
            sp.dma_start(raw[u][:, :], d["w"][u, :, :]).then_inc(raw_full[u], 16)

        first_unit(0)
        x_part(0)
        first_unit(1)
        x_part(1)
        x_part(2)
        first_unit(2)
        x_part(3)
        first_unit(3)
        x_part(4)
        for dst, name in ((ident, "ident"), (ones, "ones"), (identb, "identb"), (maskd, "maskd"), (maskw, "maskw"),
                          (maskc, "maskc")):
            sp.dma_start(dst[:, :], d[name]).then_inc(consts_in, 16)
        with sp.Fori(1, U_END // SLOTS) as r:
            for s in range(SLOTS):
                sp.wait_ge(w_lo, r * SLOTS + (s + 1 - SLOTS))
                sp.dma_start(raw[s][:, :], d["w"][bass.ds(r * SLOTS + s, 1), :, :].rearrange("a p n -> p (a n)"))\
                  .then_inc(raw_full[s], 16)
        for u in range(U_END // SLOTS * SLOTS, U_END):
            sp.wait_ge(w_lo, u + 1 - SLOTS)
            sp.dma_start(raw[u % SLOTS][:, :], d["w"][u, :, :]).then_inc(raw_full[u % SLOTS], 16)
        by_dve = by_pool = 0
        for i in range(KT):
            if i % 8 in (1, 4, 7):
                by_pool += 1
                sp.wait_ge(fin_pool, by_pool)
                j = by_pool - 1
            else:
                by_dve += 1
                sp.wait_ge(fin, by_dve)
                j = POOL_TILES + by_dve - 1
            sp.dma_start(d["out"][:, j, :], o[:, j, :]).then_inc(stored, 16)
        sp.wait_ge(stored, 16 * KT)

    @block.gpsimd
    def _(g):
        g.dma_start(posi[:, :], d["pos"]).then_inc(pos_in, 16)
        g.memset(acc[:, :], 0.0)
        for j in range(KT):
            g.drain()
            g.wait_ge(sq_done, j + 1)
            g.tensor_tensor(acc[:, :], acc[:, :], sq[j % 2][:, :], ALU.add).then_inc(sq_used, 1)
        g.drain()
        g.nop().then_inc(acc_ready, 1)
        g.wait_ge(x_lo, KT)
        g.dma_start(sel[:, :, :], d["sel"]).then_inc(tri_in, 16)
        g.dma_start(trif[:, :], d["tri"]).then_inc(tri_in, 16)
        g.wait_ge(o_done, 16)
        for j, w in ((0, 4), (4, 4), (8, 4), (12, 2)):
            g.dma_start(x_again[0][:, j:j + w, :], d["xt"][:, j:j + w, :]).then_inc(x_back, 16)
        g.dma_start(x_again[1][:, :, :], d["xt"][:, 14:16, :]).then_inc(x_back, 16)
        g.wait_ge(x_back, 16 * 5)
        for j in range(KT):
            g.wait_ge(scaled, j + 1)
            g.tensor_tensor(o[:, j, :], o[:, j, :], again[j][0][:, again[j][1], :], ALU.add).then_inc(xn_done, 1)
            if j % 4 == 3:
                g.wait_ge(xn_done, j + 1)
                g.dma_start(d["xn"][:, j - 3:j + 1, :], o[:, j - 3:j + 1, :]).then_inc(xn_out, 16)
        g.dma_start(cos2[:, :], d["cos_a"]).then_inc(tab2_in, 16)
        g.dma_start(sin2[:, :], d["sin_a"]).then_inc(tab2_in, 16)
        g.wait_ge(r_done, N_KVB)
        g.dma_start(cos2[:, :], d["cos_b"]).then_inc(tab2_in, 16)
        g.dma_start(sin2[:, :], d["sin_b"]).then_inc(tab2_in, 16)
        g.wait_ge(o_done, 32)
        for j in range(2):
            g.dma_start(xr2[j][:, :], d["xn"][:, j, :]).then_inc(xn_in if j == 0 else xn_in2, 16)
        with g.Fori(0, KT // 2 - 1) as i:
            for j in range(2):
                g.wait_ge(y_done, N_OUT2 + 1 + j + i * 2)
                g.dma_start(xr2[j][:, :], d["xn"][:, bass.ds(2 * i + 2 + j, 1), :].rearrange("p a n -> p (a n)"))\
                 .then_inc(xn_in if j == 0 else xn_in2, 16)
        g.wait_ge(prescaled, POOL_TILES)
        g.wait_ge(rb_done, 6)
        for j in range(POOL_TILES):
            g.tensor_tensor(o[:, j, :], o[:, j, :], rb[:, :], ALU.mult).then_inc(fin_pool, 1)

    def three(pe, out, ah, al, bh, bl, first, last, shared=False):
        pe.matmul(out, ah, bh, start=first, stop=False, skip_group_check=shared)
        pe.matmul(out, ah, bl, start=False, stop=False, skip_group_check=shared)
        return pe.matmul(out, al, bh, start=False, stop=last, skip_group_check=shared)

    def unit(pe, u, tiles, out, first, last, operand=(xh, xl), ready=None, free=None):
        s = u.slot()
        pe.wait_ge(w_lo, u(1))
        if free is not None:
            pe.wait_ge(y_done, free)
        for i, (a, b) in enumerate(tiles):
            if ready is not None:
                pe.wait_ge(ready[0], ready[1] + b + 1)
            cols = slice(128 * a, 128 * a + 128)
            ins = three(pe, out, wh[s][:, cols], wl[s][:, cols], operand[0][:, b, :], operand[1][:, b, :],
                        first and i == 0, last and i == len(tiles) - 1)
        ins.then_inc(w_used, 1)

    def half(pe, u, n_at, h, free, ready=None, into=None):
        unit(pe, u, [(i, 8 * h + i) for i in range(8)], (into or pj[n_at % 2])[:, :], h == 0, h == 1,
             ready=ready, free=free if h == 0 else None)

    def scores(pe, a, terms, last_a=None):
        for t in range(NQ):
            keys = slice(0, P * (t + 1))
            mine = slice(P * t, P * t + P)
            out = sb[t][:, keys]
            for i, (qq, kk, p0, rows) in enumerate(terms):
                r = slice(p0, p0 + rows)
                three(pe, out, qq[0][r, mine], qq[1][r, mine], kk[0][r, keys], kk[1][r, keys], i == 0, False)
            yield t, out, mine, keys

    def causal(pe, t, a):
        pe.matmul(sb[t][:, P * t:P * t + P], identb[:, :], maskd[:, :], start=False, stop=True).then_inc(s_done, 1)

    def pe_scores(pe, a, terms, extra=False):
        for t, out, mine, keys in scores(pe, a, terms):
            if extra:
                pe.matmul(out, augq[:, mine], augk[:, keys], start=False, stop=False)
            causal(pe, t, a)

    def pe_turn(pe, a):
        pe.wait_ge(p_norm, a + 1)
        for t in range(NQ):
            for w in range(t, NQ):
                ins = pe.transpose(sb[t][:, P * (w - t):P * (w - t) + P], prob[:, ROW[w] + P * t:ROW[w] + P * t + P],
                                   ident[:, :])
            ins.then_inc(pt_done, 1)

    def pe_out(pe, a, vv, first=True, last=True, outs_done=None):
        if first and outs_done is not None:
            pe.wait_ge(o_done, outs_done)
        for t in range(NQ):
            pe.wait_ge(pt_lo, 4 * a + t + 1)
            cols = slice(COL[t], COL[t] + S - P * t)
            ins = three(pe, po[:, P * t:S], vv[0][:, t, :], vv[1][:, t, :], pth[:, cols], ptl[:, cols],
                        first and t == 0, last and t == NQ - 1)
        if last:
            ins.then_inc(pv_done, 1)

    def pe_turn_v(pe, strip, into=px):
        pe.wait_ge(y_done, strip)
        pe.wait_ge(r_done, strip - 1)
        for t in range(NQ):
            ins = pe.transpose(into[:, P * t:P * t + P], yv[:, P * t:P * t + P], ident[:, :])
        ins.then_inc(vt_done, 1)

    def pe_aug(pe, i, which, into=px):
        pe.wait_ge(selc, i + 1)
        pe.matmul(into[:, :], selr[:, P * which:P * which + P], cum[:, :], start=True, stop=True).then_inc(aug, 1)

    def pe_together(pe, u, n_at, steps, count, order=NATURAL, strips=(0, 1), squares=None):
        for j in steps:
            pe.wait_ge(x_lo, count + j + 1)
            for s in strips:
                at_ = At(u + 2 * (j // 8) + s)
                if j % 8 == 0:
                    pe.wait_ge(w_lo, at_(1))
                if j == 0 and n_at + s >= 2:
                    pe.wait_ge(y_done, n_at + s - 1)
                cols = slice(P * (j % 8), P * (j % 8) + P)
                ins = three(pe, pj[(n_at + s) % 2][:, :], wh[at_.slot()][:, cols], wl[at_.slot()][:, cols],
                            xh[:, order[j], :], xl[:, order[j], :], j == 0, j == KT - 1)
                if j % 8 == 7:
                    ins.then_inc(w_used, 1)
            if squares is not None:
                pe.wait_ge(sq_done, squares + j + 1)
                pe.matmul(px[:, :], ones[:, :], sq[j % 2][:, :], start=j == 0, stop=j == KT - 1).then_inc(sq_used, 1)

    def pe_sum(pe, i):
        pe.wait_ge(acc_ready, i + 1)
        pe.matmul(px[:, :], ones[:, :], acc[:, :], start=True, stop=True).then_inc(sum_done, 1)

    @block.tensor
    def _(pe):
        pe_together(pe, U_MISC, N_MISC, range(KT), 0)
        pe.wait_ge(consts_in, 16 * 6)
        pe_sum(pe, 0)
        half(pe, At(U_FOX + 2), N_FOX + 1, 0, None, into=sb[0])
        half(pe, At(U_FOX + 3), N_FOX + 1, 1, None, into=sb[0])
        half(pe, At(U_FOX + 4), N_FOX + 2, 0, None, into=sb[1])
        pe.wait_ge(lfs, 1)
        for t in range(NQ):
            ins = pe.transpose(px[:, P * t:P * t + P], yv[:, P * t:P * t + P], ident[:, :])
        ins.then_inc(lft, 1)
        half(pe, At(U_FOX + 5), N_FOX + 2, 1, None, into=sb[1])
        pe.wait_ge(lfs, 3)
        for t in range(NQ):
            for part in range(2):
                ins = pe.matmul(px[:, P * t:S], lf[part][:, t, :], tri[:, 0:S - P * t],
                                start=t == 0 and part == 0, stop=t == NQ - 1 and part == 1)
        ins.then_inc(cumd, 1)
        half(pe, At(U_FOX + 6), N_FOX + 3, 0, 1)
        pe_aug(pe, 0, 0)
        pe_aug(pe, 0, 1, into=po)
        pe_turn_v(pe, N_FOX + 3, into=sb[2])
        half(pe, At(U_FOX + 7), N_FOX + 3, 1, None)
        pe.wait_ge(augd, 2)

        def fox(h, u, n_, last):
            for s in range(8):
                if s == 0:
                    pe.wait_ge(r_done, n_(-1))
                    pe_scores(pe, h, [(q, k, 0, P)], extra=True)
                if s == 2:
                    pe_turn(pe, h)
                if s == 4:
                    pe_out(pe, h, v)
                if not last:
                    if s == 5:
                        pe_aug(pe, h + 1, 0)
                    if s == 6:
                        pe.wait_ge(augd, 2 * h + 3)
                        pe_aug(pe, h + 1, 1)
                    if s == 7:
                        pe.wait_ge(augd, 2 * h + 4)
                        pe_turn_v(pe, n_(3))
                half(pe, u.on(s), n_.base + s // 2, s % 2, n_(s // 2 - 1))

        with pe.Fori(0, NHEAD - 1) as h:
            fox(h, At(U_FOX + 8, h, 8), At(N_FOX + 4, h, 4), False)
        fox(NHEAD - 1, At(U_GATE), At(N_GATE), True)
        with pe.Fori(0, 2) as i:
            for s in range(4):
                half(pe, At(U_GATE + 8 + s, i, 4), N_GATE + 4 + s // 2, s % 2, N_GATE + 3 + s // 2 + i * 2)
        with pe.Fori(0, 5) as i:
            for s in range(4):
                half(pe, At(U_LAT + s, i, 4), N_LAT + s // 2, s % 2, N_LAT - 1 + s // 2 + i * 2)
        pe_sum(pe, 1)

        def mla_unit(s, u, n_, first):
            which = [0, 1, 2, 3, 3, 4, 5, 6][s]
            if s < 2 or s >= 5 or s == 2:
                tiles = [(i, (0 if MLA_TILES[s] == 6 else QR_T) + i) for i in range(MLA_TILES[s])]
                f, l = True, True
            else:
                tiles = [(i, 3 * (s - 3) + i) for i in range(3)]
                f, l = s == 3, s == 4
            free = n_(which - 1) if which else n_(0)
            if first and which in FIRST_BANK:
                free = None
            if first and which == 5:
                free = n_(2)
            into = sb[FIRST_BANK[which]] if first and which in FIRST_BANK else pj[which % 2]
            unit(pe, u.on(s), tiles, into[:, :], f, l, ready=(x_lo, KT) if first else None,
                 free=free if f else None)

        def pe_mla_scores(a, qq, kk, part):
            pe_scores(pe, a, [(qq, kk, 0, P), (qr, kr, 64 * part, 64)])

        def mla(p, u, n_, steps):
            a = A_MLA + 2 * p
            pe.wait_ge(r_done, n_(-3))
            pe_mla_scores(a, qa, ka, 0)
            if steps:
                mla_unit(0, u, n_, False)
            else:
                pe_together(pe, U_OUT1, N_OUT1, range(8), 2 * KT - 6, EARLY, (0,))
            pe_turn_v(pe, n_(0))
            if steps:
                mla_unit(1, u, n_, False)
            pe_turn(pe, a)
            if steps:
                mla_unit(2, u, n_, False)
                mla_unit(3, u, n_, False)
            pe_out(pe, a, va, outs_done=a)
            pe.wait_ge(r_done, n_(-1))
            pe_mla_scores(a + 1, qb, kb, 1)
            if not steps:
                pe_together(pe, U_OUT1, N_OUT1, range(8), 2 * KT - 6, EARLY, (1,))
            if steps:
                mla_unit(4, u, n_, False)
                pe_turn_v(pe, n_(3))
                mla_unit(5, u, n_, False)
                mla_unit(6, u, n_, False)
            pe_turn(pe, a + 1)
            if steps:
                mla_unit(7, u, n_, False)
            else:
                pe_together(pe, U_OUT1, N_OUT1, range(8, 13), 2 * KT - 6, EARLY)
                pe.wait_ge(r_done, n_(0))
            pe_out(pe, a + 1, vb, outs_done=a + 1)

        n0 = At(N_MLA)
        for s in range(8):
            if s == 1:
                pe.wait_ge(ms_done, 2)
                pe_sum(pe, 2)
            if s == 5:
                pe_turn_v(pe, n0(3))
            mla_unit(s, At(U_MLA), n0, True)
        with pe.Fori(0, 3) as p:
            mla(p, At(U_MLA + 8, p, 8), At(N_MLA + 7, p, 7), True)
        mla(3, At(U_OUT1), At(N_OUT1), False)
        pe_together(pe, U_OUT1, N_OUT1, range(13, KT), 2 * KT - 6, EARLY)
        with pe.Fori(0, KT // 2 - 1) as i:
            for s in range(4):
                half(pe, At(U_OUT1 + 4 + s, i, 4), N_OUT1 + s // 2, s % 2, N_OUT1 + 1 + s // 2 + i * 2)
        pe_sum(pe, 3)
        pe_together(pe, U_CMPIN, N_CMPIN, range(KT), 3 * KT - 6, squares=KT)
        for s in range(4, 8):
            half(pe, At(U_CMPIN + s), N_CMPIN + s // 2, s % 2, None, into=sb[s // 2 - 2])
        with pe.Fori(0, 2) as i:
            for s in range(4):
                half(pe, At(U_KV + s, i, 4), N_KV + s // 2, s % 2, N_KV - 1 + s // 2 + i * 2)
        for s in range(8):
            half(pe, At(U_KV + 8 + s), N_KV + 4 + s // 2, s % 2, N_KV + 3 + s // 2)
            if s in (2, 4, 6):
                pe_turn_v(pe, N_KV + 4 + s // 2)
        half(pe, At(U_GA), N_GA, 0, N_GA - 1)
        pe_turn_v(pe, N_KV + 8)
        half(pe, At(U_GA + 1), N_GA, 1, None)
        pe_turn_v(pe, N_GA + 1)
        def turn_hidden(which):
            pe.wait_ge(gad, which + 1)
            for m in range(2):
                ins = pe.transpose(sb[2 + which][:, 64 * m:64 * m + 64], hid[:, P * m:P * m + P], ident[0:64, 0:64])
            ins.then_inc(hid_turned, 1)

        for which in range(2):
            pe.wait_ge(blk_lo, 2 * which + 2)
            for i in range(8):
                u = At(U_W1 + 8 * which + i)
                pe.wait_ge(w_lo, u(1))
                for a in range(4):
                    j = 4 * i + a
                    cols = slice(256 * a, 256 * a + 256)
                    ins = three(pe, sb[which][0:64, 0:256], blkp[which][0][:, j, :], blkp[which][1][:, j, :],
                                wh[u.slot()][:, cols], wl[u.slot()][:, cols], j == 0, j == JB - 1)
                ins.then_inc(w_used, 1)
                if which and i == 1:
                    turn_hidden(0)
        half(pe, At(U_Q0), N_A, 0, N_A - 1)
        turn_hidden(1)
        half(pe, At(U_Q0 + 1), N_A, 1, None)
        pe.wait_ge(hdve, 2)
        u = At(U_W2)
        pe.wait_ge(w_lo, u(1))
        pe.wait_ge(r_done, N_A)
        for which in range(2):
            for m in range(2):
                cols = slice(256 * which + 128 * m, 256 * which + 128 * m + 128)
                ins = three(pe, px[:, 64 * which:64 * which + 64], wh[u.slot()][:, cols], wl[u.slot()][:, cols],
                            hidp[0][:, which, m, :], hidp[1][:, which, m, :], m == 0, m == 1)
        ins.then_inc(w_used, 1)
        half(pe, At(U_W2 + 1), N_A + 1, 0, N_A)
        pe.wait_ge(hdve, 3)
        for g_ in range(2):
            ins = pe.transpose(px[0:32, P * g_:P * g_ + P], vct[:, 32 * g_:32 * g_ + 32], ident[:, :])
        ins.then_inc(hpe, 1)
        half(pe, At(U_W2 + 2), N_A + 1, 1, None)

        def a_head(h, g_, u, n_):
            kv = kvg[g_]
            a = A_A + 2 * h
            pe.wait_ge(r_done, n_(-1))
            pe_scores(pe, a, [(q2, kv["ks"], 0, P)])
            for t in range(NQ):
                mine = slice(P * t, P * t + P)
                three(pe, px[:, 32 * t:32 * t + 32], q2[0][:, mine], q2[1][:, mine],
                      kcp[0][:, 32 * g_:32 * g_ + 32], kcp[1][:, 32 * g_:32 * g_ + 32], True, False)
                ins = pe.matmul(px[:, 32 * t:32 * t + 32], identb[:, :], maskc[:, 32 * t:32 * t + 32],
                                start=False, stop=True)
            ins.then_inc(sc_done, 1)
            half(pe, u, n_.base, 0, n_(-1))
            pe_turn(pe, a)
            pe.wait_ge(pc_norm, h + 1)
            for t in range(NQ):
                ins = pe.transpose(px[0:32, P * t:P * t + P], pc[:, t, :], ident[:, :])
            ins.then_inc(ptc_done, 1)
            half(pe, u.on(1), n_.base, 1, None)
            pe_out(pe, a, kv["vs"], last=False, outs_done=16 + h)
            pe.wait_ge(ptc_lo, h + 1)
            three(pe, po[:, :], vcp[0][:, g_, :], vcp[1][:, g_, :], ptc[0][:, :], ptc[1][:, :], False, False)
            pe_scores(pe, a + 1, [(q2, kv["kw"], 0, P)])
            half(pe, u.on(2), n_.base + 1, 0, n_(0))
            pe_turn(pe, a + 1)
            half(pe, u.on(3), n_.base + 1, 1, None)
            pe_out(pe, a + 1, kv["vw"], first=False)

        pe.wait_ge(hdve, 4)
        with pe.Fori(0, 4) as h:
            a_head(h, 0, At(U_A, h, 4), At(N_A + 2, h, 2))
        with pe.Fori(4, 7) as h:
            a_head(h, 1, At(U_A, h, 4), At(N_A + 2, h, 2))
        a_head(7, 1, At(U_KVB), At(N_KVB))
        for s in range(4):
            if s == 1:
                pe_turn_v(pe, N_KVB + 2)
            half(pe, At(U_B + s), N_B + s // 2, s % 2, N_B - 1 + s // 2)

        def b_scores(p):
            for hh in range(2):
                r = slice(64 * hh, 64 * hh + 64)
                for t in range(NQ):
                    lo_ = max(t - 1, 0)
                    c0 = WROW[t] - (384 if t >= 2 else 0)
                    out = sb[2 * hh + t // 2]
                    w = P * (t + 1 - lo_)
                    mine = slice(P * t, P * t + P)
                    keys = slice(P * lo_, P * t + P)
                    three(pe, out[:, c0:c0 + w], q2[0][r, mine], q2[1][r, mine], kbb[0][r, keys], kbb[1][r, keys],
                          True, False)
                    if t:
                        pe.matmul(out[:, c0:c0 + P], identb[:, :], maskw[:, :], start=False, stop=False)
                    pe.matmul(out[:, c0 + w - P:c0 + w], identb[:, :], maskd[:, :], start=False, stop=True)\
                      .then_inc(s_done, 1)

        def b_pair(p, u, n_, steps):
            a = 2 * NHEAD + 16
            pe.wait_ge(r_done, n_(-1))
            b_scores(p)
            if steps:
                half(pe, u, n_.base, 0, n_(-1))
                half(pe, u.on(1), n_.base, 1, None)
            else:
                pe_together(pe, U_OUT2, N_OUT2, range(8), 4 * KT - 6)
            pe.wait_ge(p_norm, a + p + 1)
            for hh in range(2):
                for t in range(NQ):
                    for w in range(t, min(t + 2, NQ)):
                        c0 = BANDED * hh + WROW[w] + (0 if w > t or t == 0 else P)
                        ins = pe.transpose(sb[2 * hh + t // 2][:, 256 * (t % 2) + P * (w - t):256 * (t % 2) + P * (w - t) + P],
                                           prob[:, c0:c0 + P], ident[:, :])
                ins.then_inc(pt_done, 1)
            if steps:
                half(pe, u.on(2), n_.base + 1, 0, n_(0))
            else:
                pe_together(pe, U_OUT2, N_OUT2, range(8, 15), 4 * KT - 6)
            if steps:
                half(pe, u.on(3), n_.base + 1, 1, None)
            pe.wait_ge(o_done, 24 + p)
            pe.wait_ge(pt_lo, 4 * a + 2 * p + 2)
            for hh in range(2):
                for t in range(NQ):
                    w = P * (min(t + 2, NQ) - t)
                    cols = slice(BANDED * hh + WCOL[t], BANDED * hh + WCOL[t] + w)
                    ins = three(pe, po[:, P * t:P * t + w], vbz[0][:, hh, t, :], vbz[1][:, hh, t, :],
                                pth[:, cols], ptl[:, cols], hh == 0 and t == 0, hh == 1 and t == NQ - 1, True)
            ins.then_inc(pv_done, 1)

        with pe.Fori(0, NPAIR - 1) as p:
            b_pair(p, At(U_B + 4, p, 4), At(N_B + 2, p, 2), True)
        b_pair(NPAIR - 1, At(U_OUT2), At(N_OUT2), False)
        pe_together(pe, U_OUT2, N_OUT2, range(15, KT), 4 * KT - 6)
        with pe.Fori(0, KT // 2 - 1) as i:
            for s in range(4):
                half(pe, At(U_OUT2 + 4 + s, i, 4), N_OUT2 + s // 2, s % 2, N_OUT2 + 1 + s // 2 + i * 2)
        pe_sum(pe, 4)

    def act_hi(a, u, cols=1024):
        s = u.slot()
        a.wait_ge(raw_full[s], (u.round() + 1) * 16)
        if u.per or u.base >= SLOTS:
            a.wait_ge(w_used, u(1 - SLOTS))
        a.activation(wh[s][:, :cols], raw[s][:, :cols], ACT.Copy).then_inc(w_hi, 1)

    def act_part(a, n_, dst, src):
        a.wait_ge(y_done, n_ + 1)
        a.activation(dst, src, ACT.Copy).then_inc(ev_act, 1)

    def act_part_v(a, turned, dst, src=px):
        a.wait_ge(vt_done, turned)
        a.activation(dst, src[:, :].rearrange("p (t d) -> p t d", t=NQ), ACT.Copy).then_inc(ev_act, 1)

    def act_gate(a, n_, src):
        a.wait_ge(y_done, n_ + 1)
        a.activation(e_t[:, :], src, ACT.Tanh, scale=0.5).then_inc(ev_act, 1)

    def act_exps(a, i, scale):
        a.wait_ge(nm_done, i + 1)
        for t in range(NQ):
            w = P * (t + 1)
            a.activation(prob[:, ROW[t]:ROW[t] + w], sb[t][:, 0:w], ACT.Exp, bias=nms[:, t:t + 1], scale=scale,
                         accum_out=lsum[:, t:t + 1]).then_inc(p_exp, 1)

    def act_turned(a, i):
        for t in range(NQ):
            a.wait_ge(pt_done, 4 * i + t + 1)
            w = S - P * t
            a.activation(pth[:, COL[t]:COL[t] + w], sb[t][:, 0:w], ACT.Copy).then_inc(pt_hi, 1)

    def act_rms(a, i):
        a.wait_ge(ms_done, i + 1)
        a.activation(nrt[:, :], nrm[:, :], ACT.Ln)
        a.drain()
        a.activation(nrt[:, :], nrt[:, :], ACT.Exp, scale=-0.5).then_inc(rs_done, 1)

    @block.scalar
    def _(a):
        a.wait_ge(cvec_in, 16)
        a.activation(nms[:, 0:1], c("invf"), ACT.Copy)
        act_hi(a, At(0))
        act_hi(a, At(1))
        for j in range(KT):
            if j in X_PARTS:
                a.wait_ge(x_in[X_PARTS.index(j)], 16)
            a.activation(xh[:, j, :], o[:, j, :], ACT.Copy, scale=c("g_pre", j)).then_inc(x_hi, 1)
            if j >= 2:
                a.wait_ge(sq_used, j - 1)
            a.activation(sq[j % 2][:, :], o[:, j, :], ACT.Square).then_inc(sq_done, 1)
            if j in (4, 6, 10, 12):
                act_hi(a, At(j // 2 if j < 8 else j // 2 - 1))
        a.wait_ge(tab, 1)
        a.activation(sin_t[:, :], ang[0][:, :], ACT.Sin)
        a.activation(cos_t[:, :], ang[2][:, :], ACT.Sin).then_inc(red, 1)
        act_hi(a, At(6))
        act_rms(a, 0)
        a.wait_ge(y_done, 1)
        a.activation(kr[0][0:64, :], y[0:64, :], ACT.Copy)
        a.activation(kr[0][64:128, :], y[0:64, :], ACT.Copy).then_inc(ev_act, 1)
        act_hi(a, At(7))
        act_part(a, N_FOX, q[0][:, :], y[:, :])
        a.wait_ge(tri_in, 32)
        a.activation(tri[:, :], trif[:, :], ACT.Copy)
        a.wait_ge(lfs, 2)
        a.activation(zf[:, 1, :], zf[:, 1, :], ACT.Exp, scale=-1.0)
        a.drain()
        a.activation(zf[:, 1, :], zf[:, 1, :], ACT.Ln, bias=1.0).then_inc(lat_act, 1)
        act_hi(a, At(8))
        act_part(a, N_FOX + 1, k[0][:, :], y[:, :])
        a.wait_ge(cumd, 1)
        a.activation(cum[0:64, :], px[0:64, :], ACT.Copy, scale=1.0 / SC_FOX).then_inc(cumh, 1)
        act_hi(a, At(9))
        a.wait_ge(krd, 1)

        def act_sel(i, reg):
            a.activation(selr[:, :], sel[:, reg, :].rearrange("p a n -> p (a n)") if not isinstance(reg, int)
                         else sel[:, reg, :], ACT.Copy).then_inc(selc, 1)

        def act_aug(count, dst, src=px):
            a.wait_ge(aug, count)
            a.activation(dst[:, :], src[:, :], ACT.Copy).then_inc(augd, 1)

        act_sel(0, 0)
        act_hi(a, At(10))
        act_aug(1, augk)
        act_aug(2, augq, po)
        act_part_v(a, 1, v[0][:, :, :], sb[2])
        act_hi(a, At(11))

        def fox(h, u, n_, last):
            for s in range(8):
                act_hi(a, u.on(s + LEAD))
                if s == 0:
                    act_gate(a, n_(-1), y[:, :])
                    act_exps(a, h, SC_FOX)
                if s == 1 and not last:
                    act_sel(h + 1, bass.ds(h + 1, 1))
                if s == 2:
                    if last:
                        act_gate(a, n_(0), y[:, :])
                    else:
                        act_part(a, n_(0), q[0][:, :], y[:, :])
                    act_turned(a, h)
                if s == 4:
                    if last:
                        act_gate(a, n_(1), y[:, :])
                    else:
                        act_part(a, n_(1), k[0][:, :], y[:, :])
                if s == 5 and not last:
                    act_aug(2 * h + 3, augk)
                if s == 6:
                    if last:
                        act_gate(a, n_(2), y[:, :])
                    else:
                        act_aug(2 * h + 4, augq)
                if s == 7:
                    if last:
                        act_gate(a, n_(3), y[:, :])
                    else:
                        act_part_v(a, h + 2, v[0][:, :, :])

        with a.Fori(0, NHEAD - 1) as h:
            fox(h, At(U_FOX + 8, h, 8), At(N_FOX + 4, h, 4), False)
        fox(NHEAD - 1, At(U_GATE), At(N_GATE), True)

        def two_strips(u, evac):
            act_hi(a, u.on(2))
            act_hi(a, u.on(3))
            evac(0)
            act_hi(a, u.on(4))
            act_hi(a, u.on(5))
            evac(1)

        with a.Fori(0, 2) as i:
            two_strips(At(U_GATE + 8, i, 4), lambda j: act_gate(a, N_GATE + 4 + j + i * 2, y[:, :]))

        def lat_square(n_, src):
            a.wait_ge(y_done, n_ + 1)
            a.activation(e_t[:, :], src, ACT.Square).then_inc(ev_act, 1)

        def lat_hi(tiles):
            for j in tiles:
                g_ = c("g_q", j) if j < QR_T else c("g_kv", j - QR_T)
                a.activation(xh[:, j, :], lat[:, j, :], ACT.Copy, scale=g_).then_inc(x_hi, 1)

        with a.Fori(0, 4) as i:
            two_strips(At(U_LAT, i, 4), lambda j: lat_square(
                N_LAT + j + i * 2, lat[:, bass.ds(2 * i + j, 1), :].rearrange("p a n -> p (a n)")))
        u = At(U_LAT + 16)
        act_hi(a, u.on(2))
        act_hi(a, u.on(3))
        lat_square(N_LAT + 8, lat[:, 8, :])
        act_hi(a, u.on(4))
        act_hi(a, u.on(5))
        a.wait_ge(w_used, U_MLA - 1)
        lat_hi(range(8))
        lat_square(N_LAT + 9, lat[:, 9, :])
        a.wait_ge(w_used, U_MLA)
        lat_hi(range(8, QR_T + KV_T))

        def mla_evacs(n_, k_):
            if k_ in (2, 6):
                return
            dst = {0: qa, 1: ka, 3: qr, 4: qb, 5: kb}[k_]
            act_part(a, n_(k_), dst[0][:, :], (yv if k_ == 4 else y)[:, :])

        def mla_hi(u, s):
            m = (s + LEAD) % 8
            act_hi(a, u.on(s + LEAD), 1024 if m < 2 else 128 * MLA_TILES[m])

        n0 = At(N_MLA)
        u0 = At(U_MLA)
        mla_hi(u0, 0)
        act_rms(a, 1)
        mla_hi(u0, 1)
        act_rms(a, 2)
        mla_hi(u0, 2)
        for s, strip in enumerate([None, 0, 1, None, None, 3, 4, 5]):
            if s > 2:
                mla_hi(u0, s)
            if s == 5:
                act_part_v(a, NHEAD + 1, va[0][:, :, :])
            if strip is not None:
                mla_evacs(n0, strip)

        def out_hi(tiles):
            for j in tiles:
                a.activation(xh[:, j, :], o[:, j, :], ACT.Copy).then_inc(x_hi, 1)

        def mla(p, u, n_, steps):
            i = A_MLA + 2 * p
            if steps:
                mla_hi(u, 0)
            else:
                a.wait_ge(w_used, U_OUT1)
                a.wait_ge(o_done, 14)
                out_hi(EARLY[:8])
            act_exps(a, i, SC_MLA)
            if steps:
                mla_hi(u, 1)
            else:
                act_hi(a, u.on(2))
                act_hi(a, u.on(3))
            act_part_v(a, NHEAD + 2 + p * 2, vb[0][:, :, :])
            if steps:
                mla_evacs(n_, 0)
                mla_hi(u, 2)
                mla_evacs(n_, 1)
            act_turned(a, i)
            if steps:
                mla_hi(u, 3)
                mla_hi(u, 4)
            act_exps(a, i + 1, SC_MLA)
            if steps:
                mla_hi(u, 5)
                act_part_v(a, NHEAD + 3 + p * 2, va[0][:, :, :])
                mla_evacs(n_, 3)
                mla_hi(u, 6)
                mla_evacs(n_, 4)
            else:
                a.wait_ge(o_done, 15)
                out_hi(EARLY[8:13])
            act_turned(a, i + 1)
            if steps:
                mla_hi(u, 7)
                mla_evacs(n_, 5)

        with a.Fori(0, 3) as p:
            mla(p, At(U_MLA + 8, p, 8), At(N_MLA + 7, p, 7), True)
        mla(3, At(U_OUT1), At(N_OUT1), False)
        out_hi(EARLY[13:15])
        a.wait_ge(o_done, 16)
        out_hi(EARLY[15:])

        def out_square(n_, src):
            a.wait_ge(y_done, n_ + 1)
            a.activation(e_t[:, :], src, ACT.Square).then_inc(ev_act, 1)

        for j in range(2):
            act_hi(a, At(U_OUT1 + 4 + j))
        for j in range(2):
            out_square(N_OUT1 + j, o[:, j, :])
        with a.Fori(0, KT // 2 - 1) as i:
            two_strips(At(U_OUT1 + 4, i, 4), lambda j: out_square(
                N_OUT1 + 2 + j + i * 2, o[:, bass.ds(2 * i + 2 + j, 1), :].rearrange("p a n -> p (a n)")))
        act_hi(a, At(U_CMPIN + 2))
        act_hi(a, At(U_CMPIN + 3))
        act_rms(a, 3)
        for j in range(KT):
            a.wait_ge(xn_done, j + 1)
            a.activation(xh[:, j, :], o[:, j, :], ACT.Copy, scale=c("g_2", j)).then_inc(x_hi, 1)
            if j >= 2:
                a.wait_ge(sq_used, KT + j - 1)
            a.activation(sq[j % 2][:, :], o[:, j, :], ACT.Square).then_inc(sq_done, 1)
            if j in (11, 13):
                act_hi(a, At(U_CMPIN + (j - 3) // 2))
        act_hi(a, At(U_CMPIN + 6))
        act_rms(a, 4)
        act_hi(a, At(U_CMPIN + 7))
        act_hi(a, At(U_CMPIN + 8))
        act_hi(a, At(U_CMPIN + 9))

        def kv_loop(base, nbase, first_turn):
            for g_ in range(2):
                def evac(j):
                    n_ = nbase + 2 * g_ + j
                    if first_turn is None:
                        blocks_hi(2 * g_ + j)
                        act_part(a, n_, kvg[g_][("ks", "kw")[j]][0][:, :], y[:, :])
                    else:
                        act_part_v(a, first_turn + 2 * g_ + j, kvg[g_][("vs", "vw")[j]][0][:, :, :])
                two_strips(At(base + 4 * g_), evac)

        def blocks_hi(i):
            a.wait_ge(blk_made, i + 1)
            a.activation(blkp[i // 2][0][:, 16 * (i % 2):16 * (i % 2) + 16, :], blk[:, :, :], ACT.Copy).then_inc(blk_hi, 1)

        kv_loop(U_KV, N_KV, None)
        kv_loop(U_KV + 8, N_KV + 4, 17)
        act_hi(a, At(U_GA + 2))
        act_hi(a, At(U_GA + 3))
        a.wait_ge(vt_done, 21)
        a.activation(gat[:, :, :], px[:, :].rearrange("p (t d) -> p t d", t=NQ)[:, :, 0:24], ACT.Tanh,
                     scale=0.5).then_inc(ev_act, 1)
        def hidden_hi(which):
            a.wait_ge(hid_turned, which + 1)
            a.activation(hidp[0][:, which, :, :], sb[2 + which][:, 0:P].rearrange("p (m c) -> p m c", m=2), ACT.Copy,
                         scale=0.5).then_inc(hact, 1)

        for which in range(2):
            for i in range(8):
                act_hi(a, At(U_W1 + 8 * which + i + LEAD))
                if which and i == 2:
                    hidden_hi(0)
            a.wait_ge(w_used, U_W1 + 8 * which + 8)
            a.activation(hide[:, :], sb[which][0:64, 0:256], ACT.Tanh, scale=0.5).then_inc(hact, 1)
        act_hi(a, At(U_W2), 512)
        hidden_hi(1)
        act_hi(a, At(U_W2 + 1))
        act_part(a, N_A, q2[0][:, :], y[:, :])
        a.wait_ge(w_used, U_W2 + 1)
        a.activation(kcp[0][:, :], px[:, 0:64], ACT.Copy).then_inc(hact, 1)
        act_hi(a, At(U_W2 + 2))
        a.wait_ge(hpe, 1)
        a.activation(vcp[0][:, :, :], px[0:32, 0:256].rearrange("p (g d) -> p g d", g=2), ACT.Copy).then_inc(hact, 1)
        act_hi(a, At(U_A))
        act_hi(a, At(U_A + 1))

        def a_head(h, g_, u, n_, last):
            i = A_A + 2 * h
            act_hi(a, u.on(2))
            act_gate(a, n_(-1), y[:, :])
            act_exps(a, i, SC_A)
            a.wait_ge(pc_exp, h + 1)
            for t in range(NQ):
                ins = a.activation(pc[:, t, :], px[:, 32 * t:32 * t + 32], ACT.Exp, bias=nms[:, 4 + t:5 + t],
                                   scale=SC_A, accum_out=lsum[:, 4 + t:5 + t])
            ins.then_inc(hact, 1)
            act_hi(a, u.on(3))
            act_turned(a, i)
            a.wait_ge(ptc_done, h + 1)
            a.activation(ptc[0][:, :], px[0:32, :], ACT.Copy).then_inc(ptc_hi, 1)
            act_hi(a, u.on(4))
            act_exps(a, i + 1, SC_A)
            if last:
                act_part(a, n_(0), kbb[0][:, :], y[:, :])
            else:
                act_part(a, n_(0), q2[0][:, :], y[:, :])
            act_hi(a, u.on(5))
            act_turned(a, i + 1)

        with a.Fori(0, 4) as h:
            a_head(h, 0, At(U_A, h, 4), At(N_A + 2, h, 2), False)
        with a.Fori(4, 7) as h:
            a_head(h, 1, At(U_A, h, 4), At(N_A + 2, h, 2), False)
        a_head(7, 1, At(U_KVB), At(N_KVB), True)
        act_hi(a, At(U_B + 2))
        a.wait_ge(vt_done, 22)
        pxv = px[:, :].rearrange("p (t d) -> p t d", t=NQ)
        a.activation(vbz[0][:, 0, :, 0:64], pxv[:, :, 0:64], ACT.Copy)
        a.activation(vbz[0][:, 1, :, 64:128], pxv[:, :, 64:128], ACT.Copy).then_inc(ev_act, 1)
        act_hi(a, At(U_B + 3))
        act_part(a, N_B, q2[0][:, :], y[:, :])
        act_hi(a, At(U_B + 4))
        act_hi(a, At(U_B + 5))

        def b_pair(p, u, n_, steps):
            if steps:
                act_hi(a, u.on(2))
            act_gate(a, n_(-1), y[:, :])
            if not steps:
                out_hi(range(8))
            a.wait_ge(nm_done, 33 + p)
            for hh in range(2):
                snk = cvec[:, bass.ds(p + (cv["sinks"][0] + 8 * hh), 1)]
                for t in range(NQ):
                    w = P if t == 0 else 2 * P
                    c0 = WROW[t] - (384 if t >= 2 else 0)
                    a.activation(prob[:, BANDED * hh + WROW[t]:BANDED * hh + WROW[t] + w],
                                 sb[2 * hh + t // 2][:, c0:c0 + w], ACT.Exp, bias=nms[:, 4 * hh + t:4 * hh + t + 1],
                                 scale=SC_B, accum_out=lsum[:, 4 * hh + t:4 * hh + t + 1])
                ins = a.activation(lsum[:, 8 + 4 * hh:12 + 4 * hh], nms[:, 4 * hh:4 * hh + 4], ACT.Exp, bias=snk)
            ins.then_inc(p_exp, 1)
            if steps:
                act_hi(a, u.on(3))
                act_part(a, n_(0), q2[0][:, :], y[:, :])
                act_hi(a, u.on(4))
            else:
                act_hi(a, u.on(2))
                act_hi(a, u.on(3))
                a.wait_ge(o_done, 31)
                out_hi(range(8, 15))
            for hh in range(2):
                for b_ in range(2):
                    w = 512 if b_ == 0 else 384
                    if b_ == 0:
                        a.wait_ge(pt_done, 4 * 32 + 2 * p + hh + 1)
                    c0 = BANDED * hh + 512 * b_
                    ins = a.activation(pth[:, c0:c0 + w], sb[2 * hh + b_][:, 0:w], ACT.Copy)
                ins.then_inc(pt_hi, 1)
            if steps:
                act_hi(a, u.on(5))

        with a.Fori(0, NPAIR - 1) as p:
            b_pair(p, At(U_B + 4, p, 4), At(N_B + 2, p, 2), True)
        b_pair(NPAIR - 1, At(U_OUT2), At(N_OUT2), False)
        a.wait_ge(o_done, 32)
        out_hi([15])
        for j in range(2):
            act_hi(a, At(U_OUT2 + 4 + j))
        for j in range(2):
            out_square(N_OUT2 + j, o[:, j, :])
        with a.Fori(0, KT // 2 - 2) as i:
            two_strips(At(U_OUT2 + 4, i, 4), lambda j: out_square(
                N_OUT2 + 2 + j + i * 2, o[:, bass.ds(2 * i + 2 + j, 1), :].rearrange("p a n -> p (a n)")))
        for j in range(POOL_TILES):
            a.activation(o[:, j, :], o[:, j, :], ACT.Copy, scale=c("g_fin", j)).then_inc(prescaled, 1)
        act_hi(a, At(U_END - 2))
        act_hi(a, At(U_END - 1))
        for j in range(2):
            out_square(N_OUT2 + 14 + j, o[:, 14 + j, :])
        act_rms(a, 5)

    def lo(v_, u, cols=1024):
        s = u.slot()
        v_.wait_ge(w_hi, u(1))
        v_.tensor_tensor(wl[s][:, :cols], raw[s][:, :cols], wh[s][:, :cols].bitcast(F32), ALU.subtract)\
          .then_inc(w_lo, 1)

    def take(v_, n_, bank_, used, times, dst):
        v_.drain()
        v_.wait_ge(w_used, used)
        src = pj[bank_] if isinstance(bank_, int) else bank_
        v_.tensor_tensor(dst, src[:, :], times[:, :], ALU.mult).then_inc(y_done, 1)

    def take_rope(v_, bank_, used, cos_, sin_, half_, dst, rows=P, bump=True):
        v_.drain()
        v_.wait_ge(w_used, used)
        src = pj[bank_] if isinstance(bank_, int) else bank_
        for p0 in range(0, rows, 2 * half_):
            a_, b_ = slice(p0, p0 + half_), slice(p0 + half_, p0 + 2 * half_)
            v_.tensor_tensor(e_t[a_, :], src[b_, :], sin_[a_, :], ALU.mult)
            v_.tensor_tensor(e_t[b_, :], src[a_, :], sin_[b_, :], ALU.mult)
        v_.tensor_tensor(dst, src[0:rows, :], cos_[0:rows, :], ALU.mult)
        v_.drain()
        v_.tensor_tensor(dst, dst, e_t[0:rows, :], ALU.add).then_inc(y_done, 1)

    def rest(v_, n_, dst, src, hi):
        v_.drain()
        v_.wait_ge(ev_act, n_ + 1)
        v_.tensor_tensor(dst, src, hi.bitcast(F32), ALU.subtract).then_inc(r_done, 1)

    def rest_y(v_, n_, pr):
        rest(v_, n_, pr[1][:, :], y[:, :], pr[0][:, :])

    def rest_v(v_, n_, pr, src=px):
        rest(v_, n_, pr[1][:, :, :], src[:, :].rearrange("p (t d) -> p t d", t=NQ), pr[0][:, :, :])

    def silu(v_, n_, dst):
        v_.drain()
        v_.wait_ge(ev_act, n_ + 1)
        v_.scalar_tensor_tensor(dst, e_t[:, :], 1.0, y[:, :], ALU.add, ALU.mult).then_inc(r_done, 1)

    def maxima(v_, i, scale):
        v_.drain()
        for t in range(NQ):
            v_.wait_ge(s_done, 4 * i + t + 1)
            v_.tensor_reduce(nm[:, t:t + 1], sb[t][:, 0:P * (t + 1)], AX.X, ALU.max, negate=True)
        v_.drain()
        v_.tensor_scalar(nms[:, 0:4], nm[:, 0:4], scale, None, ALU.mult).then_inc(nm_done, 1)

    def divide(v_, i, times=None):
        v_.drain()
        v_.wait_ge(p_exp, 4 * i + 4)
        v_.reciprocal(rinv[:, 0:4], lsum[:, 0:4])
        v_.drain()
        if times is not None:
            v_.tensor_tensor(rinv[:, 0:4], rinv[:, 0:4], times, ALU.mult)
            v_.drain()
        for t in range(NQ):
            cols = slice(ROW[t], ROW[t] + P * (t + 1))
            ins = v_.tensor_scalar(prob[:, cols], prob[:, cols], rinv[:, t:t + 1], None, ALU.mult)
        ins.then_inc(p_norm, 1)

    def turned(v_, i):
        for t in range(NQ):
            v_.wait_ge(pt_hi, 4 * i + t + 1)
            w = S - P * t
            cols = slice(COL[t], COL[t] + w)
            v_.tensor_tensor(ptl[:, cols], sb[t][:, 0:w], pth[:, cols].bitcast(F32), ALU.subtract)\
              .then_inc(pt_lo, 1)

    def head_out(v_, i, dst, by):
        v_.drain()
        v_.wait_ge(pv_done, i + 1)
        v_.scalar_tensor_tensor(dst, po[:, :], 0.5, by, ALU.mult, ALU.mult).then_inc(o_done, 1)

    def o_at(reg):
        if isinstance(reg, int):
            return o[:, reg, :]
        return o[:, bass.ds(reg, 1), :].rearrange("p a n -> p (a n)")

    def rms_ms(v_, i, width):
        v_.drain()
        if i == 4:
            v_.wait_ge(sq_used, 2 * KT)
        else:
            v_.wait_ge(sum_done, i + 1 if i < 4 else 5)
        v_.tensor_scalar(nrm[:, :], px[:, :], 1.0 / width, EPS, ALU.mult, ALU.add).then_inc(ms_done, 1)

    def rms_rb(v_, i, dst):
        v_.drain()
        v_.wait_ge(rs_done, i + 1)
        v_.tensor_tensor(e_t[:, :], nrt[:, :], nrt[:, :], ALU.mult)
        v_.drain()
        v_.scalar_tensor_tensor(e_t[:, :], e_t[:, :], -0.5, nrm[:, :], ALU.mult, ALU.mult)
        v_.drain()
        v_.scalar_tensor_tensor(dst[:, :], e_t[:, :], 1.5, nrt[:, :], ALU.add, ALU.mult).then_inc(rb_done, 1)
        v_.drain()

    @block.vector
    def _(v_):
        v_.wait_ge(cvec_in, 16)
        v_.wait_ge(pos_in, 16)

        def angles():
            v_.tensor_copy(ang[0][:, :], posi[:, :])
            v_.drain()
            v_.tensor_scalar(ang[0][:, :], ang[0][:, :], c("invf"), None, ALU.mult)
            v_.drain()
            v_.tensor_scalar(ang[1][:, :], ang[0][:, :], 1.0 / (2 * math.pi), 12582912.0, ALU.mult, ALU.add)
            v_.drain()
            v_.tensor_scalar(ang[1][:, :], ang[1][:, :], -12582912.0, None, ALU.add)

        def reduce_angles():
            c1 = 6.28125
            c2 = float(np.float32(np.round((2 * math.pi - c1) * 2 ** 20) / 2 ** 20))
            c3 = 2 * math.pi - c1 - c2
            for part in (c1, c2, c3):
                v_.drain()
                v_.scalar_tensor_tensor(ang[0][:, :], ang[1][:, :], -part, ang[0][:, :], ALU.mult, ALU.add)

        def both_angles():
            pi = 3.1415925
            v_.drain()
            v_.tensor_scalar(ang[2][:, :], ang[0][:, :], math.pi / 2, None, ALU.add)
            v_.drain()
            v_.tensor_scalar(ang[1][:, :], ang[2][:, :], math.pi, -2 * math.pi, ALU.is_gt, ALU.mult)
            v_.tensor_scalar(ang[0][:, :], ang[0][:, :], pi, -pi, ALU.min, ALU.max)
            v_.drain()
            v_.tensor_tensor(ang[2][:, :], ang[2][:, :], ang[1][:, :], ALU.add)
            v_.drain()
            v_.tensor_scalar(ang[2][:, :], ang[2][:, :], pi, -pi, ALU.min, ALU.max).then_inc(tab, 1)

        angles()
        lo(v_, At(0))
        lo(v_, At(1))

        def x_rest(j, src, g_, count):
            v_.wait_ge(x_hi, count + j + 1)
            if g_ is None:
                v_.tensor_tensor(xl[:, j, :], src, xh[:, j, :].bitcast(F32), ALU.subtract).then_inc(x_lo, 1)
            else:
                v_.scalar_tensor_tensor(xl[:, j, :], src, g_, xh[:, j, :].bitcast(F32), ALU.mult, ALU.subtract)\
                  .then_inc(x_lo, 1)

        for j in range(KT):
            x_rest(j, o[:, j, :], c("g_pre", j), 0)
            if j == 8:
                reduce_angles()
            if j == 11:
                both_angles()
            if j in (4, 6, 10, 12):
                lo(v_, At(j // 2 if j < 8 else j // 2 - 1))
        lo(v_, At(6))
        v_.wait_ge(red, 1)
        v_.tensor_scalar(sin_t[:, :], sin_t[:, :], c("sgn64"), None, ALU.mult)
        rms_ms(v_, 0, D)
        rms_rb(v_, 0, rb)
        v_.tensor_tensor(gate[:, :], cos_t[:, :], rb[:, :], ALU.mult)
        v_.tensor_tensor(nrt[:, :], sin_t[:, :], rb[:, :], ALU.mult)
        v_.wait_ge(w_used, 3)
        v_.tensor_tensor(yv[:, :], pj[0][:, :], rb[:, :], ALU.mult).then_inc(lfs, 1)
        take_rope(v_, 0, 3, gate, nrt, 32, y[0:64, :], rows=64)
        v_.drain()
        v_.wait_ge(ev_act, 1)
        v_.tensor_tensor(kr[1][0:64, :], y[0:64, :], kr[0][0:64, :].bitcast(F32), ALU.subtract)
        v_.drain()
        v_.tensor_copy(kr[1][64:128, :], kr[1][0:64, :].bitcast(F32)).then_inc(r_done, 1)
        lo(v_, At(7))
        take(v_, N_FOX, 1, U_FOX + 2, rb, y[:, :])
        rest_y(v_, N_FOX, q)
        v_.wait_ge(lft, 1)
        z = [zf[:, i, :].rearrange("p (t h) -> p t h", t=NQ) for i in range(3)]
        v_.memset(lf[0][:, :, :].bitcast(F32), 0.0)
        v_.memset(lf[1][:, :, :].bitcast(F32), 0.0)
        v_.tensor_tensor(z[0], px[:, :].rearrange("p (t d) -> p t d", t=NQ)[:, :, 64:72],
                         c("bf", 0, 32).rearrange("p (t h) -> p t h", t=NQ), ALU.add)
        v_.drain()
        v_.scalar_tensor_tensor(zf[:, 1, :], zf[:, 0, :], -1.0, zf[:, 0, :], ALU.mult, ALU.max).then_inc(lfs, 1)
        v_.wait_ge(lat_act, 1)
        v_.scalar_tensor_tensor(zf[:, 2, :], zf[:, 0, :], 0.0, zf[:, 1, :], ALU.min, ALU.subtract)
        v_.drain()
        for col in (0, 32):
            v_.tensor_copy(lf[0][:, :, col:col + 8], z[2])
        v_.drain()
        for col in (0, 32):
            ins = v_.tensor_tensor(lf[1][:, :, col:col + 8], z[2], lf[0][:, :, col:col + 8].bitcast(F32), ALU.subtract)
        ins.then_inc(lfs, 1)
        lo(v_, At(8))
        take(v_, N_FOX + 1, sb[0], U_FOX + 4, rb, y[:, :])
        rest_y(v_, N_FOX + 1, k)
        v_.memset(cum[64:96, :].bitcast(F32), 1.0)
        v_.memset(cum[96:128, :].bitcast(F32), 0.0)
        v_.wait_ge(cumh, 1)
        v_.scalar_tensor_tensor(cum[32:64, :], px[32:64, :], 1.0 / SC_FOX, cum[32:64, :].bitcast(F32), ALU.mult,
                                ALU.subtract).then_inc(krd, 1)
        take(v_, N_FOX + 2, sb[1], U_FOX + 6, rb, yv[:, :])
        lo(v_, At(9))
        lo(v_, At(10))
        rest_v(v_, N_FOX + 2, v, sb[2])
        lo(v_, At(11))

        def fox(h, u, n_, last):
            b = n_.base % 2
            lo(v_, u.on(2))
            take(v_, None, 1 - b, u(0), rb, y[:, :])
            maxima(v_, h, SC_FOX)
            lo(v_, u.on(3))
            divide(v_, h)
            silu(v_, n_(-1), gate[:, :])
            for s in range(2, 8):
                lo(v_, u.on(s + LEAD))
                if s in (2, 4, 6):
                    j = s // 2 - 1
                    take(v_, None, (b + j) % 2, u(s), rb, yv[:, :] if j == 2 and not last else y[:, :])
                if s == 2:
                    turned(v_, h)
                    if last:
                        silu(v_, n_(0), o[:, 0, :])
                    else:
                        rest_y(v_, n_(0), q)
                if s == 4:
                    if last:
                        silu(v_, n_(1), o[:, 1, :])
                    else:
                        rest_y(v_, n_(1), k)
                    head_out(v_, h, o_at(h + 8), gate[:, :])
                if s == 6 and last:
                    silu(v_, n_(2), o[:, 2, :])
                if s == 7:
                    if last:
                        take(v_, None, (b + 3) % 2, u(8), rb, y[:, :])
                        silu(v_, n_(3), o[:, 3, :])
                    else:
                        rest_v(v_, n_(2), v)

        with v_.Fori(0, NHEAD - 1) as h:
            fox(h, At(U_FOX + 8, h, 8), At(N_FOX + 4, h, 4), False)
        fox(NHEAD - 1, At(U_GATE), At(N_GATE), True)

        def two_strips(u, evac):
            lo(v_, u.on(2))
            lo(v_, u.on(3))
            evac(0, u(2))
            lo(v_, u.on(4))
            lo(v_, u.on(5))
            evac(1, u(4))

        with v_.Fori(0, 2) as i:
            def evac(j, used):
                take(v_, None, (N_GATE + j) % 2, used, rb, y[:, :])
                silu(v_, N_GATE + 4 + j + i * 2, o_at(4 + j + i * 2))
            two_strips(At(U_GATE + 8, i, 4), evac)
        v_.memset(acc[:, :], 0.0)
        v_.memset(sq[0][:, :], 0.0)
        def lat_evac(n_, into):
            v_.drain()
            v_.wait_ge(ev_act, n_ + 1)
            v_.tensor_tensor(into[:, :], into[:, :], e_t[:, :], ALU.add).then_inc(r_done, 1)

        for first, laps, into in ((0, 3, acc), (3, 1, sq[0])):
            with v_.Fori(first, first + laps) as i:
                def evac(j, used):
                    take(v_, None, (N_LAT + j) % 2, used, rb,
                         lat[:, bass.ds(i * 2 + j, 1), :].rearrange("p a n -> p (a n)"))
                    lat_evac(N_LAT + j + i * 2, into)
                two_strips(At(U_LAT, i, 4), evac)
        v_.drain().then_inc(acc_ready, 1)

        def lat_lo(tiles):
            for j in tiles:
                x_rest(j, lat[:, j, :], c("g_q", j) if j < QR_T else c("g_kv", j - QR_T), KT)

        u = At(U_LAT + 16)
        lo(v_, u.on(2))
        lo(v_, u.on(3))
        take(v_, None, N_LAT % 2, u(2), rb, lat[:, 8, :])
        lat_evac(N_LAT + 8, sq[0])
        lo(v_, u.on(4))
        lo(v_, u.on(5))
        lat_lo(range(8))
        take(v_, None, (N_LAT + 1) % 2, u(4), rb, lat[:, 9, :])
        lat_evac(N_LAT + 9, sq[0])
        rms_ms(v_, 1, QR_T * P)
        v_.tensor_copy(acc[:, :], sq[0][:, :]).then_inc(acc_ready, 1)
        lat_lo(range(8, QR_T + KV_T))
        def mla_lo(u, s):
            m = (s + LEAD) % 8
            lo(v_, u.on(s + LEAD), 1024 if m < 2 else 128 * MLA_TILES[m])

        def mla_take(k_, used, first=False):
            from_ = sb[FIRST_BANK[k_]] if first and k_ in FIRST_BANK else k_ % 2
            if k_ == 3:
                take_rope(v_, from_, used, cosq, sinq, 32, y[:, :])
            else:
                take(v_, None, from_, used, rq if k_ in (0, 4) else rkv,
                     yv[:, :] if k_ in (2, 4, 6) else y[:, :])

        dst = {0: qa, 1: ka, 3: qr, 4: qb, 5: kb}

        def rest_of(n_, k_):
            rest(v_, n_(k_), dst[k_][1][:, :], (yv if k_ == 4 else y)[:, :], dst[k_][0][:, :])

        n0, u0 = At(N_MLA), At(U_MLA)
        mla_lo(u0, 0)
        rms_rb(v_, 1, rq)
        mla_lo(u0, 1)
        rms_ms(v_, 2, KV_T * P)
        rms_rb(v_, 2, rkv)
        mla_lo(u0, 2)
        v_.tensor_tensor(cosq[:, :], cos_t[:, :], rq[:, :], ALU.mult)
        v_.tensor_tensor(sinq[:, :], sin_t[:, :], rq[:, :], ALU.mult)
        for s, strip in enumerate([None, 0, 1, 2, None, 3, 4, 5]):
            if s > 2:
                mla_lo(u0, s)
            if strip is not None:
                mla_take(strip, u0(s), True)
            if s == 5:
                rest_v(v_, n0(2), va)
            if strip is not None and strip != 2:
                rest_of(n0, strip)

        def out_lo(steps_):
            for j in steps_:
                v_.wait_ge(x_hi, 2 * KT - 6 + j + 1)
                v_.tensor_tensor(xl[:, EARLY[j], :], o[:, EARLY[j], :], xh[:, EARLY[j], :].bitcast(F32), ALU.subtract)\
                  .then_inc(x_lo, 1)

        def mla(p, u, n_, steps):
            i = A_MLA + 2 * p
            if steps:
                mla_lo(u, 0)
            mla_take(6, u(0))
            if not steps:
                out_lo(range(4))
            maxima(v_, i, SC_MLA)
            if not steps:
                out_lo(range(4, 8))
            if steps:
                mla_lo(u, 1)
            rest_v(v_, n_(-1), vb)
            divide(v_, i)
            if not steps:
                lo(v_, u.on(2))
                lo(v_, u.on(3))
            if steps:
                mla_take(0, u(1))
                rest_y(v_, n_(0), qa)
                mla_lo(u, 2)
                mla_take(1, u(2))
                rest_y(v_, n_(1), ka)
            turned(v_, i)
            if steps:
                mla_lo(u, 3)
                mla_take(2, u(3))
                mla_lo(u, 4)
            head_out(v_, i, o_at(p * 2), o_at(p * 2))
            maxima(v_, i + 1, SC_MLA)
            if steps:
                mla_take(3, u(5))
                mla_lo(u, 5)
            divide(v_, i + 1)
            if steps:
                rest_v(v_, n_(2), va)
                mla_take(4, u(6))
                rest_of(n_, 3)
                mla_lo(u, 6)
                rest_of(n_, 4)
            else:
                out_lo(range(8, 13))
            turned(v_, i + 1)
            if steps:
                mla_lo(u, 7)
                mla_take(5, u(7))
                rest_y(v_, n_(5), kb)
            head_out(v_, i + 1, o_at(p * 2 + 1), o_at(p * 2 + 1))

        with v_.Fori(0, 3) as p:
            mla(p, At(U_MLA + 8, p, 8), At(N_MLA + 7, p, 7), True)
        mla(3, At(U_OUT1), At(N_OUT1), False)
        out_lo(range(13, KT))
        v_.memset(acc[:, :], 0.0)

        def add_square(n_):
            v_.drain()
            v_.wait_ge(ev_act, n_)
            v_.tensor_tensor(acc[:, :], acc[:, :], e_t[:, :], ALU.add).then_inc(r_done, 1)

        def out1(first, i):
            def evac(j, used):
                v_.drain()
                v_.wait_ge(w_used, used)
                v_.tensor_copy(o_at(first + j + i * 2), pj[(N_OUT1 + j) % 2][:, :]).then_inc(y_done, 1)
                add_square(N_OUT1 + 1 + first + j + i * 2)
            return evac

        for j in range(2):
            lo(v_, At(U_OUT1 + 4 + j))
        for j in range(2):
            out1(0, 0)(j, U_OUT1 + 3 + j)
        with v_.Fori(0, KT // 2 - 1) as i:
            two_strips(At(U_OUT1 + 4, i, 4), out1(2, i))
        v_.drain().then_inc(acc_ready, 1)
        lo(v_, At(U_CMPIN + 2))
        rms_ms(v_, 3, D)
        lo(v_, At(U_CMPIN + 3))
        rms_rb(v_, 3, rb)

        def scale_tile(j):
            v_.scalar_tensor_tensor(o[:, j, :], o[:, j, :], c("g_post", j), rb[:, :], ALU.mult, ALU.mult)\
              .then_inc(scaled, 1)

        for j in range(3):
            scale_tile(j)
        for j in range(KT):
            if j + 3 < KT:
                scale_tile(j + 3)
            x_rest(j, o[:, j, :], c("g_2", j), 3 * KT - 6)
            if j in (12, 14):
                lo(v_, At(U_CMPIN + j // 2 - 2))
        lo(v_, At(U_CMPIN + 6))
        rms_ms(v_, 4, D)
        rms_rb(v_, 4, rb)
        lo(v_, At(U_CMPIN + 7))
        v_.wait_ge(tab2_in, 32)
        v_.tensor_tensor(cos2[:, :], cos2[:, :], rb[:, :], ALU.mult)
        v_.tensor_tensor(sin2[:, :], sin2[:, :], rb[:, :], ALU.mult)

        def take_cmp(j, used):
            b = (N_CMPIN + j) % 2 if j < 2 else sb[j - 2]
            if j < 2:
                take_rope(v_, b, used, cos2, sin2, 64, cmp_in[0][:, j, :])
            else:
                take(v_, None, b, used, rb, cmp_in[1][:, j - 2, :])
            v_.drain().then_inc(r_done, 1)

        take_cmp(0, U_CMPIN + 3)
        take_cmp(1, U_CMPIN + 4)
        lo(v_, At(U_CMPIN + 8))
        take_cmp(2, U_CMPIN + 6)
        lo(v_, At(U_CMPIN + 9))
        take_cmp(3, U_CMPIN + 8)
        v_.wait_ge(xn_out, 16 * 4)
        v_.memset(blk[:, :, :], 0.0)

        def blocks(i):
            pos = c("pos_v" if i // 2 else "pos_k", 0, 32)
            jh = i % 2
            v_.drain()
            for g_ in range(2):
                src = cmp_in[i // 2][:, g_, :].rearrange("p (c j) -> p c j", j=16)
                ins = v_.tensor_tensor(blk[:, :, 32 * g_:32 * g_ + NCMP],
                                       src[:, jh:jh + NCMP, :].rearrange("p c j -> p j c"),
                                       pos[:, 16 * jh:16 * jh + 16].unsqueeze(2).to_broadcast([P, 16, NCMP]), ALU.add)
            ins.then_inc(blk_made, 1)

        def blocks_lo(i):
            v_.drain()
            v_.wait_ge(blk_hi, i + 1)
            half_ = slice(16 * (i % 2), 16 * (i % 2) + 16)
            v_.tensor_tensor(blkp[i // 2][1][:, half_, :], blk[:, :, :], blkp[i // 2][0][:, half_, :].bitcast(F32),
                             ALU.subtract).then_inc(blk_lo, 1)

        for g_ in range(2):
            def evac(j, used):
                blocks(2 * g_ + j)
                take_rope(v_, (N_KV + j) % 2, used, cos2, sin2, 64, y[:, :])
                blocks_lo(2 * g_ + j)
                rest_y(v_, N_KV + 2 * g_ + j - 4, kvg[g_][("ks", "kw")[j]])
            two_strips(At(U_KV + 4 * g_), evac)

        for g_ in range(2):
            def evac(j, used):
                take(v_, None, (N_KV + j) % 2, used, rb, yv[:, :])
                rest_v(v_, N_KV + 4 + 2 * g_ + j - 4, kvg[g_][("vs", "vw")[j]])
            two_strips(At(U_KV + 8 + 4 * g_), evac)
        lo(v_, At(U_GA + 2))
        lo(v_, At(U_GA + 3))
        take(v_, None, N_GA % 2, U_GA + 2, rb, yv[:, :])
        v_.wait_ge(ev_act, N_GA + 1 - 4)
        v_.tensor_scalar(gat[:, :, :], gat[:, :, :], 1.0, 0.5, ALU.add, ALU.mult).then_inc(r_done, 1)
        def hidden_lo(which):
            v_.drain()
            v_.wait_ge(hact, 2 * which + 2)
            v_.scalar_tensor_tensor(hidp[1][:, which, :, :], sb[2 + which][:, 0:P].rearrange("p (m c) -> p m c", m=2),
                                    0.5, hidp[0][:, which, :, :].bitcast(F32), ALU.mult, ALU.subtract).then_inc(hdve, 1)

        for which in range(2):
            for i in range(8):
                lo(v_, At(U_W1 + 8 * which + i + LEAD))
                if which and i == 2:
                    hidden_lo(0)
            v_.drain()
            v_.wait_ge(hact, 2 * which + 1)
            v_.scalar_tensor_tensor(hid[:, :], hide[:, :], 1.0, sb[which][0:64, 0:256], ALU.add, ALU.mult).then_inc(gad, 1)
        lo(v_, At(U_W2), 512)
        hidden_lo(1)
        lo(v_, At(U_W2 + 1))
        take_rope(v_, N_A % 2, U_Q0 + 2, cos2, sin2, 64, y[:, :])
        rest_y(v_, N_A - 4, q2)
        v_.wait_ge(hact, 5)
        v_.tensor_tensor(kcp[1][:, :], px[:, 0:64], kcp[0][:, :].bitcast(F32), ALU.subtract)
        v_.tensor_copy(vct[:, :], px[:, 64:128]).then_inc(hdve, 1)
        lo(v_, At(U_W2 + 2))
        v_.wait_ge(hact, 6)
        v_.tensor_tensor(vcp[1][:, :, :], px[0:32, 0:256].rearrange("p (g d) -> p g d", g=2),
                         vcp[0][:, :, :].bitcast(F32), ALU.subtract).then_inc(hdve, 1)
        lo(v_, At(U_A))
        lo(v_, At(U_A + 1))

        def a_head(h, g_, u, n_, last):
            i = A_A + 2 * h
            b = n_.base % 2

            def gate_of(branch):
                return gat[:, :, bass.ds(h * 3 + branch, 1)].rearrange("p t a -> p (t a)")

            lo(v_, u.on(2))
            take(v_, None, 1 - b, u(0), rb, y[:, :])
            maxima(v_, i, SC_A)
            v_.wait_ge(sc_done, h + 1)
            v_.tensor_reduce(nm[:, 4:8], px[:, 0:128].rearrange("p (t c) -> p t c", t=NQ), AX.X, ALU.max, negate=True)
            v_.drain()
            v_.tensor_scalar(nms[:, 4:8], nm[:, 4:8], SC_A, 1e20, ALU.mult, ALU.min).then_inc(pc_exp, 1)
            divide(v_, i, gate_of(1))
            v_.wait_ge(hact, h + 7)
            v_.tensor_scalar(rinv[:, 4:8], lsum[:, 4:8], 1e-30, None, ALU.max)
            v_.drain()
            v_.reciprocal(rinv[:, 4:8], rinv[:, 4:8])
            v_.drain()
            v_.tensor_tensor(rinv[:, 4:8], rinv[:, 4:8], gate_of(0), ALU.mult)
            v_.drain()
            v_.tensor_tensor(rinv[:, 4:8], rinv[:, 4:8], c("rowok", 0, 4), ALU.mult)
            v_.drain()
            v_.tensor_tensor(pc[:, :, :], pc[:, :, :], rinv[:, 4:8].unsqueeze(2).to_broadcast([P, NQ, 32]), ALU.mult)\
              .then_inc(pc_norm, 1)
            lo(v_, u.on(3))
            turned(v_, i)
            v_.wait_ge(ptc_hi, h + 1)
            v_.tensor_tensor(ptc[1][:, :], px[0:32, :], ptc[0][:, :].bitcast(F32), ALU.subtract).then_inc(ptc_lo, 1)
            silu(v_, n_(-1) - 4, gate[:, :])
            lo(v_, u.on(4))
            maxima(v_, i + 1, SC_A)
            if last:
                v_.wait_ge(tab2_in, 64)
                v_.tensor_tensor(cos2[:, :], cos2[:, :], rb[:, :], ALU.mult)
                v_.tensor_tensor(sin2[:, :], sin2[:, :], rb[:, :], ALU.mult)
            divide(v_, i + 1, gate_of(2))
            take_rope(v_, b, u(2), cos2, sin2, 32 if last else 64, y[:, :])
            rest_y(v_, n_(0) - 4, kbb if last else q2)
            lo(v_, u.on(5))
            turned(v_, i + 1)
            if last:
                v_.memset(vbz[0][:, :, :, :].bitcast(F32), 0.0)
                v_.memset(vbz[1][:, :, :, :].bitcast(F32), 0.0)
                take(v_, None, 1 - b, u(4), rb, yv[:, :])
            head_out(v_, h + 16, o_at(h), gate[:, :])

        with v_.Fori(0, 4) as h:
            a_head(h, 0, At(U_A, h, 4), At(N_A + 2, h, 2), False)
        with v_.Fori(4, 7) as h:
            a_head(h, 1, At(U_A, h, 4), At(N_A + 2, h, 2), False)
        a_head(7, 1, At(U_KVB), At(N_KVB), True)
        lo(v_, At(U_B + 2))
        v_.wait_ge(ev_act, N_KVB + 2 - 4)
        pxv = px[:, :].rearrange("p (t d) -> p t d", t=NQ)
        v_.tensor_tensor(vbz[1][:, 0, :, 0:64], pxv[:, :, 0:64], vbz[0][:, 0, :, 0:64].bitcast(F32), ALU.subtract)
        v_.tensor_tensor(vbz[1][:, 1, :, 64:128], pxv[:, :, 64:128], vbz[0][:, 1, :, 64:128].bitcast(F32),
                         ALU.subtract).then_inc(r_done, 1)
        lo(v_, At(U_B + 3))
        take_rope(v_, N_B % 2, U_B + 2, cos2, sin2, 32, y[:, :])
        rest_y(v_, N_B - 4, q2)
        v_.tensor_scalar(nsink[:, :], c("sinks", 0, 16), -1.0, None, ALU.mult)
        lo(v_, At(U_B + 4))
        lo(v_, At(U_B + 5))

        def b_pair(p, u, n_, steps):
            b = n_.base % 2
            if steps:
                lo(v_, u.on(2))
            take(v_, None, 1 - b, u(0), rb, y[:, :])
            if not steps:
                for j in range(4):
                    x_rest(j, o[:, j, :], None, 4 * KT - 6)
            for hh in range(2):
                for t in range(NQ):
                    if t % 2 == 0:
                        v_.wait_ge(s_done, 4 * 32 + 8 * p + 4 * hh + t + 2)
                    w = P if t == 0 else 2 * P
                    c0 = WROW[t] - (384 if t >= 2 else 0)
                    v_.tensor_reduce(nm[:, 4 * hh + t:4 * hh + t + 1], sb[2 * hh + t // 2][:, c0:c0 + w], AX.X, ALU.max,
                                     negate=True)
            v_.drain()
            for hh in range(2):
                ins = v_.tensor_scalar(nms[:, 4 * hh:4 * hh + 4], nm[:, 4 * hh:4 * hh + 4], SC_B,
                                       nsink[:, bass.ds(p + 8 * hh, 1)], ALU.mult, ALU.min)
            ins.then_inc(nm_done, 1)
            if not steps:
                for j in range(4, 8):
                    x_rest(j, o[:, j, :], None, 4 * KT - 6)
            v_.wait_ge(p_exp, 4 * 32 + 1 + p)
            v_.tensor_tensor(rinv[:, 0:8], lsum[:, 0:8], lsum[:, 8:16], ALU.add)
            v_.drain()
            v_.reciprocal(rinv[:, 0:8], rinv[:, 0:8])
            v_.drain()
            for hh in range(2):
                for t in range(NQ):
                    w = P if t == 0 else 2 * P
                    cols = slice(BANDED * hh + WROW[t], BANDED * hh + WROW[t] + w)
                    ins = v_.tensor_scalar(prob[:, cols], prob[:, cols], rinv[:, 4 * hh + t:4 * hh + t + 1], None, ALU.mult)
            ins.then_inc(p_norm, 1)
            if steps:
                lo(v_, u.on(3))
            else:
                lo(v_, u.on(2))
                lo(v_, u.on(3))
                for j in range(8, 15):
                    x_rest(j, o[:, j, :], None, 4 * KT - 6)
            silu(v_, n_(-1) - 4, gate[:, :])
            if steps:
                take_rope(v_, b, u(2), cos2, sin2, 32, y[:, :])
                rest_y(v_, n_(0) - 4, q2)
                lo(v_, u.on(4))
            for hh in range(2):
                v_.wait_ge(pt_hi, 4 * 32 + 2 * p + hh + 1)
                for b_ in range(2):
                    w = 512 if b_ == 0 else 384
                    c0 = BANDED * hh + 512 * b_
                    ins = v_.tensor_tensor(ptl[:, c0:c0 + w], sb[2 * hh + b_][:, 0:w], pth[:, c0:c0 + w].bitcast(F32),
                                           ALU.subtract)
                ins.then_inc(pt_lo, 1)
            if steps:
                lo(v_, u.on(5))
            head_out(v_, p + 24, o_at(p + 8), gate[:, :])

        with v_.Fori(0, NPAIR - 1) as p:
            b_pair(p, At(U_B + 4, p, 4), At(N_B + 2, p, 2), True)
        b_pair(NPAIR - 1, At(U_OUT2), At(N_OUT2), False)
        x_rest(15, o[:, 15, :], None, 4 * KT - 6)
        v_.memset(acc[:, :], 0.0)

        def out2(first, i):
            def evac(j, used):
                v_.drain()
                v_.wait_ge(xn_in if j == 0 else xn_in2, 16 * (first // 2 + 1) + i * 16)
                v_.wait_ge(w_used, used)
                v_.tensor_tensor(o_at(first + j + i * 2), pj[(N_OUT2 + j) % 2][:, :], xr2[j][:, :], ALU.add)\
                  .then_inc(y_done, 1)
                add_square(N_OUT2 + 1 - 4 + first + j + i * 2)
            return evac

        for j in range(2):
            lo(v_, At(U_OUT2 + 4 + j))
        for j in range(2):
            out2(0, 0)(j, U_OUT2 + 3 + j)
        with v_.Fori(0, KT // 2 - 2) as i:
            two_strips(At(U_OUT2 + 4, i, 4), out2(2, i))
        lo(v_, At(U_END - 2))
        lo(v_, At(U_END - 1))
        out2(14, 0)(0, U_END - 2)
        out2(14, 0)(1, U_END)
        v_.drain().then_inc(acc_ready, 1)
        rms_ms(v_, 5, D)
        rms_rb(v_, 5, rb)
        for j in range(POOL_TILES, KT):
            v_.scalar_tensor_tensor(o[:, j, :], o[:, j, :], c("g_fin", j), rb[:, :], ALU.mult, ALU.mult)\
              .then_inc(fin, 1)


def kernel(**inputs):
    import concourse.bacc as bacc
    from concourse.bass_utils import run_bass_kernel_spmd

    a = {k_: np.asarray(v_) for k_, v_ in inputs.items()}
    f = np.float32

    def cols(g):
        return np.ascontiguousarray(g.reshape(-1, P).T)

    units = []

    def put(tiles):
        u = np.zeros((P, 1024), f)
        for i, tile in enumerate(tiles):
            u[:, P * i:P * i + tile.shape[1]] = tile
        units.append(u)

    def strip(w, order, per=8):
        kt = w.shape[0] // P
        for k0 in range(0, kt, per):
            put([w[P * i:P * i + P][:, order] for i in range(k0, min(k0 + per, kt))])

    r = np.arange
    w1, w2 = a["w_in"][0], a["w_in_2"][0]
    off = np.cumsum([0, 768, 512, 64, 1024, 1024, 1024, 1024, 8, 1024])
    misc = np.concatenate([w1[:, off[2]:off[3]], w1[:, off[7]:off[8]]], 1)
    strip(misc, r(misc.shape[1]))
    for h in range(NHEAD):
        for part in (4, 5, 6, 8):
            strip(w1, off[part] + P * h + r(P))
    units[1], units[2] = units[2], units[1]
    for h in range(NHEAD):
        strip(w1, off[3] + P * h + r(P))
    for i in range(QR_T):
        strip(w1, off[0] + P * i + r(P))
    for i in range(KV_T):
        strip(w1, off[1] + P * i + r(P))
    uq, ukv = a["w_uq"][0], a["w_ukv"][0]
    for p in range(4):
        ha, hb = 2 * p, 2 * p + 1
        strip(uq, 192 * ha + r(P))
        strip(ukv, 256 * ha + r(P))
        strip(ukv, 256 * ha + P + r(P))
        strip(uq, np.concatenate([192 * ha + P + r(64), 192 * hb + P + r(64)]), per=3)
        strip(uq, 192 * hb + r(P))
        strip(ukv, 256 * hb + r(P))
        strip(ukv, 256 * hb + P + r(P))
    for j in range(KT):
        w = a["w_out"][0].reshape(KT, P, D)
        strip((w[EARLY] if j < 2 else w).reshape(D, D), P * j + r(P))
    units[U_OUT1 + 1], units[U_OUT1 + 2] = units[U_OUT1 + 2], units[U_OUT1 + 1]
    off = np.cumsum([0, 1024, 256, 256, 256, 256, 256, 256, 1024, 24, 1024, 128, 128, 1024])
    for part in (1, 2):
        for g in range(2):
            strip(w2, off[part] + P * g + r(P))
    units[U_CMPIN + 1], units[U_CMPIN + 2] = units[U_CMPIN + 2], units[U_CMPIN + 1]
    for parts in ((3, 5), (4, 6)):
        for g in range(2):
            for part in parts:
                strip(w2, off[part] + P * g + r(P))
    strip(w2, off[8] + r(24))
    for name in ("cmp_k_w1_2", "cmp_v_w1_2"):
        w = a[name][0]
        for i in range(8):
            put([w[P * (4 * i + t // 2):P * (4 * i + t // 2) + P, P * (t % 2):P * (t % 2) + P] for t in range(8)])
    strip(w2, off[0] + r(P))
    put([a[name][0][P * m:P * m + P] for name in ("cmp_k_w2_2", "cmp_v_w2_2") for m in range(2)])
    strip(w2, off[7] + r(P))
    for h in range(1, NHEAD):
        strip(w2, off[0] + P * h + r(P))
        strip(w2, off[7] + P * h + r(P))
    strip(w2, off[10] + r(P))
    strip(w2, off[11] + r(P))
    both = [np.concatenate([64 * p + r(64), 64 * (p + 8) + r(64)]) for p in range(NPAIR)]
    for p in range(NPAIR):
        strip(w2, off[9] + both[p])
        strip(w2, off[12] + both[p])
    wo2 = np.concatenate([a["w_out_2"][0][:1024]] + [a["w_out_2"][0][1024 + b] for b in both], 0)
    for j in range(KT):
        strip(wo2, P * j + r(P))
    units[U_OUT2 + 1], units[U_OUT2 + 2] = units[U_OUT2 + 2], units[U_OUT2 + 1]
    assert len(units) == U_END

    inv64 = (np.float32(10000.0) ** (-r(0, 64, 2).astype(f) / np.float32(64))).astype(f)
    inv128 = (np.float32(10000.0) ** (-r(0, 128, 2).astype(f) / np.float32(128))).astype(f)
    part = r(P)
    sgn64 = np.where(part % 64 < 32, -1, 1).astype(f)
    sgn128 = np.where(part < 64, -1, 1).astype(f)
    tok = r(S).astype(f)
    ang_a = (tok[None, :] * inv128[part % 64][:, None]).astype(f)
    ang_b = (tok[None, :] * inv64[part % 32][:, None]).astype(f)
    rowok = ((P * r(NQ)[None, :] + part[:, None]) >= JB - 1).astype(f)
    bf = np.broadcast_to(np.tile(a["b_forget"][0], NQ), (P, 4 * NHEAD))
    cvec = np.concatenate([
        cols(a["g_pre"][0]), cols(a["g_q_latent"][0]), cols(a["g_kv_latent"][0]), cols(a["g_post"][0]),
        cols(a["norm_g_2"][0]), cols(a["final_g_2"]), bf, np.broadcast_to(a["sinks_2"][0], (P, 16)),
        inv64[part % 32][:, None], sgn64[:, None], rowok, a["cmp_k_pos_2"][0].T, a["cmp_v_pos_2"][0].T], 1).astype(f)
    import ml_dtypes
    bf16 = ml_dtypes.bfloat16
    i_, j_ = part[:, None], part[None, :]
    c_ = r(32)
    cmask = np.zeros((P, NQ, 32), f)
    for t in range(NQ):
        cmask[:, t, :] = np.where((c_[None, :] < NCMP) & (16 * c_[None, :] + JB - 1 <= P * t + part[:, None]), 0, NEG)
    sel = np.zeros((P, NHEAD, 256), f)
    for h in range(NHEAD):
        sel[h, h, 0], sel[32 + h, h, 32], sel[64, h, 64], sel[64, h, 96] = -1, -1, 1, 1
        sel[64, h, P], sel[64, h, P + 32], sel[h, h, P + 64], sel[32 + h, h, P + 96] = 1, 1, 1, 1
    tri = np.concatenate([(i_ <= j_).astype(f), np.ones((P, S - P), f)], 1)
    arrays = {
        "w": np.stack(units), "xt": np.ascontiguousarray(a["x"][0].T.reshape(KT, P, S).transpose(1, 0, 2)),
        "pos": np.ascontiguousarray(np.broadcast_to(a["positions"][0], (P, S))).astype(np.int32),
        "cvec": np.ascontiguousarray(cvec), "ident": np.eye(P, dtype=f), "ones": np.ones((P, P), f),
        "identb": np.eye(P).astype(bf16), "maskd": np.where(j_ <= i_, 0, NEG).astype(bf16),
        "maskw": np.where(j_ > i_, 0, NEG).astype(bf16), "maskc": cmask.reshape(P, P).astype(bf16),
        "sel": sel, "tri": tri,
        "cos_a": np.cos(ang_a).astype(f), "sin_a": (np.sin(ang_a) * sgn128[:, None]).astype(f),
        "cos_b": np.cos(ang_b).astype(f), "sin_b": (np.sin(ang_b) * sgn64[:, None]).astype(f),
    }
    nc = bacc.Bacc("TRN2", target_bir_lowering=False, num_devices=1)
    d = {k_: nc.dram_tensor(f"in_{k_}", v_.shape, mybir.dt.from_np(v_.dtype), kind="ExternalInput").ap()
         for k_, v_ in arrays.items()}
    d["xn"] = nc.dram_tensor("xn", (P, KT, S), F32, kind="Internal").ap()
    d["out"] = nc.dram_tensor("out", (P, KT, S), F32, kind="ExternalOutput").ap()
    build(nc, d)
    res = run_bass_kernel_spmd(nc, [{f"in_{k_}": v_ for k_, v_ in arrays.items()}], core_ids=[0])
    out = res.results[0]["out"]
    return np.ascontiguousarray(out.transpose(1, 0, 2).reshape(D, S).T)[None]
```
